# Optimizing a Trainium2 kernel written in Bass

```python
import jax, jax.numpy as jnp
from jax import lax
import numpy as np
import math

D_MODEL = 1024
BATCH = 1
SEQ = 1024
DEPTH = 2

N_META = 16
H_A = 4
QK_NOPE = 128
QK_ROPE = 64
V_DIM = 128
Q_LORA = 256
KV_LORA = 128
ROPE_THETA = 10000.0
Q_BLOCK = 128
H_B = 8
N_B = 64
RW = H_B * N_B
DECAY_LORA = 64
AAA_LORA = 64
GATE_LORA = 128
VRES_LORA = 32
RWKV_GN_EPS = 64e-5
MIX = H_A * V_DIM + RW
MLA_COLS = Q_LORA + KV_LORA + QK_ROPE
RWKV_COLS = 3 * RW + 2 * DECAY_LORA + 2 * AAA_LORA + GATE_LORA
IN_COLS = MLA_COLS + RWKV_COLS
N_GROUPS = 4
EXPERTS_PER_GROUP = 8
N_EXPERTS = N_GROUPS * EXPERTS_PER_GROUP
TOP_K = 2
E_HID = 256
MOE_BLOCK = 128
DN_ALPHA = (2 * DEPTH) ** 0.25
DN_BETA = (8 * DEPTH) ** -0.25
LN_EPS = 1e-5
RMS_EPS = 1e-6


def _split(t, sizes):
    return jnp.split(t, np.cumsum(sizes)[:-1].tolist(), axis=-1)

def _layer_norm(x, g, b):
    xf = x.astype(jnp.float32)
    mu = jnp.mean(xf, -1, keepdims=True)
    var = jnp.mean(jnp.square(xf - mu), -1, keepdims=True)
    return ((xf - mu) * lax.rsqrt(var + LN_EPS) * g + b).astype(x.dtype)

def _rms_norm(x, g):
    xf = x.astype(jnp.float32)
    return (xf * lax.rsqrt(jnp.mean(xf * xf, -1, keepdims=True) + RMS_EPS) * g).astype(x.dtype)

def _rope(t, cos, sin):
    half = t.shape[-1] // 2
    t1, t2 = t[..., :half], t[..., half:]
    return jnp.concatenate([t1 * cos - t2 * sin, t2 * cos + t1 * sin], -1).astype(t.dtype)

def _centred_shift(p, mu_prev, mu_next):
    prev = jnp.pad(p[:, :-1], ((0, 0), (1, 0), (0, 0)))
    nxt = jnp.pad(p[:, 1:], ((0, 0), (0, 1), (0, 0)))
    return p + mu_prev * (prev - p) + mu_next * (nxt - p)

def _mla(c_q, c_kv, k_pe, cos, sin, q_norm, kv_norm, w_uq, w_ukv, out_norm):
    B, L, _ = c_q.shape
    q = (_rms_norm(c_q, q_norm) @ w_uq).reshape(B, L, H_A, QK_NOPE + QK_ROPE)
    q_nope = q[..., :QK_NOPE]
    q_pe = _rope(q[..., QK_NOPE:], cos[:, :, None, :], sin[:, :, None, :])
    kv = (_rms_norm(c_kv, kv_norm) @ w_ukv).reshape(B, L, H_A, QK_NOPE + V_DIM)
    k_nope, v = kv[..., :QK_NOPE], kv[..., QK_NOPE:]
    k_pe = _rope(k_pe, cos, sin)
    scale = (QK_NOPE + QK_ROPE) ** -0.5

    def attend(blk):
        qn, qp = blk
        s = jnp.einsum('bqhd,bkhd->bhqk', qn, k_nope) + jnp.einsum('bqhd,bkd->bhqk', qp, k_pe)
        p = jax.nn.softmax(s.astype(jnp.float32) * scale, axis=-1).astype(v.dtype)
        return jnp.einsum('bhqk,bkhd->bqhd', p, v)

    out_meta = attend((q_nope[:, :N_META], q_pe[:, :N_META]))
    n_blk = (L - N_META) // Q_BLOCK

    def to_blocks(t):
        return jnp.moveaxis(t[:, N_META:].reshape(B, n_blk, Q_BLOCK, H_A, t.shape[-1]), 1, 0)

    out_real = lax.map(attend, (to_blocks(q_nope), to_blocks(q_pe)))
    out_real = jnp.moveaxis(out_real, 0, 1).reshape(B, L - N_META, H_A, V_DIM)
    out = jnp.concatenate([out_meta, out_real], axis=1)
    out = _rms_norm(out, out_norm.reshape(H_A, V_DIM))
    return out.reshape(B, L, H_A * V_DIM)

def _wkv_scan(r, decay, k, v, kk, a, reverse):
    B = r.shape[0]

    def step(S, inp):
        r_t, w_t, k_t, v_t, kk_t, b_t = inp
        sa = jnp.einsum('bhvk,bhk->bhv', S, kk_t)
        S = S * w_t[:, :, None, :] - sa[..., None] * b_t[:, :, None, :] + v_t[..., None] * k_t[:, :, None, :]
        return S, jnp.einsum('bhvk,bhk->bhv', S, r_t)

    xs = tuple(jnp.moveaxis(t, 1, 0) for t in (r, decay, k, v, kk, kk * a))
    S0 = jnp.zeros((B, H_B, N_B, N_B), jnp.float32)
    _, ys = lax.scan(step, S0, xs, reverse=reverse)
    return jnp.moveaxis(ys, 0, 1)

def _rwkv_bidir(u, v_first, vres, w0, w2, a0, a2, g2, k_k, k_a, r_k, gn_g, gn_b):
    dt = u.dtype
    u = u.astype(jnp.float32)
    B, L, _ = u.shape
    r, k, v, wd_f, wd_b, ad_f, ad_b, gd = _split(
        u, [RW, RW, RW, DECAY_LORA, DECAY_LORA, AAA_LORA, AAA_LORA, GATE_LORA])
    if vres is None:
        v_first = v
    else:
        v0, v1, v2 = vres
        v = v + (v_first - v) * jax.nn.sigmoid(v0 + (v @ v1) @ v2)
    g = jax.nn.sigmoid(gd) @ g2

    def heads(t):
        return t.reshape(B, L, H_B, N_B)

    kk = heads(k * k_k)
    kk = kk * lax.rsqrt(jnp.sum(kk * kk, -1, keepdims=True) + 1e-12)
    rh, vh = heads(r), heads(v)

    def direction(d, wd, ad, reverse):
        wl = w0[d] + jnp.tanh(wd) @ w2[d]
        decay = jnp.exp(-jnp.exp(-jax.nn.softplus(-wl) - 0.5))
        a = jax.nn.sigmoid(a0[d] + ad @ a2[d])
        kd = heads(k * (1.0 + (a - 1.0) * k_a))
        y = _wkv_scan(rh, heads(decay), kd, vh, kk, heads(a), reverse)
        bonus = jnp.sum(rh * kd * r_k, -1, keepdims=True) * vh
        return y, bonus

    y_f, bonus_f = direction(0, wd_f, ad_f, False)
    y_b, bonus_b = direction(1, wd_b, ad_b, True)
    y = y_f + y_b
    mu = jnp.mean(y, -1, keepdims=True)
    var = jnp.mean(jnp.square(y - mu), -1, keepdims=True)
    yn = ((y - mu) * lax.rsqrt(var + RWKV_GN_EPS)).reshape(B, L, RW) * gn_g + gn_b
    out = (yn + (bonus_f + bonus_b).reshape(B, L, RW)) * g
    return out.astype(dt), v_first

def _hier_moe(h, w_group, b_group, w_expert, b_expert, w1, w3, w2):
    T, D = h.shape
    g_prob = jax.nn.softmax((h @ w_group).astype(jnp.float32) + b_group, axis=-1)
    g_top_p, g_top = lax.top_k(g_prob, 1)
    e_logits = ((h @ w_expert).astype(jnp.float32) + b_expert).reshape(T, N_GROUPS, EXPERTS_PER_GROUP)
    e_logits = jnp.take_along_axis(e_logits, g_top[:, :, None], axis=1)[:, 0]
    e_top_p, e_top = lax.top_k(jax.nn.softmax(e_logits, axis=-1), TOP_K)
    gate = (g_top_p * e_top_p).reshape(-1)
    flat_e = (g_top * EXPERTS_PER_GROUP + e_top).reshape(-1)
    flat_tok = jnp.repeat(jnp.arange(T, dtype=jnp.int32), TOP_K)
    order = jnp.argsort(flat_e)
    se = flat_e[order]
    counts = jnp.bincount(flat_e, length=N_EXPERTS)
    starts = jnp.cumsum(counts) - counts
    padded = (counts + MOE_BLOCK - 1) // MOE_BLOCK * MOE_BLOCK
    pends = jnp.cumsum(padded)
    dest = (pends - padded)[se] + jnp.arange(T * TOP_K) - starts[se]
    n_rows = (T * TOP_K + N_EXPERTS * (MOE_BLOCK - 1) + MOE_BLOCK - 1) // MOE_BLOCK * MOE_BLOCK
    n_blocks = n_rows // MOE_BLOCK
    row_tok = jnp.zeros((n_rows,), jnp.int32).at[dest].set(flat_tok[order])
    row_gate = jnp.zeros((n_rows,), jnp.float32).at[dest].set(gate[order])
    block_e = jnp.clip(jnp.searchsorted(pends, jnp.arange(n_blocks) * MOE_BLOCK, side='right'),
                       0, N_EXPERTS - 1)
    xb = h[row_tok].reshape(n_blocks, MOE_BLOCK, D)

    def expert_block(args):
        xe, e = args
        return (jax.nn.silu(xe @ w1[e]) * (xe @ w3[e])) @ w2[e]

    yb = lax.map(expert_block, (xb, block_e)).reshape(n_rows, D)
    y = jnp.zeros((T, D), jnp.float32).at[row_tok].add(yb.astype(jnp.float32) * row_gate[:, None])
    return y.astype(h.dtype)

def first_inputs(seed: int = 0) -> dict:
    key = jax.random.key(seed)
    ks = iter(jax.random.split(key, 48))

    def nrm(shape, s):
        return jax.random.normal(next(ks), shape, jnp.float32) * s

    def uni(shape, lo, hi):
        return jax.random.uniform(next(ks), shape, jnp.float32, lo, hi)

    D = D_MODEL
    return {
        'x': nrm((BATCH, SEQ, D), 1.0),
        'positions': jnp.tile(jnp.arange(SEQ, dtype=jnp.int32)[None], (BATCH, 1)),
        'meta_tokens': nrm((N_META, D), 1.0),
        'emb_ln_g': 1.0 + nrm((D,), 0.02),
        'emb_ln_b': nrm((D,), 0.02),
        'w_in': nrm((DEPTH, D, IN_COLS), D ** -0.5),
        'mla_q_norm': 1.0 + nrm((DEPTH, Q_LORA), 0.02),
        'mla_kv_norm': 1.0 + nrm((DEPTH, KV_LORA), 0.02),
        'mla_w_uq': nrm((DEPTH, Q_LORA, H_A * (QK_NOPE + QK_ROPE)), Q_LORA ** -0.5),
        'mla_w_ukv': nrm((DEPTH, KV_LORA, H_A * (QK_NOPE + V_DIM)), KV_LORA ** -0.5),
        'mla_out_norm': 1.0 + nrm((DEPTH, H_A * V_DIM), 0.02),
        'rwkv_mu_prev': uni((DEPTH, RWKV_COLS), 0.0, 0.5),
        'rwkv_mu_next': uni((DEPTH, RWKV_COLS), 0.0, 0.5),
        'rwkv_w0': uni((DEPTH, 2, RW), -4.0, 0.0),
        'rwkv_w2': nrm((DEPTH, 2, DECAY_LORA, RW), 0.1),
        'rwkv_a0': nrm((DEPTH, 2, RW), 0.3),
        'rwkv_a2': nrm((DEPTH, 2, AAA_LORA, RW), 0.1),
        'rwkv_g2': nrm((DEPTH, GATE_LORA, RW), GATE_LORA ** -0.5),
        'rwkv_k_k': 0.85 + nrm((DEPTH, RW), 0.05),
        'rwkv_k_a': 1.0 + nrm((DEPTH, RW), 0.05),
        'rwkv_r_k': nrm((DEPTH, H_B, N_B), 0.1),
        'rwkv_gn_g': 1.0 + nrm((DEPTH, RW), 0.02),
        'rwkv_gn_b': nrm((DEPTH, RW), 0.02),
        'rwkv_v0': nrm((DEPTH - 1, RW), 0.3),
        'rwkv_v1': nrm((DEPTH - 1, RW, VRES_LORA), RW ** -0.5),
        'rwkv_v2': nrm((DEPTH - 1, VRES_LORA, RW), 0.5 * VRES_LORA ** -0.5),
        'w_out': nrm((DEPTH, MIX, D), DN_BETA * MIX ** -0.5),
        'ln1_g': 1.0 + nrm((DEPTH, D), 0.02),
        'ln1_b': nrm((DEPTH, D), 0.02),
        'moe_w_group': nrm((DEPTH, D, N_GROUPS), D ** -0.5),
        'moe_b_group': nrm((DEPTH, N_GROUPS), 0.01),
        'moe_w_expert': nrm((DEPTH, D, N_EXPERTS), D ** -0.5),
        'moe_b_expert': nrm((DEPTH, N_EXPERTS), 0.01),
        'moe_w1': nrm((DEPTH, N_EXPERTS, D, E_HID), D ** -0.5),
        'moe_w3': nrm((DEPTH, N_EXPERTS, D, E_HID), D ** -0.5),
        'moe_w2': nrm((DEPTH, N_EXPERTS, E_HID, D), DN_BETA * E_HID ** -0.5),
        'ln2_g': 1.0 + nrm((DEPTH, D), 0.02),
        'ln2_b': nrm((DEPTH, D), 0.02),
    }

def first_block(x, positions, meta_tokens, emb_ln_g, emb_ln_b, w_in, mla_q_norm, mla_kv_norm,
              mla_w_uq, mla_w_ukv, mla_out_norm, rwkv_mu_prev, rwkv_mu_next, rwkv_w0, rwkv_w2,
              rwkv_a0, rwkv_a2, rwkv_g2, rwkv_k_k, rwkv_k_a, rwkv_r_k, rwkv_gn_g, rwkv_gn_b,
              rwkv_v0, rwkv_v1, rwkv_v2, w_out, ln1_g, ln1_b, moe_w_group, moe_b_group,
              moe_w_expert, moe_b_expert, moe_w1, moe_w3, moe_w2, ln2_g, ln2_b):
    B = x.shape[0]
    meta = jnp.broadcast_to(meta_tokens.astype(x.dtype)[None], (B, N_META, D_MODEL))
    h = _layer_norm(jnp.concatenate([meta, x], axis=1), emb_ln_g, emb_ln_b)
    L = h.shape[1]
    pos = jnp.concatenate([jnp.broadcast_to(jnp.arange(N_META, dtype=jnp.int32), (B, N_META)),
                           positions + N_META], axis=1)
    inv_freq = ROPE_THETA ** (-jnp.arange(0, QK_ROPE, 2, dtype=jnp.float32) / QK_ROPE)
    ang = pos.astype(jnp.float32)[..., None] * inv_freq
    cos, sin = jnp.cos(ang), jnp.sin(ang)
    v_first = None
    for li in range(DEPTH):
        proj = h @ w_in[li]
        c_q, c_kv, k_pe, rw = _split(proj, [Q_LORA, KV_LORA, QK_ROPE, RWKV_COLS])
        y_att = _mla(c_q, c_kv, k_pe, cos, sin, mla_q_norm[li], mla_kv_norm[li],
                     mla_w_uq[li], mla_w_ukv[li], mla_out_norm[li])
        u = _centred_shift(rw, rwkv_mu_prev[li], rwkv_mu_next[li])
        vres = None if li == 0 else (rwkv_v0[li - 1], rwkv_v1[li - 1], rwkv_v2[li - 1])
        y_rwkv, v_first = _rwkv_bidir(u, v_first, vres, rwkv_w0[li], rwkv_w2[li], rwkv_a0[li],
                                      rwkv_a2[li], rwkv_g2[li], rwkv_k_k[li], rwkv_k_a[li],
                                      rwkv_r_k[li], rwkv_gn_g[li], rwkv_gn_b[li])
        mixed = jnp.concatenate([y_att, y_rwkv], axis=-1) @ w_out[li]
        h = _layer_norm(DN_ALPHA * h + mixed, ln1_g[li], ln1_b[li])
        ff = _hier_moe(h.reshape(B * L, D_MODEL), moe_w_group[li], moe_b_group[li],
                       moe_w_expert[li], moe_b_expert[li], moe_w1[li], moe_w3[li],
                       moe_w2[li]).reshape(B, L, D_MODEL)
        h = _layer_norm(DN_ALPHA * h + ff, ln2_g[li], ln2_b[li])
    return h[:, N_META:]


DEPTH_2 = 1

CHUNK = 64
ATT_WIDTH = D_MODEL // 2
N_DIFF_HEADS = 4
DIFF_HEAD_DIM = ATT_WIDTH // (2 * N_DIFF_HEADS)
GMLP_WIDTH = D_MODEL - ATT_WIDTH
N_GMLP_GROUPS = 4
GMLP_GROUP_DIM = GMLP_WIDTH // N_GMLP_GROUPS
GMLP_CHUNK = 128
IN_WIDTH = 3 * ATT_WIDTH + 2 * GMLP_WIDTH
D_FF = 2816
CONV_WIDTH = 3
DEEPNORM_ALPHA = (2 * DEPTH_2) ** 0.25
DEEPNORM_BETA = (8 * DEPTH_2) ** -0.25


def layer_norm(x, g, b):
    xf = x.astype(jnp.float32)
    mu = jnp.mean(xf, axis=-1, keepdims=True)
    var = jnp.mean(jnp.square(xf - mu), axis=-1, keepdims=True)
    y = (xf - mu) * lax.rsqrt(var + LN_EPS) * g.astype(jnp.float32) + b.astype(jnp.float32)
    return y.astype(x.dtype)

def rms_norm(x, g):
    xf = x.astype(jnp.float32)
    y = xf * lax.rsqrt(jnp.mean(jnp.square(xf), axis=-1, keepdims=True) + LN_EPS) * g.astype(jnp.float32)
    return y.astype(x.dtype)

def rope_tables(seq_len):
    pos = jnp.arange(seq_len, dtype=jnp.float32)
    inv_freq = 1.0 / (ROPE_THETA ** (jnp.arange(0, DIFF_HEAD_DIM, 2, dtype=jnp.float32) / DIFF_HEAD_DIM))
    ang = pos[:, None] * inv_freq[None, :]
    ang = jnp.concatenate([ang, ang], axis=-1)
    return jnp.cos(ang), jnp.sin(ang)

def apply_rope(t, cos, sin):
    half = DIFF_HEAD_DIM // 2
    t1, t2 = t[..., :half], t[..., half:]
    rot = jnp.concatenate([-t2, t1], axis=-1)
    out = t.astype(jnp.float32) * cos[None, :, None, :] + rot.astype(jnp.float32) * sin[None, :, None, :]
    return out.astype(t.dtype)

def diff_attention(q, k, v, lam, cos, sin):
    B, S = q.shape[0], q.shape[1]
    n_blk = S // Q_BLOCK
    q = apply_rope(q, cos, sin) * (DIFF_HEAD_DIM ** -0.5)
    k = apply_rope(k, cos, sin)
    q_blocks = q.reshape(B, n_blk, Q_BLOCK, 2 * N_DIFF_HEADS, DIFF_HEAD_DIM).transpose(1, 0, 3, 2, 4)
    kt = k.transpose(0, 2, 1, 3)
    vt = v.transpose(0, 2, 1, 3)
    k_chunk = jnp.arange(S, dtype=jnp.int32) // CHUNK
    q_chunk = k_chunk.reshape(n_blk, Q_BLOCK)

    def one_block(args):
        q_blk, qc = args
        s = jnp.einsum('bhqd,bhkd->bhqk', q_blk, kt, preferred_element_type=jnp.float32)
        mask = k_chunk[None, :] <= qc[:, None]
        p = jax.nn.softmax(jnp.where(mask, s, -jnp.inf), axis=-1)
        p = p.reshape(B, N_DIFF_HEADS, 2, Q_BLOCK, S)
        a = (p[:, :, 0] - lam * p[:, :, 1]).astype(vt.dtype)
        return jnp.einsum('bhqk,bhkd->bhqd', a, vt)

    o = lax.map(one_block, (q_blocks, q_chunk))
    return o.transpose(1, 0, 3, 2, 4).reshape(B, S, N_DIFF_HEADS, 2 * DIFF_HEAD_DIM)

def spatial_gating(z, ln_g, ln_b, w_s, b_s):
    B, S = z.shape[0], z.shape[1]
    n_c = S // GMLP_CHUNK
    u, vg = z[..., :GMLP_WIDTH], z[..., GMLP_WIDTH:]
    vg = vg.reshape(B, S, N_GMLP_GROUPS, GMLP_GROUP_DIM)
    vg = layer_norm(vg, ln_g.reshape(N_GMLP_GROUPS, GMLP_GROUP_DIM), ln_b.reshape(N_GMLP_GROUPS, GMLP_GROUP_DIM))
    vg = vg.reshape(B, n_c, GMLP_CHUNK, N_GMLP_GROUPS, GMLP_GROUP_DIM)
    w_causal = jnp.tril(w_s)
    gate = jnp.einsum('gts,bcsgd->bctgd', w_causal, vg) + b_s.T[None, None, :, :, None]
    u = u.reshape(B, n_c, GMLP_CHUNK, N_GMLP_GROUPS, GMLP_GROUP_DIM)
    return (u * gate).reshape(B, S, GMLP_WIDTH)

def causal_dwconv(h, w, b):
    S = h.shape[1]
    hp = jnp.pad(h, ((0, 0), (CONV_WIDTH - 1, 0), (0, 0)))
    y = b
    for j in range(CONV_WIDTH):
        y = y + w[j] * hp[:, j:j + S]
    return y

def second_inputs(seed: int = 0) -> dict:
    key = jax.random.key(seed)
    ks = jax.random.split(key, 24)
    f32 = jnp.float32
    nrm = lambda k, shape, scale: jax.random.normal(k, shape, f32) * scale
    L = DEPTH_2
    return {
        "x": jax.random.normal(ks[0], (BATCH, SEQ, D_MODEL), f32),
        "w_in": nrm(ks[1], (L, D_MODEL, IN_WIDTH), D_MODEL ** -0.5),
        "lambda_q1": nrm(ks[2], (L, DIFF_HEAD_DIM), 0.1),
        "lambda_k1": nrm(ks[3], (L, DIFF_HEAD_DIM), 0.1),
        "lambda_q2": nrm(ks[4], (L, DIFF_HEAD_DIM), 0.1),
        "lambda_k2": nrm(ks[5], (L, DIFF_HEAD_DIM), 0.1),
        "subln_g": 1.0 + nrm(ks[6], (L, 2 * DIFF_HEAD_DIM), 0.02),
        "gmlp_ln_g": 1.0 + nrm(ks[7], (L, GMLP_WIDTH), 0.02),
        "gmlp_ln_b": nrm(ks[8], (L, GMLP_WIDTH), 0.02),
        "w_spatial": nrm(ks[9], (L, N_GMLP_GROUPS, GMLP_CHUNK, GMLP_CHUNK), GMLP_CHUNK ** -0.5),
        "b_spatial": 1.0 + nrm(ks[10], (L, N_GMLP_GROUPS, GMLP_CHUNK), 0.02),
        "w_out": nrm(ks[11], (L, D_MODEL, D_MODEL), D_MODEL ** -0.5 * DEEPNORM_BETA),
        "ln1_g": 1.0 + nrm(ks[12], (L, D_MODEL), 0.02),
        "ln1_b": nrm(ks[13], (L, D_MODEL), 0.02),
        "w_gate": nrm(ks[14], (L, D_MODEL, D_FF), D_MODEL ** -0.5),
        "w_up": nrm(ks[15], (L, D_MODEL, D_FF), D_MODEL ** -0.5),
        "conv_w": nrm(ks[16], (L, CONV_WIDTH, D_FF), CONV_WIDTH ** -0.5),
        "conv_b": nrm(ks[17], (L, D_FF), 0.02),
        "w_down": nrm(ks[18], (L, D_FF, D_MODEL), D_FF ** -0.5 * DEEPNORM_BETA),
        "ln2_g": 1.0 + nrm(ks[19], (L, D_MODEL), 0.02),
        "ln2_b": nrm(ks[20], (L, D_MODEL), 0.02),
    }

def second_block(x, w_in, lambda_q1, lambda_k1, lambda_q2, lambda_k2, subln_g, gmlp_ln_g, gmlp_ln_b,
              w_spatial, b_spatial, w_out, ln1_g, ln1_b, w_gate, w_up, conv_w, conv_b, w_down,
              ln2_g, ln2_b):
    B, S, _ = x.shape
    cos, sin = rope_tables(S)
    for l in range(DEPTH_2):
        lambda_init = 0.8 - 0.6 * math.exp(-0.3 * l)
        h = jnp.einsum('bsd,de->bse', x, w_in[l])
        qa = h[..., :ATT_WIDTH].reshape(B, S, 2 * N_DIFF_HEADS, DIFF_HEAD_DIM)
        ka = h[..., ATT_WIDTH:2 * ATT_WIDTH].reshape(B, S, 2 * N_DIFF_HEADS, DIFF_HEAD_DIM)
        va = h[..., 2 * ATT_WIDTH:3 * ATT_WIDTH].reshape(B, S, N_DIFF_HEADS, 2 * DIFF_HEAD_DIM)
        zb = h[..., 3 * ATT_WIDTH:]

        lam = (jnp.exp(jnp.sum(lambda_q1[l].astype(jnp.float32) * lambda_k1[l].astype(jnp.float32)))
               - jnp.exp(jnp.sum(lambda_q2[l].astype(jnp.float32) * lambda_k2[l].astype(jnp.float32)))
               + lambda_init)
        oa = diff_attention(qa, ka, va, lam, cos, sin)
        oa = (rms_norm(oa, subln_g[l]) * (1.0 - lambda_init)).reshape(B, S, ATT_WIDTH)

        ob = spatial_gating(jax.nn.gelu(zb, approximate=False), gmlp_ln_g[l], gmlp_ln_b[l],
                            w_spatial[l], b_spatial[l])

        mix = jnp.einsum('bse,ed->bsd', jnp.concatenate([oa, ob], axis=-1), w_out[l])
        x = layer_norm(DEEPNORM_ALPHA * x + mix, ln1_g[l], ln1_b[l])

        g = jnp.einsum('bsd,df->bsf', x, w_gate[l])
        up = jnp.einsum('bsd,df->bsf', x, w_up[l])
        g = causal_dwconv(g, conv_w[l], conv_b[l])
        f = jnp.einsum('bsf,fd->bsd', jax.nn.silu(g) * up, w_down[l])
        x = layer_norm(DEEPNORM_ALPHA * x + f, ln2_g[l], ln2_b[l])
    return x


_first_inputs = second_inputs


def second_inputs(seed=0):
    import zlib

    import numpy as np

    out = dict(_first_inputs(seed))
    spreads = {}
    factors = {'lambda_k2': 6.396,
     'subln_g': 25.63,
     'gmlp_ln_g': 49.6,
     'gmlp_ln_b': 52.383,
     'b_spatial': 33.494,
     'ln1_g': 2.766,
     'conv_b': 8.0,
     'ln2_g': 8.029,
     'ln2_b': 8.363,
     'ln1_b': 6.191}
    for name, (base, spread) in spreads.items():
        noise = np.random.default_rng([zlib.crc32(name.encode()), seed]).standard_normal(out[name].shape)
        drawn = base * np.exp(spread * noise) if base else spread * noise
        out[name] = __import__('jax').numpy.asarray(drawn.astype(out[name].dtype))
    for name, factor in factors.items():
        out[name] = (out[name] * factor).astype(out[name].dtype)
    return out


_narrow_inputs = second_inputs


def second_inputs(seed=0):

    out = dict(_narrow_inputs(seed))
    wider = {'subln_g': 4.39,
     'gmlp_ln_g': 4.62,
     'gmlp_ln_b': 4.6,
     'b_spatial': 4.42,
     'ln2_g': 3.19,
     'ln2_b': 3.19}
    for name, times in wider.items():
        mean = out[name].mean()
        out[name] = (mean + times * (out[name] - mean)).astype(out[name].dtype)
    return out


def setup_inputs(seed=0):
    out = dict(first_inputs(seed))
    for name, value in second_inputs(seed + 1).items():
        if name != "x":
            out[name + "_2"] = value
    return out


def reference(
    x, positions, meta_tokens, emb_ln_g, emb_ln_b, w_in, mla_q_norm, mla_kv_norm, mla_w_uq,
    mla_w_ukv, mla_out_norm, rwkv_mu_prev, rwkv_mu_next, rwkv_w0, rwkv_w2, rwkv_a0, rwkv_a2,
    rwkv_g2, rwkv_k_k, rwkv_k_a, rwkv_r_k, rwkv_gn_g, rwkv_gn_b, rwkv_v0, rwkv_v1, rwkv_v2,
    w_out, ln1_g, ln1_b, moe_w_group, moe_b_group, moe_w_expert, moe_b_expert, moe_w1, moe_w3,
    moe_w2, ln2_g, ln2_b, w_in_2, lambda_q1_2, lambda_k1_2, lambda_q2_2, lambda_k2_2, subln_g_2,
    gmlp_ln_g_2, gmlp_ln_b_2, w_spatial_2, b_spatial_2, w_out_2, ln1_g_2, ln1_b_2, w_gate_2,
    w_up_2, conv_w_2, conv_b_2, w_down_2, ln2_g_2, ln2_b_2,
):
    x = first_block(
        x, positions, meta_tokens, emb_ln_g, emb_ln_b, w_in, mla_q_norm, mla_kv_norm, mla_w_uq,
        mla_w_ukv, mla_out_norm, rwkv_mu_prev, rwkv_mu_next, rwkv_w0, rwkv_w2, rwkv_a0, rwkv_a2,
        rwkv_g2, rwkv_k_k, rwkv_k_a, rwkv_r_k, rwkv_gn_g, rwkv_gn_b, rwkv_v0, rwkv_v1, rwkv_v2,
        w_out, ln1_g, ln1_b, moe_w_group, moe_b_group, moe_w_expert, moe_b_expert, moe_w1,
        moe_w3, moe_w2, ln2_g, ln2_b,
    )
    return second_block(
        x, w_in_2, lambda_q1_2, lambda_k1_2, lambda_q2_2, lambda_k2_2, subln_g_2, gmlp_ln_g_2,
        gmlp_ln_b_2, w_spatial_2, b_spatial_2, w_out_2, ln1_g_2, ln1_b_2, w_gate_2, w_up_2,
        conv_w_2, conv_b_2, w_down_2, ln2_g_2, ln2_b_2,
    )


_drawn_inputs = setup_inputs


def setup_inputs(seed=0):
    import zlib

    import numpy as np

    out = dict(_drawn_inputs(seed))
    spreads = {}
    factors = {'mla_q_norm': 5.829,
     'mla_out_norm': 3.084,
     'rwkv_w2': 2.949,
     'rwkv_k_k': 6.218,
     'rwkv_k_a': 3.461,
     'rwkv_gn_g': 8.0,
     'rwkv_gn_b': 3.307,
     'moe_b_group': 8.0,
     'moe_b_expert': 8.0,
     'lambda_q1_2': 21.937,
     'lambda_k1_2': 28.874,
     'lambda_q2_2': 33.386}
    for name, (base, spread) in spreads.items():
        noise = np.random.default_rng([zlib.crc32(name.encode()), seed]).standard_normal(out[name].shape)
        drawn = base * np.exp(spread * noise) if base else spread * noise
        out[name] = __import__('jax').numpy.asarray(drawn.astype(out[name].dtype))
    for name, factor in factors.items():
        out[name] = (out[name] * factor).astype(out[name].dtype)
    return out
```

```python
import math
from contextlib import ExitStack

import numpy as np
import concourse.bass as bass
from concourse import mybir

ALU = mybir.AluOpType
ACT = mybir.ActivationFunctionType
AX = mybir.AxisListType
F32 = mybir.dt.float32
I32 = mybir.dt.int32

DEPTH, D, SEQ, NMETA = 2, 1024, 1024, 16
L = SEQ + NMETA
C, NT = 104, 10
GROUPS = [(0, 416), (416, 416), (832, 208)]
KAPPA = math.exp(-0.5)
ALPHA1 = 4.0 ** 0.25
ALPHA2 = 2.0 ** 0.25
NBLK = 48
NROWS = NBLK * 128
EH = 256
SKIP = 1 << 20
DFF = 2816
NF = DFF // 128
EPS = {1e-6: 0, 1e-5: 1, 64e-5: 2, 1e-12: 3, 0.0: 4}

CONSTS = [
    ("ident", 128), ("ones", 128), ("blk", 128), ("rot", 64), ("rot2", 128), ("seg", 416),
    ("mf", 7 * C), ("mb", 7 * C), ("qf", 2 * C), ("qb", 2 * C), ("tri", C),
    ("eps", 5), ("freq", 1), ("rev4", 4), ("rev8", 8), ("m128", 9), ("blkid", NBLK), ("pid", 1),
    ("tok2", 2 * NT), ("negrow", 128), ("lastcol", 128), ("causal", 128), ("metapos", NMETA),
]
COFF = {}
_o = 0
for _n, _w in CONSTS:
    COFF[_n] = (_o, _w)
    _o += _w
CW = _o


def make_consts():
    a = np.zeros((128, CW), np.float32)

    def put(name, v, rows=128):
        o, w = COFF[name]
        a[:rows, o:o + w] = v

    p = np.arange(128)[:, None]
    f = np.arange(128)[None, :]
    put("ident", p == f)
    put("ones", 1.0)
    put("blk", p // 64 == f // 64)
    f64 = np.arange(64)[None, :]
    p64 = np.arange(64)[:, None]
    put("rot", np.where(p64 == f64 + 32, -1.0, 0.0) + np.where(p64 == f64 - 32, 1.0, 0.0), 64)
    same = p // 64 == f // 64
    put("rot2", np.where(same & (p == f + 32) & (f % 64 < 32), -1.0, 0.0)
        + np.where(same & (p == f - 32) & (f % 64 >= 32), 1.0, 0.0))
    seg = np.ones(416)
    seg[::C] = 0.0
    put("seg", seg[None, :])
    s = np.arange(C)[:, None]
    t = np.arange(C)[None, :]
    mf, mb = [], []
    for lv in range(7):
        h = 1 << lv
        same = (s // (2 * h)) == (t // (2 * h))
        mf.append(same & (t % (2 * h) >= h) & (s % (2 * h) < h))
        mb.append(same & (s % (2 * h) >= h) & (t % (2 * h) < h))
    put("mf", np.concatenate(mf, 1), C)
    put("mb", np.concatenate(mb, 1), C)
    put("qf", np.concatenate([s < t, s <= t], 1), C)
    put("qb", np.concatenate([s > t, s >= t], 1), C)
    put("tri", s < t, C)
    for k, i in EPS.items():
        a[:, COFF["eps"][0] + i] = k
    put("freq", (np.float32(10000.0) ** (-(np.arange(64) % 32 * 2).astype(np.float32) / np.float32(64)))[:, None], 64)
    put("rev4", (4 - np.arange(4))[None, :])
    put("rev8", (8 - np.arange(8))[None, :])
    put("m128", (128 * np.arange(9))[None, :])
    put("blkid", np.arange(NBLK)[None, :])
    put("pid", p)
    tk = (np.arange(NT)[None, :, None] * C + np.arange(C)[:, None, None]) * 2 + np.arange(2)[None, None, :]
    put("tok2", tk.reshape(C, 2 * NT), C)
    put("negrow", np.where(f < 64, -1e30, 0.0))
    put("lastcol", f >= 64)
    put("causal", p <= f)
    put("metapos", np.arange(NMETA)[None, :])
    return a


COLUMNS = ["rwkv_mu_prev", "rwkv_mu_next", "mla_q_norm", "mla_kv_norm", "rwkv_k_k", "rwkv_k_a", "rwkv_w0",
           "rwkv_a0", "rwkv_v0", "rwkv_r_k", "conv_w_2", "conv_b_2"]


def lay_out(inputs):
    out = {n: np.ascontiguousarray(a) for n, a in inputs.items()}
    for n in COLUMNS:
        a = out[n]
        if n == "rwkv_r_k":
            a = a.reshape(a.shape[0], -1)
        out[n + "_c"] = np.ascontiguousarray(np.swapaxes(a.reshape(a.shape[:-1] + (-1, 128)), -1, -2))
    out["b_spatial_2_c"] = np.ascontiguousarray(np.swapaxes(out["b_spatial_2"], -1, -2))
    out["consts"] = make_consts()
    out["tables"] = make_tables()
    return out


def make_tables():
    pos = np.arange(SEQ, dtype=np.float32)
    inv = (1.0 / (np.float32(10000.0) ** (np.arange(0, 64, 2, dtype=np.float32) / np.float32(64)))).astype(np.float32)
    ang = (pos[:, None] * inv[None, :]).astype(np.float32).astype(np.float64)
    row = np.arange(128) % 32
    return np.stack([np.cos(ang)[:, row].T, np.sin(ang)[:, row].T], 1).astype(np.float32)


class Sem:
    def __init__(self, handle):
        self.handle = handle
        self.count = 0


class Queue:

    def __init__(self, sem, serial):
        self.sem, self.serial = sem, serial
        self.items, self.seen, self.fence = [], {}, []

    def now(self):
        return (self.sem, self.sem.count)

    def push(self, issue, toks, sem, step):
        waits = []
        for s, v in list(toks) + self.fence:
            if v > self.seen.get(s, 0):
                self.seen[s] = v
                waits.append((s, v))
        self.fence = []
        sem.count += step
        self.items.append((waits, issue, sem, step))
        return (sem, sem.count)

    def emit(self, eng):
        for waits, issue, sem, step in self.items:
            for s, v in waits:
                eng.wait_ge(s.handle, v)
            last = issue(eng)
            if step:
                last.then_inc(sem.handle, step)


class Program:
    def __init__(self, nc, ctx, T, upto):
        self.nc, self.T, self.upto = nc, T, upto
        self.ctx = ctx
        self.nsem = 0

        def q(serial):
            return Queue(self.sem(), serial)

        self.pe, self.act, self.dve, self.pool, self.sp = q(False), q(True), q(True), q(True), q(False)
        self.engs = [self.pe, self.act, self.dve, self.pool, self.sp]
        self.big = ctx.enter_context(nc.sbuf_tensor("big", [128, 53100], F32))
        self.ps = [ctx.enter_context(nc.psum_tensor(f"ps{i}", [128, 512], F32)) for i in range(8)]
        self.psfree = [[] for _ in range(8)]
        self.top = 0
        self.streams = {}
        self.K = {}

    def sem(self):
        self.nsem += 1
        return Sem(self.ctx.enter_context(self.nc.semaphore(f"s{self.nsem}")))

    def stream(self, name):
        if name not in self.streams:
            self.streams[name] = self.sem()
        return self.streams[name]

    def region(self, width):
        o = self.top
        self.top += width
        assert self.top <= 53100, self.top
        return self.big[:, o:o + width]

    def region2(self, a, b):
        return self.region(a * b).rearrange("p (a b) -> p a b", b=b)

    def region3(self, a, b, c):
        return self.region(a * b * c).rearrange("p (a b c) -> p a b c", b=b, c=c)

    def barrier(self):
        toks = [e.now() for e in self.engs if e.sem.count] + [(s, s.count) for s in self.streams.values() if s.count]
        for e in self.engs:
            e.fence = list(toks)
        self.psfree = [[] for _ in range(8)]

    def mms(self, mats, *toks):
        def issue(eng):
            for out, a, b, st, sp in mats:
                last = eng.matmul(out, a, b, start=st, stop=sp)
            return last
        return self.pe.push(issue, toks, self.pe.sem, 1)

    def trs(self, pairs, *toks):
        def issue(eng):
            for out, a in pairs:
                n = a.shape[0]
                last = eng.transpose(out, a, self.K["ident"][0:n, 0:n])
            return last
        return self.pe.push(issue, toks, self.pe.sem, 1)

    def step(self, q, issue, toks, after=True):
        toks = list(toks)
        if after and q.serial and q.sem.count:
            toks.append(q.now())
        return q.push(issue, toks, q.sem, 1)

    def v(self, issue, *toks, after=True):
        return self.step(self.dve, issue, toks, after)

    def a(self, issue, *toks, after=True):
        return self.step(self.act, issue, toks, after)

    def g(self, issue, *toks, after=True):
        return self.step(self.pool, issue, toks, after)

    def tt(self, q, out, x, y, op, *toks):
        return self.step(q, lambda e: e.tensor_tensor(out, x, y, op), toks)

    def copy(self, q, out, x, *toks):
        if q is self.act:
            return self.step(q, lambda e: e.activation(out, x, ACT.Copy), toks)
        return self.step(q, lambda e: e.tensor_copy(out, x), toks)

    def actf(self, out, x, f, *toks, bias=None, scale=1.0, accum=None):
        kw = {} if bias is None else {"bias": bias}
        return self.a(lambda e: e.activation(out, x, f, scale=scale, accum_out=accum, **kw), *toks)

    def dma(self, q, out, x, stream, *toks, **kw):
        s = self.stream(stream)
        return q.push(lambda e: e.dma_start(out, x, **kw), toks, s, 16)

    def gather(self, out, table, idx, bound, stream, *toks):
        s = self.stream(stream)
        return self.pool.push(lambda e: e.indirect_dma_start(
            out, None, table, bass.IndirectOffsetOnAxis(idx, 0), bounds_check=bound, oob_is_err=False), toks, s, 16)

    def scatter(self, table, idx, x, bound, stream, *toks):
        s = self.stream(stream)
        return self.pool.push(lambda e: e.indirect_dma_start(
            table, bass.IndirectOffsetOnAxis(idx, 0), x, None, bounds_check=bound, oob_is_err=False), toks, s, 16)


def rows(ap, n):
    return ap.unsqueeze(0).to_broadcast([n, ap.shape[0]])


def bc(ap, shape):
    return ap.to_broadcast(shape)


def layer_norm(P, x, n, gt, bt, tmp, st, eps, *toks):
    s12, mv, sd = tmp[0:n, 0:12], tmp[0:n, 12:14], tmp[0:n, 14:15]
    rs = tmp[0:n, 15:16]
    xx = x[0:n, :]
    P.v(lambda e: e.bn_stats(s12[:, 0:6], xx[:, 0:512]), *toks)
    P.v(lambda e: e.bn_stats(s12[:, 6:12], xx[:, 512:1024]))
    t = P.v(lambda e: e.bn_aggr(mv, s12))
    t = P.actf(sd, mv[:, 1:2], ACT.Sqrt, t, bias=P.K["eps"][0:n, EPS[eps]:EPS[eps] + 1])
    P.v(lambda e: e.reciprocal(rs, sd), t)
    P.v(lambda e: e.tensor_scalar(xx, xx, mv[:, 0:1], rs, ALU.subtract, ALU.mult))
    P.tt(P.dve, xx, xx, gt[0:n, :], ALU.mult)
    return P.tt(P.dve, xx, xx, bt[0:n, :], ALU.add)


def feature_major(P, x, n, hT, col, banks, tx):
    out = []
    for half in range(2):
        b = banks[half]
        psv = P.ps[b][:, 0:4 * n].rearrange("p (j t) -> p j t", t=n)
        t = P.trs([(psv[:, j, :], x[0:n, 128 * (4 * half + j):128 * (4 * half + j + 1)]) for j in range(4)],
                  tx, *P.psfree[b])
        q = P.act if half else P.dve
        t = P.copy(q, hT[:, 4 * half:4 * half + 4, col:col + n], psv, t)
        P.psfree[b] = [t]
        out.append(t)
    return out


def load_consts(P):
    P.cr = P.region(CW)
    for n, (o, w) in COFF.items():
        P.K[n] = P.cr[:, o:o + w]
    t = P.dma(P.sp, P.cr, P.T["consts"], "k")
    P.kt = t
    P.barrier()


def positions(P):
    T = P.T
    P.cos, P.sin = P.region(L), P.region(L)
    base = P.top
    pi = P.region(SEQ).bitcast(I32)
    six = P.region(SEQ).bitcast(I32)
    ang, k, r = P.region(L), P.region(L), P.region(L)
    n = 64
    t = P.dma(P.sp, pi[0:n, :], rows(T["positions"][0], n), "k")
    P.v(lambda e: e.memset(six[0:n, :], NMETA))
    P.tt(P.dve, pi[0:n, :], pi[0:n, :], six[0:n, :], ALU.add, t)
    P.copy(P.dve, ang[0:n, 0:NMETA], P.K["metapos"][0:n, :])
    P.copy(P.dve, ang[0:n, NMETA:L], pi[0:n, :])
    a, kk, rr = ang[0:n, :], k[0:n, :], r[0:n, :]
    P.v(lambda e: e.tensor_scalar(a, a, P.K["freq"][0:n, :], None, ALU.mult))
    magic = 1.5 * 2 ** 23
    P.v(lambda e: e.tensor_scalar(kk, a, float(np.float32(1 / (2 * math.pi))), magic, ALU.mult, ALU.add))
    P.v(lambda e: e.tensor_scalar(kk, kk, magic, None, ALU.subtract))
    two_pi = 2 * math.pi
    c1 = 6.28125
    c2 = float(np.float32(round((two_pi - c1) * 2 ** 19) / 2 ** 19))
    c3 = two_pi - c1 - c2
    P.v(lambda e: e.scalar_tensor_tensor(rr, kk, -c1, a, ALU.mult, ALU.add))
    P.v(lambda e: e.scalar_tensor_tensor(rr, kk, -c2, rr, ALU.mult, ALU.add))
    P.v(lambda e: e.scalar_tensor_tensor(rr, kk, -c3, rr, ALU.mult, ALU.add))
    t = P.v(lambda e: e.tensor_scalar(rr, rr, 3.1415925, -3.1415925, ALU.min, ALU.max))
    P.actf(P.sin[0:n, :], rr, ACT.Sin, t)
    t = P.actf(P.cos[0:n, :], rr, ACT.Sin, scale=0.5)
    co = P.cos[0:n, :]
    P.tt(P.dve, co, co, co, ALU.mult, t)
    P.v(lambda e: e.tensor_scalar(co, co, -2.0, 1.0, ALU.mult, ALU.add))
    P.barrier()
    P.top = base


def embed(P, hT):
    T = P.T
    base = P.top
    gt, bt = P.region(D), P.region(D)
    P.dma(P.sp, gt[0:C, :], rows(T["emb_ln_g"], C), "k")
    tg = P.dma(P.sp, bt[0:C, :], rows(T["emb_ln_b"], C), "k")
    xs = [P.region(D) for _ in range(3)]
    tmp = [P.region(16) for _ in range(3)]
    free = [[], [], []]
    for i in range(NT):
        s = i % 3
        x = xs[s]
        if i == 0:
            P.dma(P.sp, x[0:NMETA, :], T["meta_tokens"], f"x{s}", *free[s])
            t = P.dma(P.sp, x[NMETA:C, :], T["x"][0, 0:C - NMETA, :], f"x{s}", *free[s])
        else:
            t = P.dma(P.sp, x[0:C, :], T["x"][0, C * i - NMETA:C * (i + 1) - NMETA, :], f"x{s}", *free[s])
        t = layer_norm(P, x, C, gt, bt, tmp[s], None, 1e-5, t, tg)
        td = P.dma(P.sp, T["h"][C * i:C * (i + 1), :], x[0:C, :], f"ho{s}", t)
        free[s] = feature_major(P, x, C, hT, C * i, (2 * (i % 4), 2 * (i % 4) + 1), t) + [td]
    P.barrier()
    P.top = base


def project(P, li, hT, cq, ckv, kpe, u):
    T = P.T
    base = P.top
    NW = 3
    ws = [P.region2(8, 128) for _ in range(NW)]
    pt = [P.region(L + 2) for _ in range(2)]
    mu = P.region2(3, 15)
    tm = P.dma(P.sp, mu[:, 0, :], T["rwkv_mu_prev_c"][li], "k")
    tm = P.dma(P.sp, mu[:, 1, :], T["rwkv_mu_next_c"][li], "k")
    P.tt(P.dve, mu[:, 2, :], mu[:, 0, :], mu[:, 1, :], ALU.add, tm)
    tmu = P.v(lambda e: e.tensor_scalar(mu[:, 2, :], mu[:, 2, :], -1.0, 1.0, ALU.mult, ALU.add))
    for b in range(2):
        P.v(lambda e, b=b: e.memset(pt[b][:, 0:1], 0.0))
        tz = P.v(lambda e, b=b: e.memset(pt[b][:, L + 1:L + 2], 0.0))
    cols = [("q", 0, 0, 128), ("q", 1, 128, 128), ("kv", 0, 256, 128), ("pe", 0, 384, 64)]
    cols += [("u", j, 448 + 128 * j, 128) for j in range(15)]
    wfree = [[] for _ in range(NW)]
    pfree = [[], []]
    bank = 0
    for n, (kind, j, c0, m) in enumerate(cols):
        w = ws[n % NW]
        tw = P.dma(P.sp, w[:, :, 0:m], T["w_in"][li, :, c0:c0 + m].rearrange("(t p) n -> p t n", p=128),
                   f"w{n % NW}", *wfree[n % NW])
        ev = []
        for gi, (t0, tn) in enumerate(GROUPS):
            b = bank % 6
            bank += 1
            out = P.ps[b][0:m, 0:tn]
            t = P.mms([(out, w[:, k, 0:m], hT[:, k, t0:t0 + tn], k == 0, k == 7) for k in range(8)],
                      tw, *P.psfree[b])
            if kind == "u":
                dst = pt[j % 2][:, 1 + t0:1 + t0 + tn]
            else:
                dst = {"q": cq[:, j, :] if kind == "q" else None, "kv": ckv, "pe": kpe}[kind][0:m, t0:t0 + tn]
            te = P.copy(P.act, dst, out, t, *(pfree[j % 2] + [tz] if kind == "u" and gi == 0 else []))
            P.psfree[b] = [te]
            wfree[n % NW] = [t]
        if kind == "u":
            p = pt[j % 2]
            o = u[:, j, :]
            ta = P.a(lambda e, o=o, p=p, j=j: e.activation(o, p[:, 1:L + 1], ACT.Copy, scale=mu[:, 2, j:j + 1]), tmu)
            P.v(lambda e, o=o, p=p, j=j: e.scalar_tensor_tensor(
                o, p[:, 0:L], mu[:, 0, j:j + 1], o, ALU.mult, ALU.add), ta)
            tv = P.v(lambda e, o=o, p=p, j=j: e.scalar_tensor_tensor(
                o, p[:, 2:L + 2], mu[:, 1, j:j + 1], o, ALU.mult, ALU.add))
            pfree[j % 2] = [tv]
    P.barrier()
    P.top = base


def mla(P, li, cq, ckv, kpe):
    T = P.T
    base = P.top
    wuq = P.region2(2, 768)
    wkv = P.region(1024)
    gq, gkv = P.region(2), P.region(1)
    on = P.region(512)
    rk = P.region(L)
    raw = P.region(L)
    qn = P.region2(4, L)
    qp = P.region2(4, L)
    kn = P.region2(4, L)
    vt = P.region2(NT, 512)
    Pr = [P.region(L) for _ in range(2)]
    PT = [P.region2(NT, C) for _ in range(2)]
    st = [P.region(8) for _ in range(4)]
    ot = [rk[:, 0:512], rk[:, 512:1024]]
    sq = qn
    P.dma(P.sp, wuq, T["mla_w_uq"][li].rearrange("(t p) n -> p t n", p=128), "k")
    P.dma(P.sp, wkv, T["mla_w_ukv"][li], "k")
    P.dma(P.sp, gq, T["mla_q_norm_c"][li], "k")
    P.dma(P.sp, gkv, T["mla_kv_norm_c"][li], "k")
    tk = P.dma(P.sp, on[0:C, :], rows(T["mla_out_norm"][li], C), "k")
    for j in range(2):
        t1 = P.actf(sq[:, j, :], cq[:, j, :], ACT.Square)
    t1 = P.actf(sq[:, 2, :], ckv, ACT.Square)
    for which in range(2):
        parts = [0, 1] if which == 0 else [2]
        tl = []
        for g, (t0, tn) in enumerate(GROUPS):
            out = P.ps[g][:, 0:tn]
            t = P.mms([(out, P.K["ones"], sq[:, j, t0:t0 + tn], j == parts[0], j == parts[-1]) for j in parts],
                      t1, *P.psfree[g])
            te = P.actf(rk[:, t0:t0 + tn], out, ACT.Sqrt, t, bias=P.K["eps"][:, 0:1],
                        scale=1.0 / (128 * len(parts)))
            P.psfree[g] = [te]
        P.v(lambda e: e.reciprocal(rk, rk), te)
        if which == 0:
            for j in range(2):
                tv = P.v(lambda e, j=j: e.scalar_tensor_tensor(cq[:, j, :], cq[:, j, :], gq[:, j:j + 1], rk,
                                                               ALU.mult, ALU.mult), tk)
            P.act.fence.append(tv)
        else:
            tn_ = P.v(lambda e: e.scalar_tensor_tensor(ckv, ckv, gkv[:, 0:1], rk, ALU.mult, ALU.mult), tk)
    bank = 0

    def fm(dst, m, terms, *toks):
        nonlocal bank
        for t0, tn in GROUPS:
            b = bank % 6
            bank += 1
            out = P.ps[b][0:m, 0:tn]
            t = P.mms([(out, w, x[:, t0:t0 + tn], i == 0, i == len(terms) - 1) for i, (w, x) in enumerate(terms)],
                      *toks, *P.psfree[b])
            te = P.copy(P.act, dst[0:m, t0:t0 + tn], out, t)
            P.psfree[b] = [te]
        return te

    def rope(dst, src, ts):
        nonlocal bank
        tm = None
        for t0, tn in GROUPS:
            b = bank % 6
            bank += 1
            out = P.ps[b][0:64, 0:tn]
            t = P.mms([(out, P.K["rot"][0:64, 0:64], src[0:64, t0:t0 + tn], True, True)], ts, *P.psfree[b])
            P.tt(P.dve, raw[0:64, t0:t0 + tn], out, P.sin[0:64, t0:t0 + tn], ALU.mult, t)
            P.tt(P.dve, dst[0:64, t0:t0 + tn], src[0:64, t0:t0 + tn], P.cos[0:64, t0:t0 + tn], ALU.mult)
            tm = P.tt(P.dve, dst[0:64, t0:t0 + tn], dst[0:64, t0:t0 + tn], raw[0:64, t0:t0 + tn], ALU.add)
            P.psfree[b] = [tm]
        return tm

    tr = rope(kpe, kpe, tn_)
    for h in range(4):
        tq = fm(qn[:, h, :], 128, [(wuq[:, j, 192 * h:192 * h + 128], cq[:, j, :]) for j in range(2)], tk, tn_)
        tp = fm(qp[:, h, :], 64, [(wuq[:, j, 192 * h + 128:192 * h + 192], cq[:, j, :]) for j in range(2)])
        tr = rope(qp[:, h, :], qp[:, h, :], tp)
        tq = fm(kn[:, h, :], 128, [(wkv[:, 256 * h:256 * h + 128], ckv)])
    for i in range(NT):
        b = bank % 6
        bank += 1
        wv = wkv.rearrange("p (h e) -> p h e", h=4)[:, :, 128:256]
        t = P.mms([(P.ps[b][0:C, 0:512].rearrange("p (h e) -> p h e", h=4), ckv[:, C * i:C * i + C], wv, True, True)],
                  *P.psfree[b])
        tv = P.copy(P.act, vt[0:C, i, :], P.ps[b][0:C, 0:512], t)
        P.psfree[b] = [tv]
    scale = 192.0 ** -0.5
    prfree, ptfree, ofree = [[], []], [[], []], [[], []]
    items = [(i, h) for i in range(NT) for h in range(4)]
    tsc = {}

    def scores(n):
        i, h = items[n]
        s = 0
        free = [x for b in range(3) for x in P.psfree[b]]
        mats = []
        for b, (t0, tn) in enumerate(GROUPS):
            mats.append((P.ps[b][0:C, 0:tn], qn[:, h, C * i:C * i + C], kn[:, h, t0:t0 + tn], True, False))
            mats.append((P.ps[b][0:C, 0:tn], qp[0:64, h, C * i:C * i + C], kpe[0:64, t0:t0 + tn], False, True))
        tsc[n] = P.mms(mats, tv, tr, tq, *free)

    scores(0)
    for n, (i, h) in enumerate(items):
        p = Pr[n % 2]
        z = st[n % 4]
        for b, (t0, tn) in enumerate(GROUPS):
            tx = P.v(lambda e, b=b, tn=tn, z=z: e.tensor_reduce(z[0:C, b:b + 1], P.ps[b][0:C, 0:tn], AX.X, ALU.max),
                     tsc[n])
        P.v(lambda e, z=z: e.tensor_reduce(z[0:C, 3:4], z[0:C, 0:3], AX.X, ALU.max))
        tm = P.v(lambda e, z=z: e.tensor_scalar(z[0:C, 3:4], z[0:C, 3:4], -scale, None, ALU.mult))
        for b, (t0, tn) in enumerate(GROUPS):
            te = P.actf(p[0:C, t0:t0 + tn], P.ps[b][0:C, 0:tn], ACT.Exp, tm, *prfree[n % 2],
                        bias=z[0:C, 3:4], scale=scale, accum=z[0:C, 4 + b:5 + b])
            P.psfree[b] = [te]
        if n + 1 < len(items):
            scores(n + 1)
        pt = PT[n % 2]
        for b in range(3):
            lo, hi = 4 * b, min(4 * b + 4, NT)
            pv = P.ps[3 + b][0:C, 0:C * (hi - lo)].rearrange("p (j t) -> p j t", t=C)
            t = P.trs([(pv[:, j - lo, :], p[0:C, C * j:C * j + C]) for j in range(lo, hi)], te, *P.psfree[3 + b])
            q = P.dve if b < 2 else P.act
            tc = P.copy(q, pt[0:C, lo:hi, :], pv, t, *ptfree[n % 2])
            P.psfree[3 + b] = [tc]
            if b == 1:
                tc1 = tc
        prfree[n % 2] = [t]
        ob = 6 + n % 2
        out = P.ps[ob][0:C, 0:128]
        t = P.mms([(out, pt[0:C, j, :], vt[0:C, j, 128 * h:128 * h + 128], j == 0, j == NT - 1) for j in range(NT)],
                  tc, tc1, *P.psfree[ob])
        ptfree[n % 2] = [t]
        o = ot[i % 2][0:C, 128 * h:128 * h + 128]
        P.v(lambda e, z=z: e.tensor_reduce(z[0:C, 7:8], z[0:C, 4:7], AX.X, ALU.add), te)
        P.v(lambda e, z=z: e.reciprocal(z[0:C, 7:8], z[0:C, 7:8]))
        to = P.v(lambda e, o=o, out=out, z=z: e.tensor_scalar(o, out, z[0:C, 7:8], None, ALU.mult), t, *ofree[i % 2])
        P.psfree[ob] = [to]
        t = P.actf(raw[0:C, 0:128], o, ACT.Square, to, accum=z[0:C, 0:1])
        t = P.actf(z[0:C, 1:2], z[0:C, 0:1], ACT.Sqrt, bias=P.K["eps"][0:C, 0:1], scale=1.0 / 128)
        P.v(lambda e, z=z: e.reciprocal(z[0:C, 1:2], z[0:C, 1:2]), t)
        to = P.v(lambda e, o=o, z=z, h=h: e.scalar_tensor_tensor(o, o, z[0:C, 1:2], on[0:C, 128 * h:128 * h + 128],
                                                                 ALU.mult, ALU.mult))
        if h == 3:
            ofree[i % 2] = [P.dma(P.sp, T["mix"][C * i:C * i + C, 0:512], ot[i % 2][0:C, :], f"ho{i % 2}", to)]
    P.barrier()
    P.top = base


def rwkv(P, li, u):
    T = P.T
    base = P.top
    r, k, v = u[:, 0:4, :], u[:, 4:8, :], u[:, 8:12, :]
    kk = P.region2(4, L)
    par = P.region2(9, 4)
    names = [("rwkv_k_k", None), ("rwkv_k_a", None), ("rwkv_w0", 0), ("rwkv_w0", 1), ("rwkv_a0", 0), ("rwkv_a0", 1)]
    for i, (n, d) in enumerate(names):
        src = T[n + "_c"][li] if d is None else T[n + "_c"][li, d]
        tp = P.dma(P.sp, par[:, i, :], src, "k")
    tp = P.dma(P.sp, par[:, 6, :], T["rwkv_r_k_c"][li], "k")
    w2, a2 = P.region(512), P.region(512)
    for d in range(2):
        P.dma(P.sp, w2[64 * d:64 * d + 64, :], T["rwkv_w2"][li, d], "k")
        tp = P.dma(P.sp, a2[64 * d:64 * d + 64, :], T["rwkv_a2"][li, d], "k")
    P.v(lambda e: e.tensor_scalar(par[:, 7, :], par[:, 1, :], -1.0, 1.0, ALU.mult, ALU.add), tp)
    rk2 = P.region2(4, 2)
    tb = P.tt(P.dve, rk2, bc(par[:, 6, :].unsqueeze(2), [128, 4, 2]),
              bc(P.K["blk"][:, 0:128:64].unsqueeze(1), [128, 4, 2]), ALU.mult)
    tmpb = P.top
    if li == 0:
        P.dma(P.sp, T["vfirst"].rearrange("p (j t) -> p j t", j=4), v, "vf")
    else:
        vf = P.region2(4, 416)
        v1, v2, v0, t32 = P.region2(4, 32), P.region(512), P.region(4), P.region(416)
        gate = P.region(416)
        P.dma(P.sp, v1, T["rwkv_v1"][li - 1].rearrange("(t p) n -> p t n", p=128), "k2")
        P.dma(P.sp, v2[0:32, :], T["rwkv_v2"][li - 1], "k2")
        tk = P.dma(P.sp, v0, T["rwkv_v0_c"][li - 1], "k2")
        vd = T["vfirst"].rearrange("p (j t) -> p j t", j=4)
        tv = None
        for t0, tn in GROUPS:
            tf = P.dma(P.sp, vf[:, :, 0:tn], vd[:, :, t0:t0 + tn], "vf", *([tv] if tv else []))
            t = P.mms([(P.ps[0][0:32, 0:tn], v1[:, j, :], v[:, j, t0:t0 + tn], j == 0, j == 3) for j in range(4)],
                      tk, *P.psfree[0])
            te = P.copy(P.act, t32[0:32, 0:tn], P.ps[0][0:32, 0:tn], t)
            P.psfree[0] = [te]
            for j in range(4):
                t = P.mms([(P.ps[1 + j][:, 0:tn], v2[0:32, 128 * j:128 * j + 128], t32[0:32, 0:tn], True, True)],
                          te, *P.psfree[1 + j])
                tg = P.actf(gate[:, 0:tn], P.ps[1 + j][:, 0:tn], ACT.Sigmoid, t, *([tv] if tv else []),
                            bias=v0[:, j:j + 1])
                P.psfree[1 + j] = [tg]
                P.tt(P.dve, vf[:, j, 0:tn], vf[:, j, 0:tn], v[:, j, t0:t0 + tn], ALU.subtract, tf, tg)
                P.tt(P.dve, vf[:, j, 0:tn], vf[:, j, 0:tn], gate[:, 0:tn], ALU.mult)
                tv = P.tt(P.dve, v[:, j, t0:t0 + tn], v[:, j, t0:t0 + tn], vf[:, j, 0:tn], ALU.add)
        P.barrier()
        P.top = tmpb
    sq = P.region(L)
    ls = None
    for j in range(4):
        tv = P.v(lambda e, j=j: e.tensor_scalar(kk[:, j, :], k[:, j, :], par[:, 0, j:j + 1], None, ALU.mult), tp)
        ts = P.actf(sq, kk[:, j, :], ACT.Square, tv, *([ls] if ls else []))
        for g, (t0, tn) in enumerate(GROUPS):
            out = P.ps[g][:, 0:tn]
            t = P.mms([(out, P.K["blk"], sq[:, t0:t0 + tn], True, True)], ts, *P.psfree[g])
            te = P.actf(sq[:, t0:t0 + tn], out, ACT.Sqrt, t, bias=P.K["eps"][:, 3:4])
            P.psfree[g] = [te]
        P.v(lambda e: e.reciprocal(sq, sq), te)
        ls = P.tt(P.dve, kk[:, j, :], kk[:, j, :], sq, ALU.mult)
    P.actf(u[:, 12, :], u[:, 12, :], ACT.Tanh)
    P.actf(u[:, 14, :], u[:, 14, :], ACT.Sigmoid)
    P.barrier()
    P.top = tmpb
    y = P.region2(NT, 512)
    bon = P.region2(NT, 8)
    S = [P.region2(4, 64) for _ in range(2)]
    tot = [P.region(4) for _ in range(2)]
    fac = [P.region(8) for _ in range(2)]
    sig, cs, ea, ei, aa, x1 = (P.region2(4, C) for _ in range(6))
    W = []
    for d in range(2):
        W.append(dict(kr=P.region3(4, 2, C), hb=P.region3(2, 4, C), tm=P.region2(2, 512), vt=P.region(512),
                      ak=P.region3(8, 2, C), ab=P.region3(8, 2, C)))
    T1, TT, XX, LM, = P.region2(8, C), P.region2(8, C), P.region2(8, C), P.region2(8, C)
    TTd = [TT, P.region2(8, C)]
    rh, uu = P.region(512), P.region(512)
    tS = [None, None]
    for d in range(2):
        P.v(lambda e, d=d: e.memset(S[d], 0.0))
    chain_done = [[], []]
    t1free = []

    def prep(i, d):
        nonlocal t1free
        w = W[d]
        c0 = C * i
        sl = slice(c0, c0 + C)
        base_r = slice(64 * d, 64 * d + 64)
        b = 0
        psw = P.ps[0][:, 0:416].rearrange("p (j t) -> p j t", t=C)
        psa = P.ps[1][:, 0:416].rearrange("p (j t) -> p j t", t=C)
        t0 = P.mms([(psw[:, j, :], w2[base_r, 128 * j:128 * j + 128], u[base_r, 12, sl], True, True) for j in range(4)],
                   *P.psfree[0])
        t1 = P.mms([(psa[:, j, :], a2[base_r, 128 * j:128 * j + 128], u[base_r, 13, sl], True, True) for j in range(4)],
                   *P.psfree[1])
        P.tt(P.dve, sig, psw, bc(par[:, 2 + d, :].unsqueeze(2), [128, 4, C]), ALU.add, t0)
        ta = P.tt(P.dve, aa, psa, bc(par[:, 4 + d, :].unsqueeze(2), [128, 4, C]), ALU.add, t1)
        P.psfree[0] = [ta]
        P.psfree[1] = [ta]
        ts = P.actf(sig, sig, ACT.Sigmoid, ta)
        ta = P.actf(aa, aa, ACT.Sigmoid)
        P.v(lambda e: e.tensor_tensor_scan(cs.rearrange("p j t -> p (j t)"), P.K["seg"],
                                           sig.rearrange("p j t -> p (j t)"), 0.0, ALU.mult, ALU.add), ts)
        ot = fac[d]
        P.copy(P.dve, ot[:, 4:8], tot[d]) if tS[d] is not None else None
        P.copy(P.dve, tot[d], cs[:, :, C - 1])
        P.v(lambda e: e.scalar_tensor_tensor(cs, bc(tot[d].unsqueeze(2), [128, 4, C]), -0.5, cs, ALU.mult, ALU.add))
        tc = P.tt(P.dve, x1, *((cs, sig) if d == 0 else (sig, cs)), ALU.subtract)
        kr, hb = w["kr"], w["hb"]
        sR = -KAPPA
        if d == 0:
            P.actf(ea, cs, ACT.Exp, tc, scale=-KAPPA)
            P.actf(ei, cs, ACT.Exp, scale=KAPPA)
            te = P.actf(x1, x1, ACT.Exp, scale=-KAPPA)
            eK = x1
        else:
            P.actf(sig, cs, ACT.Exp, tc, scale=KAPPA)
            P.actf(ea, x1, ACT.Exp, scale=-KAPPA)
            te = P.actf(ei, x1, ACT.Exp, scale=KAPPA)
            eK = sig
        free = chain_done[d]
        P.tt(P.dve, kr[:, :, 0, :], kk[:, :, sl], eK, ALU.mult, te, *free)
        tk = P.tt(P.dve, kr[:, :, 1, :], r[:, :, sl], ea, ALU.mult)
        t = P.v(lambda e: e.scalar_tensor_tensor(hb[:, 1, :, :], aa, -1.0, kk[:, :, sl], ALU.mult, ALU.mult), ta)
        P.tt(P.dve, hb[:, 1, :, :], hb[:, 1, :, :], ei, ALU.mult)
        P.tt(P.dve, aa, aa, bc(par[:, 1, :].unsqueeze(2), [128, 4, C]), ALU.mult)
        P.tt(P.dve, aa, aa, bc(par[:, 7, :].unsqueeze(2), [128, 4, C]), ALU.add)
        P.tt(P.dve, aa, aa, k[:, :, sl], ALU.mult)
        th = P.tt(P.dve, hb[:, 0, :, :], aa, ei, ALU.mult)
        tz = P.tt(P.dve, ea, r[:, :, sl], aa, ALU.mult)
        t = P.mms([(P.ps[0][0:C, 2 * j:2 * j + 2], ea[:, j, :], rk2[:, j, :], True, True) for j in range(4)],
                  tz, *P.psfree[0])
        if first(i, d):
            tb = P.copy(P.dve, bon[0:C, i, :], P.ps[0][0:C, 0:8], t)
        else:
            tb = P.tt(P.dve, bon[0:C, i, :], bon[0:C, i, :], P.ps[0][0:C, 0:8], ALU.add, t)
        P.psfree[0] = [tb]
        for m in range(2):
            bk = 1 + m
            pv = P.ps[bk][0:C, 0:512].rearrange("p (j c) -> p j c", c=128)
            t = P.trs([(pv[:, j, :], hb[:, m, j, :]) for j in range(4)], th, *P.psfree[bk])
            tc = P.copy(P.act, w["tm"][0:C, m, :], P.ps[bk][0:C, :], t, *free)
            P.psfree[bk] = [tc]
        pv = P.ps[3][0:C, 0:512].rearrange("p (j c) -> p j c", c=128)
        t = P.trs([(pv[:, j, :], v[:, j, sl]) for j in range(4)], *P.psfree[3])
        tc = P.copy(P.act, w["vt"][0:C, :], P.ps[3][0:C, :], t)
        P.psfree[3] = [tc]
        bk = 4
        for m, dst in ((1, w["ab"]), (0, w["ak"])):
            for o in range(2):
                pr = slice(64 * o, 64 * o + 64)
                for jj in range(2):
                    b = bk % 8
                    bk += 1
                    mats = [(P.ps[b][0:C, 208 * x:208 * x + 208].rearrange("p (a t) -> p a t", a=2),
                             hb[pr, m, 2 * jj + x, :], kr[pr, 2 * jj + x, :, :], True, True) for x in range(2)]
                    t = P.mms(mats, th, *P.psfree[b])
                    pv = P.ps[b][0:C, 0:416].rearrange("p (o x) -> p o x", o=2)
                    h0 = 4 * o + 2 * jj
                    mk = bc(P.K["qf" if d == 0 else "qb"][0:C, :].unsqueeze(1), [C, 2, 2 * C])
                    tA = P.tt(P.dve, dst[0:C, h0:h0 + 2, :, :].rearrange("p o a t -> p o (a t)"), pv, mk, ALU.mult, t)
                    P.psfree[b] = [tA]
            if m == 1:
                tB = tA
        mk = P.K["mf" if d == 0 else "mb"]
        TTx = TTd[d]
        ident = bc(P.K["ident"][0:C, 0:C].unsqueeze(1), [C, 4, C])
        tT = [None, None]
        for lv in range(7):
            for g in range(2):
                hs = slice(4 * g, 4 * g + 4)
                lm = P.tt(P.pool, LM[0:C, hs, :], w["ab"][0:C, hs, 0, :],
                          bc(mk[0:C, C * lv:C * lv + C].unsqueeze(1), [C, 4, C]), ALU.mult, tB, *t1free)
                bx = 3 * g
                pv = P.ps[bx][0:C, 0:416].rearrange("p (j t) -> p j t", t=C)
                if lv == 0:
                    t = P.mms([(pv[:, j, :], LM[0:C, 4 * g + j, :], P.K["ident"][0:C, 0:C], True, True)
                               for j in range(4)], lm, *P.psfree[bx])
                    P.tt(P.dve, T1[0:C, hs, :], pv, ident, ALU.add, t)
                    tT[g] = P.tt(P.dve, TTx[0:C, hs, :], LM[0:C, hs, :], ident, ALU.add)
                    P.psfree[bx] = [tT[g]]
                    continue
                t = P.mms([(pv[:, j, :], LM[0:C, 4 * g + j, :], T1[0:C, 4 * g + j, :], True, True)
                           for j in range(4)], lm, tT[g], *P.psfree[bx])
                tx = P.copy(P.act, XX[0:C, hs, :], pv, t)
                P.psfree[bx] = [tx]
                pa = P.ps[bx + 1][0:C, 0:416].rearrange("p (j t) -> p j t", t=C)
                pb = P.ps[bx + 2][0:C, 0:416].rearrange("p (j t) -> p j t", t=C)
                t2 = P.mms([(pb[:, j, :], XX[0:C, 4 * g + j, :], TTx[0:C, 4 * g + j, :], True, True)
                            for j in range(4)], tx, *P.psfree[bx + 2])
                if lv < 6:
                    t = P.mms([(pa[:, j, :], TTx[0:C, 4 * g + j, :], XX[0:C, 4 * g + j, :], True, True)
                               for j in range(4)], tx, *P.psfree[bx + 1])
                    t3 = P.tt(P.dve, T1[0:C, hs, :], T1[0:C, hs, :], pa, ALU.add, t)
                    P.psfree[bx + 1] = [t3]
                tT[g] = P.tt(P.dve, TTx[0:C, hs, :], TTx[0:C, hs, :], pb, ALU.add, t2)
                P.psfree[bx + 2] = [tT[g]]
            t1free = [tT[0], tT[1], P.pe.now()]
        return tT, tA, tc

    def first(i, d):
        return i < 5 if d == 0 else i >= 5

    def chain(i, d, toks):
        w = W[d]
        tT, tA, tc = toks
        Sd = S[d]
        c0 = C * i
        kr = w["kr"]
        TTx = TTd[d]
        f = fac[d]
        if tS[d] is None:
            tf = P.v(lambda e: e.memset(f[:, 0:4], 0.0))
        else:
            t = P.tt(P.dve, f[:, 0:4], f[:, 4:8], tot[d], ALU.add)
            tf = P.actf(f[:, 0:4], f[:, 0:4], ACT.Exp, t, scale=-0.5 * KAPPA)
        tS[d] = P.tt(P.dve, Sd, Sd, bc(f[:, 0:4].unsqueeze(2), [128, 4, 64]), ALU.mult, tf)
        hd = [(4 * o + j, slice(64 * o, 64 * o + 64), j, slice(128 * j + 64 * o, 128 * j + 64 * o + 64))
              for o in range(2) for j in range(4)]
        tr = []
        for o in range(2):
            mats = []
            for g, pr, j, hc in hd[4 * o:4 * o + 4]:
                dst = P.ps[6 + o][0:C, 64 * j:64 * j + 64]
                mats.append((dst, kr[pr, j, 0, :], Sd[pr, j, :], True, False))
                mats.append((dst, w["ak"][0:C, g, 0, :], w["vt"][0:C, hc], False, True))
            t = P.mms(mats, tS[d], tA, tc, *P.psfree[6 + o])
            tr.append(P.copy(P.act, rh[0:C, 256 * o:256 * o + 256], P.ps[6 + o][0:C, 0:256], t))
            P.psfree[6 + o] = [tr[-1]]
        t = P.mms([(P.ps[5][0:C, 64 * g:64 * g + 64], TTx[0:C, g, :], rh[0:C, 64 * g:64 * g + 64], True, True)
                   for g, pr, j, hc in hd], *tr, *tT, *P.psfree[5])
        t = P.copy(P.act, uu[0:C, :], P.ps[5][0:C, :], t)
        P.psfree[5] = [t]
        mats = []
        for g, pr, j, hc in hd:
            o = P.ps[0][pr, 64 * j:64 * j + 64]
            mats.append((o, w["tm"][0:C, 0, hc], w["vt"][0:C, hc], True, False))
            mats.append((o, w["tm"][0:C, 1, hc], uu[0:C, 64 * g:64 * g + 64], False, True))
        ts = P.mms(mats, t, *P.psfree[0])
        for o in range(2):
            mats = []
            for g, pr, j, hc in hd[4 * o:4 * o + 4]:
                dst = P.ps[1 + o][0:C, 64 * j:64 * j + 64]
                mats.append((dst, kr[pr, j, 1, :], Sd[pr, j, :], True, False))
                mats.append((dst, w["ak"][0:C, g, 1, :], w["vt"][0:C, hc], False, False))
                mats.append((dst, w["ab"][0:C, g, 1, :], uu[0:C, 64 * g:64 * g + 64], False, True))
            ty = P.mms(mats, *P.psfree[1 + o])
            yv = y[0:C, i, :].rearrange("p (j o n) -> p o j n", o=2, n=64)[:, o, :, :]
            pv = P.ps[1 + o][0:C, 0:256].rearrange("p (j n) -> p j n", n=64)
            if first(i, d):
                t = P.copy(P.dve, yv, pv, ty)
            else:
                t = P.tt(P.dve, yv, yv, pv, ALU.add, ty)
            P.psfree[1 + o] = [t]
        t = P.tt(P.dve, Sd, Sd, P.ps[0][:, 0:256].rearrange("p (j c) -> p j c", c=64), ALU.add, ts)
        P.psfree[0] = [t]
        chain_done[d] = [ty]

    for i in range(NT):
        a = prep(i, 0)
        chain(i, 0, a)
        a = prep(NT - 1 - i, 1)
        chain(NT - 1 - i, 1, a)
    P.barrier()
    P.top = tmpb
    y = P.region2(NT, 512)
    bon = P.region2(NT, 8)
    g2, gng, gnb = P.region(512), P.region(512), P.region(512)
    P.dma(P.sp, g2, T["rwkv_g2"][li], "k")
    P.dma(P.sp, gng[0:C, :], rows(T["rwkv_gn_g"][li], C), "k")
    tk = P.dma(P.sp, gnb[0:C, :], rows(T["rwkv_gn_b"][li], C), "k")
    sqs = [P.region(512) for _ in range(2)]
    st = [P.region2(3, 8) for _ in range(2)]
    for i in range(NT):
        b = 2 * (i % 4)
        yy = y[0:C, i, :]
        y3 = yy.rearrange("p (h n) -> p h n", h=8)
        s = st[i % 2]
        q = sqs[i % 2][0:C, :]
        q3 = q.rearrange("p (h n) -> p h n", h=8)
        m, vr = s[0:C, 0, :], s[0:C, 1, :]
        pv = P.ps[b][0:C, 0:512].rearrange("p (j c) -> p j c", c=128)
        tvt = P.trs([(pv[:, j, :], v[:, j, C * i:C * i + C]) for j in range(4)], *P.psfree[b])
        tgt = P.mms([(P.ps[b + 1][0:C, :], u[:, 14, C * i:C * i + C], g2, True, True)], tk, *P.psfree[b + 1])
        P.v(lambda e, m=m, y3=y3: e.tensor_reduce(m, y3, AX.X, ALU.add))
        P.v(lambda e, m=m: e.tensor_scalar(m, m, 1.0 / 64, None, ALU.mult))
        t = P.tt(P.dve, y3, y3, bc(m.unsqueeze(2), [C, 8, 64]), ALU.subtract)
        t = P.actf(q, yy, ACT.Square, t)
        t = P.v(lambda e, vr=vr, q3=q3: e.tensor_reduce(vr, q3, AX.X, ALU.add), t)
        t = P.actf(vr, vr, ACT.Sqrt, t, bias=P.K["eps"][0:C, 2:3], scale=1.0 / 64)
        P.v(lambda e, vr=vr: e.reciprocal(vr, vr), t)
        P.tt(P.dve, y3, y3, bc(vr.unsqueeze(2), [C, 8, 64]), ALU.mult)
        P.tt(P.dve, yy, yy, gng[0:C, :], ALU.mult, tk)
        P.tt(P.dve, yy, yy, gnb[0:C, :], ALU.add)
        t = P.tt(P.dve, q3, P.ps[b][0:C, :].rearrange("p (h n) -> p h n", h=8),
                 bc(bon[0:C, i, :].unsqueeze(2), [C, 8, 64]), ALU.mult, tvt)
        P.psfree[b] = [t]
        P.tt(P.dve, yy, yy, q, ALU.add)
        t = P.tt(P.dve, yy, yy, P.ps[b + 1][0:C, :], ALU.mult, tgt)
        P.psfree[b + 1] = [t]
        P.dma(P.sp, T["mix"][C * i:C * i + C, 512:1024], yy, "ho2", t)
    P.barrier()
    P.top = base


def reload_transposed(P, hT):
    base = P.top
    xs = [P.region(D) for _ in range(4)]
    free = [[] for _ in range(4)]
    for i in range(NT):
        s = i % 4
        t = P.dma(P.sp, xs[s][0:C, :], P.T["h"][C * i:C * (i + 1), :], f"x{s}", *free[s])
        free[s] = feature_major(P, xs[s], C, hT, C * i, (2 * (i % 4), 2 * (i % 4) + 1), t)
    P.barrier()
    P.top = base


def mixer_out(P, li):
    T = P.T
    P.gates = P.region2(2, NT)
    P.slots = P.region(NBLK).bitcast(I32)
    P.toks = P.region(NBLK).bitcast(I32)
    P.widx = P.region(NBLK).bitcast(I32)
    base = P.top
    lg = P.region2(NT, 36)
    bias = P.region(36)
    wr = P.region2(8, 36)
    wo = P.region2(8, D)
    gt, bt = P.region(D), P.region(D)
    mx = [P.region(D) for _ in range(2)]
    hx = [P.region(D) for _ in range(2)]
    x1 = [P.region(D) for _ in range(2)]
    mT = [P.region2(8, C) for _ in range(2)]
    hT = [P.region2(8, C) for _ in range(2)]
    tmp = [P.region(16) for _ in range(2)]
    loads = {}

    def load(i):
        s = i % 2
        a = P.dma(P.sp, mx[s][0:C, :], T["mix"][C * i:C * i + C, :], f"x{s}", *mfree[s])
        b = P.dma(P.sp, hx[s][0:C, :], T["h"][C * i:C * i + C, :], f"x{2 + s}", *hfree[s])
        loads[i] = (a, b)

    mfree, hfree, xfree = [[], []], [[], []], [[], []]
    load(0)
    tw = P.dma(P.act, wo, T["w_out"][li].rearrange("(t p) n -> p t n", p=128), "w0")
    P.dma(P.sp, gt[0:C, :], rows(T["ln1_g"][li], C), "k")
    P.dma(P.sp, bt[0:C, :], rows(T["ln1_b"][li], C), "k")
    P.dma(P.sp, wr[:, :, 0:4], T["moe_w_group"][li].rearrange("(t p) n -> p t n", p=128), "k")
    P.dma(P.sp, wr[:, :, 4:36], T["moe_w_expert"][li].rearrange("(t p) n -> p t n", p=128), "k")
    P.dma(P.sp, bias[0:C, 0:4], rows(T["moe_b_group"][li], C), "k")
    tk = P.dma(P.sp, bias[0:C, 4:36], rows(T["moe_b_expert"][li], C), "k")
    for i in range(NT):
        s = i % 2
        if i + 1 < NT:
            load(i + 1)
        ta, tb = loads[i]
        tt = feature_major(P, mx[s], C, mT[s], 0, (0, 1), ta)
        mfree[s] = [P.pe.now()]
        x = x1[s]
        ts = []
        for c in range(2):
            b = 2 + c + 2 * (i % 2)
            t = P.mms([(P.ps[b][0:C, :], mT[s][:, k, :], wo[:, k, 512 * c:512 * c + 512], k == 0, k == 7)
                       for k in range(8)], tw, *tt, *P.psfree[b])
            t = P.v(lambda e, x=x, s=s, c=c, b=b: e.scalar_tensor_tensor(
                x[0:C, 512 * c:512 * c + 512], hx[s][0:C, 512 * c:512 * c + 512], ALPHA1, P.ps[b][0:C, :],
                ALU.mult, ALU.add), t, tb, *xfree[s])
            P.psfree[b] = [t]
        hfree[s] = [t]
        t = layer_norm(P, x, C, gt, bt, tmp[s], None, 1e-5, tk, t)
        td = P.dma(P.sp, T["h"][C * i:C * i + C, :], x[0:C, :], f"ho{s}", t)
        tt = feature_major(P, x, C, hT[s], 0, (6, 7), t)
        xfree[s] = tt + [td]
        t = P.mms([(P.ps[6][0:C, 0:36], hT[s][:, k, :], wr[:, k, :], k == 0, k == 7) for k in range(8)], *tt)
        t = P.copy(P.act, lg[0:C, i, :], P.ps[6][0:C, 0:36], t)
        P.psfree[6] = [t]
    P.barrier()
    P.top = base + NT * 36 + 36
    n = C

    def r3(w):
        return P.region2(NT, w)[0:n]

    lgc = lg[0:n]
    col = [P.region(NT)[0:n, :] for _ in range(8)]
    gm, gs, gp, em, es_, m2, p2, mx4 = col
    eg, og, sc = r3(4), r3(4), r3(4)
    es, ex, o1, o2, sc8 = r3(8), r3(8), r3(8), r3(8), r3(8)
    O1, O2, OO, run, rk = r3(32), r3(32), r3(32), r3(32), r3(32)
    tot, cnt, nb, cum, start = (P.region(32) for _ in range(5))
    cm9 = P.region2(32, 9)
    cmb = P.region2(NBLK, 32)
    eb = P.region(NBLK)
    dst = P.region2(2, NT)[0:n]
    di = P.region2(2, NT).bitcast(I32)[0:n]
    dq = P.region2(2, NT).bitcast(I32)[0:n]
    dr = P.region2(2, NT).bitcast(I32)[0:n]
    tv = P.region(2 * NT).bitcast(I32)
    full = P.region(NBLK).bitcast(I32)

    def b3(x, w):
        return bc(x.unsqueeze(2), [n, NT, w])

    def first_of(out, x, m, score, rev, w):
        P.tt(P.dve, score, x, b3(m, w), ALU.is_equal)
        P.tt(P.dve, score, score, bc(rev[0:n, :].unsqueeze(1), [n, NT, w]), ALU.mult)
        P.v(lambda e: e.tensor_reduce(mx4, score, AX.X, ALU.max))
        P.tt(P.dve, out, score, b3(mx4, w), ALU.is_equal)

    def top(x, m):
        P.v(lambda e: e.tensor_reduce(m, x, AX.X, ALU.max))

    P.v(lambda e: e.memset(full, SKIP))
    tf = P.dma(P.sp, T["rowtab"].rearrange("(p b) a -> p (b a)", p=128), full, "rt", P.dve.now())
    P.tt(P.dve, lgc, lgc, bc(bias[0:n, :].unsqueeze(1), [n, NT, 36]), ALU.add)
    G = lgc[:, :, 0:4]
    top(G, gm)
    t = P.tt(P.dve, eg, G, b3(gm, 4), ALU.subtract)
    t = P.actf(eg, eg, ACT.Exp, t)
    P.v(lambda e: e.tensor_reduce(gs, eg, AX.X, ALU.add), t)
    P.v(lambda e: e.reciprocal(gp, gs))
    first_of(og, G, gm, sc, P.K["rev4"], 4)
    for g in range(4):
        E = lgc[:, :, 4 + 8 * g:12 + 8 * g]
        dst8 = es if g == 0 else ex
        P.tt(P.dve, dst8, E, bc(og[:, :, g:g + 1], [n, NT, 8]), ALU.mult)
        if g:
            P.tt(P.dve, es, es, ex, ALU.add)
    top(es, em)
    t = P.tt(P.dve, ex, es, b3(em, 8), ALU.subtract)
    t = P.actf(ex, ex, ACT.Exp, t)
    P.v(lambda e: e.tensor_reduce(es_, ex, AX.X, ALU.add), t)
    P.v(lambda e: e.reciprocal(es_, es_))
    first_of(o1, es, em, sc8, P.K["rev8"], 8)
    P.v(lambda e: e.scalar_tensor_tensor(es, o1, -1e30, es, ALU.mult, ALU.add))
    top(es, m2)
    first_of(o2, es, m2, sc8, P.K["rev8"], 8)
    t = P.tt(P.dve, p2, m2, em, ALU.subtract)
    t = P.actf(p2, p2, ACT.Exp, t)
    g1, g2 = P.gates[0:n, 0, :], P.gates[0:n, 1, :]
    P.tt(P.dve, g1, gp, es_, ALU.mult, t)
    P.tt(P.dve, g2, g1, p2, ALU.mult)
    for g in range(4):
        for o, O in ((o1, O1), (o2, O2)):
            P.tt(P.dve, O[:, :, 8 * g:8 * g + 8], o, bc(og[:, :, g:g + 1], [n, NT, 8]), ALU.mult)
    P.tt(P.dve, OO, O1, O2, ALU.add)
    P.v(lambda e: e.memset(run[:, 0, :], 0.0))
    for i in range(1, NT):
        P.tt(P.dve, run[:, i, :], run[:, i - 1, :], OO[:, i - 1, :], ALU.add)
    t = P.tt(P.dve, tot[0:n, :], run[:, NT - 1, :], OO[:, NT - 1, :], ALU.add)
    pr = P.ps[0][0:n, 0:320]
    t1 = P.mms([(pr, P.K["tri"][0:n, :], OO.rearrange("p i e -> p (i e)"), True, False),
                (pr, P.K["ones"][0:n, 0:n], run.rearrange("p i e -> p (i e)"), False, True)], t)
    t2 = P.mms([(P.ps[1][:, 0:32], P.K["ones"][0:n, :], tot[0:n, :], True, True)])
    P.copy(P.dve, cnt, P.ps[1][:, 0:32], t2)
    P.tt(P.dve, cm9, bc(cnt.unsqueeze(2), [128, 32, 9]), bc(P.K["m128"].unsqueeze(1), [128, 32, 9]), ALU.is_gt)
    P.v(lambda e: e.tensor_reduce(nb, cm9, AX.X, ALU.add))
    P.v(lambda e: e.tensor_tensor_scan(cum, P.K["ones"][:, 0:32], nb, 0.0, ALU.mult, ALU.add))
    P.tt(P.dve, start, cum, nb, ALU.subtract)
    P.v(lambda e: e.tensor_scalar(start, start, 128.0, None, ALU.mult))
    P.tt(P.dve, rk, pr.rearrange("p (i e) -> p i e", e=32), bc(start[0:n, :].unsqueeze(1), [n, NT, 32]), ALU.add, t1)
    for kx, O in enumerate((O1, O2)):
        P.tt(P.dve, O, O, rk, ALU.mult)
        P.v(lambda e, kx=kx, O=O: e.tensor_reduce(dst[:, kx, :], O, AX.X, ALU.add))
    P.copy(P.dve, di, dst)
    P.v(lambda e: e.tensor_scalar(dq, di, 7, None, ALU.arith_shift_right))
    P.v(lambda e: e.tensor_scalar(dr, di, 127, None, ALU.bitwise_and))
    P.v(lambda e: e.scalar_tensor_tensor(di, dr, float(NBLK), dq, ALU.mult, ALU.add))
    P.copy(P.dve, tv[0:n, :], P.K["tok2"][0:n, :])
    P.tt(P.dve, cmb, bc(cum.unsqueeze(1), [128, NBLK, 32]), bc(P.K["blkid"].unsqueeze(2), [128, NBLK, 32]), ALU.is_le)
    P.v(lambda e: e.tensor_reduce(eb, cmb, AX.X, ALU.add))
    P.v(lambda e: e.tensor_scalar(eb, eb, 128.0, P.K["pid"], ALU.mult, ALU.add))
    t = P.v(lambda e: e.tensor_scalar(P.widx, eb, float(4096 * li), None, ALU.add))
    for i in range(NT):
        for kx in range(2):
            ts = P.scatter(T["rowtab"], di[:, kx, i:i + 1], tv[0:n, 2 * i + kx:2 * i + kx + 1], NROWS - 1, "rs", t, tf)
    t = P.dma(P.sp, P.slots, T["rowtab"].rearrange("(p b) a -> p (b a)", p=128), "rt", ts)
    P.v(lambda e: e.tensor_scalar(P.toks, P.slots, 1, None, ALU.arith_shift_right), t)
    P.barrier()
    P.top = base


def moe(P, li):
    T = P.T
    base = P.top
    NB = 3
    w13 = [P.region2(2, 2048) for _ in range(NB)]
    w2 = [P.region(2048) for _ in range(NB)]
    xb = [P.region(D) for _ in range(NB)]
    xT = [P.region2(8, 128) for _ in range(2)]
    sg = [P.region(256) for _ in range(2)]
    aT = [P.region2(2, 128) for _ in range(2)]
    yo = [P.region(D) for _ in range(2)]
    for s in range(NB):
        for q, x in ((P.pool, w13[s]), (P.dve, w2[s]), (P.dve, xb[s])):
            P.step(q, lambda e, x=x: e.memset(x, 0.0), [])
    P.barrier()
    v1 = T["moe_w1"].rearrange("l e (p t) n -> (l e p) (t n)", p=128)
    v3 = T["moe_w3"].rearrange("l e (p t) n -> (l e p) (t n)", p=128)
    v2 = T["moe_w2"].rearrange("l e (p t) n -> (l e p) (t n)", p=128)
    wb = 4096 * (li + 1) - 1
    wfree, w2free, xfree = [[] for _ in range(NB)], [[] for _ in range(NB)], [[] for _ in range(NB)]
    got = {}

    def load(b):
        s = b % NB
        tx = P.gather(xb[s], T["h"], P.toks[:, b:b + 1], L - 1, f"gx{s}", *xfree[s])
        ix = P.widx[:, b:b + 1]
        P.gather(w13[s][:, 0, :], v1, ix, wb, f"gw{s}", *wfree[s])
        tw = P.gather(w13[s][:, 1, :], v3, ix, wb, f"gw{s}")
        t2 = P.gather(w2[s], v2, ix, wb, f"gv{s}", *w2free[s])
        got[b] = (tx, tw, t2)

    acts = {}
    xTfree, sgfree, aTfree, yofree = [[], []], [[], []], [[], []], [[], []]

    def up(b):
        s, o = b % NB, b % 2
        tx, tw, _ = got[b]
        xv = xb[s].rearrange("p (f t) -> p t f", t=8)
        te = []
        for half in range(2):
            pv = P.ps[half][:, 0:512].rearrange("p (j t) -> p j t", t=128)
            t = P.trs([(pv[:, j, :], xv[:, 4 * half + j, :]) for j in range(4)], tx, *P.psfree[half])
            q = P.act if half else P.dve
            te.append(P.copy(q, xT[o][:, 4 * half:4 * half + 4, :], pv, t, *xTfree[o]))
            P.psfree[half] = [te[-1]]
        xfree[s] = [t]
        bk = 2 + o
        out = P.ps[bk][:, :].rearrange("p (m n) -> p m n", m=2)
        t = P.mms([(out, xT[o][:, k, :], w13[s][:, :, 256 * k:256 * k + 256], k == 0, k == 7) for k in range(8)],
                  tw, *te, *P.psfree[bk])
        xTfree[o] = [t]
        wfree[s] = [t]
        t = P.actf(sg[o], P.ps[bk][:, 0:256], ACT.Silu, t, *sgfree[o])
        t = P.tt(P.dve, sg[o], sg[o], P.ps[bk][:, 256:512], ALU.mult, t)
        P.psfree[bk] = [t]
        acts[b] = t

    def down(b):
        s, o = b % NB, b % 2
        av = sg[o].rearrange("p (f t) -> p t f", t=2)
        pv = P.ps[4][:, 0:256].rearrange("p (j t) -> p j t", t=128)
        t = P.trs([(pv[:, j, :], av[:, j, :]) for j in range(2)], acts[b], *P.psfree[4])
        sgfree[o] = [t]
        ta = P.copy(P.act, aT[o], pv, t, *aTfree[o])
        P.psfree[4] = [ta]
        te = []
        for c in range(2):
            bk = 5 + c
            t = P.mms([(P.ps[bk][:, :], aT[o][:, k, :], w2[s][:, 1024 * k + 512 * c:1024 * k + 512 * c + 512],
                        k == 0, k == 1) for k in range(2)], ta, got[b][2], *P.psfree[bk])
            q = P.act if c else P.dve
            te.append(P.copy(q, yo[o][:, 512 * c:512 * c + 512], P.ps[bk][:, :], t, *yofree[o]))
            P.psfree[bk] = [te[-1]]
        w2free[s] = [t]
        aTfree[o] = [t]
        yofree[o] = [P.scatter(T["ys"], P.slots[:, b:b + 1], yo[o], 2 * L - 1, f"so{o}", *te)]

    for b in range(NB - 1):
        load(b)
    up(0)
    for b in range(NBLK):
        if b + NB - 1 < NBLK:
            load(b + NB - 1)
        if b + 1 < NBLK:
            up(b + 1)
        down(b)
    P.barrier()
    P.top = base
    gt, bt = P.region(D), P.region(D)
    yv = [P.region2(2, D) for _ in range(3)]
    hx = [P.region(D) for _ in range(3)]
    tmp = [P.region(16) for _ in range(3)]
    P.dma(P.sp, gt[0:C, :], rows(T["ln2_g"][li], C), "k")
    tk = P.dma(P.sp, bt[0:C, :], rows(T["ln2_b"][li], C), "k")
    free = [[], [], []]
    for i in range(NT):
        s = i % 3
        P.dma(P.act, yv[s][0:C], T["ys"][2 * C * i:2 * C * (i + 1), :].rearrange("(t k) n -> t k n", k=2),
              f"x{s}", *free[s])
        t = P.dma(P.act, hx[s][0:C, :], T["h"][C * i:C * i + C, :], f"x{s}")
        x = hx[s][0:C, :]
        P.v(lambda e, x=x: e.tensor_scalar(x, x, ALPHA1, None, ALU.mult), t)
        for kx in range(2):
            t = P.v(lambda e, x=x, s=s, kx=kx, i=i: e.scalar_tensor_tensor(
                x, yv[s][0:C, kx, :], P.gates[0:C, kx, i:i + 1], x, ALU.mult, ALU.add))
        t = layer_norm(P, hx[s], C, gt, bt, tmp[s], None, 1e-5, tk)
        free[s] = [P.dma(P.sp, T["h"][C * i:C * i + C, :], x, f"ho{s}", t)]
    P.barrier()
    P.top = base


def b2_projections(P, x0, qk, vt, cat):
    T = P.T
    base = P.top
    xT = P.region2(8, SEQ)
    xs = [P.region(D) for _ in range(3)]
    free = [[], [], []]
    for i in range(8):
        s = i % 3
        t = P.dma(P.sp, xs[s], T["h"][NMETA + 128 * i:NMETA + 128 * (i + 1), :], f"x{s}", *free[s])
        free[s] = feature_major(P, xs[s], 128, xT, 128 * i, (2 * (i % 4), 2 * (i % 4) + 1), t)
    P.barrier()
    P.top = base + 8 * SEQ
    low = P.top
    tab = P.region2(2, SEQ)
    tt_ = P.dma(P.sp, tab, T["tables"], "k")
    ws = [P.region2(8, 128) for _ in range(3)]
    rot = [P.region(512) for _ in range(2)]
    wfree = [[], [], []]
    rfree = [[], []]
    bank = 0
    for n in range(8):
        w = ws[n % 3]
        tw = P.dma(P.act, w, T["w_in_2"][0, :, 128 * n:128 * n + 128].rearrange("(t p) n -> p t n", p=128),
                   f"w{n % 3}", *wfree[n % 3])
        for c in range(2):
            cs = slice(512 * c, 512 * c + 512)
            b = bank % 3
            br = 3 + bank % 3
            bank += 1
            t = P.mms([(P.ps[b][:, :], w[:, k, :], xT[:, k, cs], k == 0, k == 7) for k in range(8)],
                      tw, *P.psfree[b])
            wfree[n % 3] = [t]
            dst = qk[:, n, cs]
            te = P.copy(P.act, dst, P.ps[b][:, :], t)
            P.psfree[b] = [te]
            t = P.mms([(P.ps[br][:, :], P.K["rot2"], dst, True, True)], te, *P.psfree[br])
            r = rot[c]
            tr = P.tt(P.dve, r, P.ps[br][:, :], tab[:, 1, cs], ALU.mult, t, tt_)
            P.psfree[br] = [tr]
            P.tt(P.dve, dst, dst, tab[:, 0, cs], ALU.mult)
            P.tt(P.dve, dst, dst, r, ALU.add)
    P.barrier()
    P.top = low
    wv = P.region2(8, 1536)
    wsp = P.region2(4, 128)
    wT = P.region2(4, 128)
    bs, lg, lb = P.region(4), P.region(512), P.region(512)
    z = [P.region(D) for _ in range(2)]
    sq = P.region(512)
    st = [P.region2(2, 4) for _ in range(2)]
    tw = P.dma(P.act, wv, T["w_in_2"][0, :, 1024:2560].rearrange("(t p) n -> p t n", p=128), "w0")
    ts = P.dma(P.sp, wsp, T["w_spatial_2"][0].rearrange("g t s -> t g s"), "k")
    P.dma(P.sp, bs, T["b_spatial_2_c"][0], "k")
    P.dma(P.sp, lg, rows(T["gmlp_ln_g_2"][0], 128), "k")
    tk = P.dma(P.sp, lb, rows(T["gmlp_ln_b_2"][0], 128), "k")
    pv = P.ps[7][:, :].rearrange("p (g s) -> p g s", g=4)
    t = P.trs([(pv[:, g, :], wsp[:, g, :]) for g in range(4)], tk)
    t = P.tt(P.dve, wT, pv, bc(P.K["causal"].unsqueeze(1), [128, 4, 128]), ALU.mult, t)
    P.psfree[7] = [t]
    zfree = [[], []]
    for i in range(8):
        o = i % 2
        zz = z[o]
        tk_ = []
        for c in range(3):
            b = 3 * o + c
            t = P.mms([(P.ps[b][:, :], xT[:, k, 128 * i:128 * i + 128], wv[:, k, 512 * c:512 * c + 512],
                        k == 0, k == 7) for k in range(8)], tw, *P.psfree[b])
            if c == 0:
                te = P.copy(P.act, vt[:, i, :], P.ps[b][:, :], t)
            else:
                te = P.actf(zz[:, 512 * (c - 1):512 * c], P.ps[b][:, :], ACT.Gelu, t, *zfree[o])
            P.psfree[b] = [te]
        vg = zz[:, 512:1024]
        v3 = vg.rearrange("p (g n) -> p g n", g=4)
        m, vr = st[o][:, 0, :], st[o][:, 1, :]
        P.v(lambda e, m=m, v3=v3: e.tensor_reduce(m, v3, AX.X, ALU.add), te)
        P.v(lambda e, m=m: e.tensor_scalar(m, m, 1.0 / 128, None, ALU.mult))
        t = P.tt(P.dve, v3, v3, bc(m.unsqueeze(2), [128, 4, 128]), ALU.subtract)
        t = P.actf(sq, vg, ACT.Square, t)
        t = P.v(lambda e, vr=vr: e.tensor_reduce(vr, sq.rearrange("p (g n) -> p g n", g=4), AX.X, ALU.add), t)
        t = P.actf(vr, vr, ACT.Sqrt, t, bias=P.K["eps"][:, 1:2], scale=1.0 / 128)
        P.v(lambda e, vr=vr: e.reciprocal(vr, vr), t)
        P.tt(P.dve, v3, v3, bc(vr.unsqueeze(2), [128, 4, 128]), ALU.mult)
        P.tt(P.dve, vg, vg, lg, ALU.mult, tk)
        t = P.tt(P.dve, vg, vg, lb, ALU.add)
        b = 6 + o
        pg = P.ps[b][:, :].rearrange("p (g s) -> p g s", g=4)
        t = P.mms([(pg[:, g, :], wT[:, g, :], v3[:, g, :], True, True) for g in range(4)], t, *P.psfree[b])
        ob = cat[:, i, 512:1024]
        ob3 = ob.rearrange("p (g n) -> p g n", g=4)
        t = P.tt(P.dve, ob3, pg, bc(bs.unsqueeze(2), [128, 4, 128]), ALU.add, t)
        P.psfree[b] = [t]
        t = P.tt(P.dve, ob, ob, zz[:, 0:512], ALU.mult)
        zfree[o] = [t]
    P.barrier()
    P.top = base


def b2_attention(P, qk, vt, cat):
    T = P.T
    base = P.top
    lq = P.region2(4, 64)
    lam = P.region(4)
    sub = P.region(128)
    pr = [[P.region(SEQ) for _ in range(2)] for _ in range(2)]
    pT = [P.region2(8, 128) for _ in range(2)]
    st = [P.region(16) for _ in range(4)]
    jk = P.region(128)
    for j, n in enumerate(["lambda_q1_2", "lambda_k1_2", "lambda_q2_2", "lambda_k2_2"]):
        P.dma(P.sp, lq[:, j, :], rows(T[n][0], 128), "k")
    tk = P.dma(P.sp, sub, rows(T["subln_g_2"][0], 128), "k")
    for j in range(2):
        P.tt(P.dve, lq[:, 2 * j, :], lq[:, 2 * j, :], lq[:, 2 * j + 1, :], ALU.mult, tk)
        t = P.v(lambda e, j=j: e.tensor_reduce(lam[:, j:j + 1], lq[:, 2 * j, :], AX.X, ALU.add))
    t = P.actf(lam[:, 0:2], lam[:, 0:2], ACT.Exp, t)
    P.tt(P.dve, lam[:, 2:3], lam[:, 1:2], lam[:, 0:1], ALU.subtract, t)
    init = 0.8 - 0.6 * math.exp(-0.3 * 0)
    P.v(lambda e: e.tensor_scalar(lam[:, 2:3], lam[:, 2:3], -init, None, ALU.add))
    P.v(lambda e: e.tensor_scalar(sub, sub, 1.0 - init, None, ALU.mult))
    scale = 64.0 ** -0.5
    items = [(i, h) for i in range(8) for h in range(4)]
    tsc = {}

    def scores(n):
        i, h = items[n]
        nk = 128 * (i + 1)
        toks = []
        for o in range(2):
            prt = slice(64 * o, 64 * o + 64)
            one = slice(64 * o, 64 * o + 1)
            mats = []
            free = []
            for c in range(0, nk, 512):
                b = 2 * o + c // 512
                w = min(512, nk - c)
                last = c + w == nk
                free += P.psfree[b]
                mats.append((P.ps[b][:, 0:w], qk[prt, h, 128 * i:128 * i + 128], qk[prt, 4 + h, c:c + w], True, not last))
                if last:
                    mats.append((P.ps[b][:, w - 128:w], P.K["negrow"][one, :], P.K["lastcol"][one, :], False, True))
            toks.append(P.mms(mats, *free))
        tsc[n] = toks

    scores(0)
    prfree, pTfree = [[], []], [[], []]
    for n, (i, h) in enumerate(items):
        z = st[n % 4]
        nk = 128 * (i + 1)
        p = pr[n % 2]
        for o in range(2):
            for c in range(0, nk, 512):
                b, w = 2 * o + c // 512, min(512, nk - c)
                k = o + 2 * (c // 512)
                P.v(lambda e, z=z, k=k, b=b, w=w: e.tensor_reduce(z[:, k:k + 1], P.ps[b][:, 0:w], AX.X, ALU.max),
                    tsc[n][o])
        if nk > 512:
            P.tt(P.dve, z[:, 0:2], z[:, 0:2], z[:, 2:4], ALU.max)
        t = P.v(lambda e, z=z: e.tensor_scalar(z[:, 0:2], z[:, 0:2], -scale, None, ALU.mult))
        for c in range(0, nk, 512):
            for o in range(2):
                b, w = 2 * o + c // 512, min(512, nk - c)
                te = P.actf(p[o][:, c:c + w], P.ps[b][:, 0:w], ACT.Exp, t, *prfree[n % 2], bias=z[:, o:o + 1],
                            scale=scale, accum=z[:, 4 + o + 2 * (c // 512):5 + o + 2 * (c // 512)])
                P.psfree[b] = [te]
        if n + 1 < len(items):
            scores(n + 1)
        if nk > 512:
            P.tt(P.dve, z[:, 4:6], z[:, 4:6], z[:, 6:8], ALU.add, te)
        P.v(lambda e, z=z: e.reciprocal(z[:, 4:6], z[:, 4:6]), te)
        P.tt(P.dve, z[:, 5:6], z[:, 5:6], lam[:, 2:3], ALU.mult)
        P.v(lambda e, z=z, p=p, nk=nk: e.tensor_scalar(p[1][:, 0:nk], p[1][:, 0:nk], z[:, 5:6], None, ALU.mult))
        ta = P.v(lambda e, z=z, p=p, nk=nk: e.scalar_tensor_tensor(p[0][:, 0:nk], p[0][:, 0:nk], z[:, 4:5],
                                                                   p[1][:, 0:nk], ALU.mult, ALU.add))
        tcs = []
        pt = pT[n % 2]
        for half in range(0, i + 1, 4):
            hi = min(half + 4, i + 1)
            b = 4 + half // 4
            pv = P.ps[b][:, 0:128 * (hi - half)].rearrange("p (j t) -> p j t", t=128)
            t = P.trs([(pv[:, j - half, :], p[0][:, 128 * j:128 * j + 128]) for j in range(half, hi)], ta,
                      *P.psfree[b])
            q = P.act if half else P.dve
            tcs.append(P.copy(q, pt[:, half:hi, :], pv, t, *pTfree[n % 2]))
            P.psfree[b] = [tcs[-1]]
        prfree[n % 2] = [t]
        b = 6 + n % 2
        out = P.ps[b][:, 0:128]
        t = P.mms([(out, pt[:, j, :], vt[:, j, 128 * h:128 * h + 128], j == 0, j == i) for j in range(i + 1)],
                  *tcs, *P.psfree[b])
        pTfree[n % 2] = [t]
        t = P.actf(jk, out, ACT.Square, t, accum=z[:, 8:9])
        t = P.actf(z[:, 9:10], z[:, 8:9], ACT.Sqrt, bias=P.K["eps"][:, 1:2], scale=1.0 / 128)
        P.v(lambda e, z=z: e.reciprocal(z[:, 9:10], z[:, 9:10]), t)
        t = P.v(lambda e, z=z, out=out, i=i, h=h: e.scalar_tensor_tensor(
            cat[:, i, 128 * h:128 * h + 128], out, z[:, 9:10], sub, ALU.mult, ALU.mult))
        P.psfree[b] = [t]
    P.barrier()
    P.top = base


def b2_out(P, cat, x1T):
    T = P.T
    base = P.top
    wo = P.region2(8, D)
    gt, bt = P.region(D), P.region(D)
    hx = [P.region(D) for _ in range(2)]
    x1 = [P.region(D) for _ in range(2)]
    cT = [P.region2(8, 128) for _ in range(2)]
    tmp = [P.region(16) for _ in range(2)]
    tw = P.dma(P.act, wo, T["w_out_2"][0].rearrange("(t p) n -> p t n", p=128), "w0")
    P.dma(P.sp, gt, rows(T["ln1_g_2"][0], 128), "k")
    tk = P.dma(P.sp, bt, rows(T["ln1_b_2"][0], 128), "k")
    hfree, xfree = [[], []], [[], []]
    for i in range(8):
        s = i % 2
        tb = P.dma(P.sp, hx[s], T["h"][NMETA + 128 * i:NMETA + 128 * (i + 1), :], f"x{s}", *hfree[s])
        tt = feature_major(P, cat[:, i, :], 128, cT[s], 0, (0, 1), tk)
        x = x1[s]
        for c in range(2):
            b = 2 + c + 2 * s
            t = P.mms([(P.ps[b][:, :], cT[s][:, k, :], wo[:, k, 512 * c:512 * c + 512], k == 0, k == 7)
                       for k in range(8)], tw, *tt, *P.psfree[b])
            t = P.v(lambda e, x=x, s=s, c=c, b=b: e.scalar_tensor_tensor(
                x[:, 512 * c:512 * c + 512], hx[s][:, 512 * c:512 * c + 512], ALPHA2, P.ps[b][:, :],
                ALU.mult, ALU.add), t, tb, *xfree[s])
            P.psfree[b] = [t]
        hfree[s] = [t]
        t = layer_norm(P, x, 128, gt, bt, tmp[s], None, 1e-5, tk, t)
        td = P.dma(P.sp, T["mix"][128 * i:128 * i + 128, :], x, f"ho{s}", t)
        xfree[s] = feature_major(P, x, 128, x1T, 128 * i, (6, 7), t) + [td]
    P.barrier()
    P.top = base


def b2_ffn(P, act, x1T):
    T = P.T
    base = P.top
    NW = 3
    wg = [P.region2(8, 128) for _ in range(NW)]
    wu = [P.region2(8, 128) for _ in range(NW)]
    gp = [P.region(SEQ + 2) for _ in range(2)]
    cv = [P.region(SEQ) for _ in range(2)]
    cw, cb = P.region2(3, NF), P.region(NF)
    P.dma(P.sp, cw, T["conv_w_2_c"][0].rearrange("j p f -> p j f"), "k")
    tk = P.dma(P.sp, cb, T["conv_b_2_c"][0], "k")
    for o in range(2):
        tz = P.v(lambda e, o=o: e.memset(gp[o][:, 0:2], 0.0))
    wfree = [[] for _ in range(NW)]
    gfree = [[], []]
    for f in range(NF):
        o, s = f % 2, f % NW
        P.dma(P.sp, wg[s], T["w_gate_2"][0, :, 128 * f:128 * f + 128].rearrange("(t p) n -> p t n", p=128),
              f"w{s}", *wfree[s])
        tw = P.dma(P.sp, wu[s], T["w_up_2"][0, :, 128 * f:128 * f + 128].rearrange("(t p) n -> p t n", p=128),
                   f"w{s}", *wfree[s])
        for c in range(2):
            b = c + 2 * o
            t = P.mms([(P.ps[b][:, :], wg[s][:, k, :], x1T[:, k, 512 * c:512 * c + 512], k == 0, k == 7)
                       for k in range(8)], tw, *P.psfree[b])
            te = P.copy(P.act, gp[o][:, 2 + 512 * c:514 + 512 * c], P.ps[b][:, :], t, tz, *gfree[o])
            P.psfree[b] = [te]
        ub = []
        for c in range(2):
            b = 4 + c + 2 * o
            ub.append(P.mms([(P.ps[b][:, :], wu[s][:, k, :], x1T[:, k, 512 * c:512 * c + 512], k == 0, k == 7)
                             for k in range(8)], *P.psfree[b]))
        wfree[s] = [ub[-1]]
        y, g = cv[o], gp[o]
        P.v(lambda e, y=y, g=g, f=f: e.tensor_scalar(y, g[:, 2:SEQ + 2], cw[:, 2, f:f + 1], cb[:, f:f + 1],
                                                     ALU.mult, ALU.add), te, tk)
        P.v(lambda e, y=y, g=g, f=f: e.scalar_tensor_tensor(y, g[:, 1:SEQ + 1], cw[:, 1, f:f + 1], y,
                                                            ALU.mult, ALU.add))
        t = P.v(lambda e, y=y, g=g, f=f: e.scalar_tensor_tensor(y, g[:, 0:SEQ], cw[:, 0, f:f + 1], y,
                                                                ALU.mult, ALU.add))
        gfree[o] = [t]
        t = P.actf(y, y, ACT.Silu, t)
        for c in range(2):
            b = 4 + c + 2 * o
            tm = P.tt(P.dve, act[:, f, 512 * c:512 * c + 512], y[:, 512 * c:512 * c + 512], P.ps[b][:, :], ALU.mult,
                      t, ub[c])
            P.psfree[b] = [tm]
    P.barrier()


def b2_down(P, act):
    T = P.T
    wd = [P.region2(NF, 256) for _ in range(2)]
    res = P.region2(8, D)
    gt, bt = P.region(D), P.region(D)
    tmp = [P.region(16) for _ in range(2)]
    tx = P.dma(P.act, res, T["mix"][0:SEQ, :].rearrange("(i p) n -> p i n", p=128), "x0")
    P.dma(P.act, gt, rows(T["ln2_g_2"][0], 128), "k")
    tk = P.dma(P.act, bt, rows(T["ln2_b_2"][0], 128), "k")
    wfree = [[], []]
    for q in range(4):
        s = q % 2
        tw = P.dma(P.sp, wd[s], T["w_down_2"][0, :, 256 * q:256 * q + 256].rearrange("(f p) n -> p f n", p=128),
                   f"w{s}", *wfree[s])
        for i in range(8):
            b = i
            t = P.mms([(P.ps[b][:, 0:256], act[:, f, 128 * i:128 * i + 128], wd[s][:, f, :], f == 0, f == NF - 1)
                       for f in range(NF)], tw, *P.psfree[b])
            r = res[:, i, 256 * q:256 * q + 256]
            te = P.v(lambda e, r=r, b=b: e.scalar_tensor_tensor(r, r, ALPHA2, P.ps[b][:, 0:256], ALU.mult, ALU.add),
                     t, tx)
            P.psfree[b] = [te]
            if q == 3:
                te = layer_norm(P, res[:, i, :], 128, gt, bt, tmp[i % 2], None, 1e-5, tk)
                P.dma(P.sp, T["out"][0, 128 * i:128 * i + 128, :], res[:, i, :], f"ho{i % 2}", te)
        wfree[s] = [t]
    P.barrier()


def second_block(P):
    base = P.top = CW
    cat = P.region2(8, D)
    qk = P.region2(8, SEQ)
    vt = P.region2(8, 512)
    b2_projections(P, None, qk, vt, cat)
    b2_attention(P, qk, vt, cat)
    P.top = base
    act = P.region2(NF, SEQ)
    x1T = P.region2(8, SEQ)
    b2_out(P, cat, x1T)
    b2_ffn(P, act, x1T)
    P.top = base + NF * SEQ
    b2_down(P, act)


def build(nc, T, upto="all"):
    with ExitStack() as ctx:
        P = Program(nc, ctx, T, upto)
        block = ctx.enter_context(nc.Block())
        load_consts(P)
        first_block(P)
        if upto == "all":
            second_block(P)
        P.barrier()
        P.sp.push(lambda e: e.nop(), [], P.sp.sem, 1)

        @block.sync
        def _(eng):
            P.sp.emit(eng)

        @block.scalar
        def _(eng):
            P.act.emit(eng)

        @block.vector
        def _(eng):
            P.dve.emit(eng)

        @block.gpsimd
        def _(eng):
            P.pool.emit(eng)

        @block.tensor
        def _(eng):
            P.pe.emit(eng)


def first_block(P):
    upto = P.upto
    positions(P)
    if upto == "pos":
        return
    mark = P.top
    for li in range(DEPTH):
        P.top = mark
        u = P.region2(15, L)
        cq, ckv, kpe = P.region2(2, L), P.region(L), P.region(L)
        m2 = P.top
        hT = P.region2(8, L)
        if li == 0:
            embed(P, hT)
        else:
            reload_transposed(P, hT)
        if upto == f"embed{li}":
            return
        project(P, li, hT, cq, ckv, kpe, u)
        P.top = m2
        if upto == f"proj{li}":
            return
        mla(P, li, cq, ckv, kpe)
        if upto == f"mla{li}":
            return
        P.top = mark + 15 * L
        rwkv(P, li, u)
        if upto == f"rwkv{li}":
            return
        P.top = mark
        mixer_out(P, li)
        if upto == f"out{li}":
            return
        moe(P, li)
        if upto == f"moe{li}":
            return


SCRATCH = [("h", (L, D)), ("mix", (L, D)), ("vfirst", (128, 4 * L)), ("ys", (2 * L, D)),
           ("rowtab", (NROWS, 1))]


def kernel(**inputs):
    import concourse.bacc as _bacc
    from concourse.bass_utils import run_bass_kernel_spmd as _run

    nc = _bacc.Bacc("TRN2", target_bir_lowering=False, num_devices=1)
    arrays, T = {}, {}
    for name, a in lay_out(inputs).items():
        arrays[f"in_{name}_dram"] = a
        T[name] = nc.dram_tensor(f"in_{name}_dram", a.shape, mybir.dt.from_np(a.dtype), kind="ExternalInput").ap()
    for name, shape in SCRATCH:
        T[name] = nc.dram_tensor(f"t_{name}", shape, I32 if name == "rowtab" else F32, kind="Internal").ap()
    T["out"] = nc.dram_tensor("out_0_dram", (1, SEQ, D), F32, kind="ExternalOutput").ap()
    build(nc, T)
    r = _run(nc, [arrays], core_ids=[0])
    return r.results[0]["out_0_dram"]
```

```python
import math
from contextlib import ExitStack

import numpy as np
import concourse.bass as bass
from concourse import mybir

ALU = mybir.AluOpType
ACT = mybir.ActivationFunctionType
AX = mybir.AxisListType
F32 = mybir.dt.float32
I32 = mybir.dt.int32
F32R = mybir.dt.float32r
SB = 53000

DEPTH, D, SEQ, NMETA = 2, 1024, 1024, 16
L = SEQ + NMETA
C, NT = 104, 10
GROUPS = [(0, 416), (416, 416), (832, 208)]
STAGGER = 11
KAPPA = math.exp(-0.5)
ALPHA1 = 4.0 ** 0.25
ALPHA2 = 2.0 ** 0.25
NBLK = 48
NROWS = NBLK * 128
EH = 256
SKIP = 1 << 20
DFF = 2816
NF = DFF // 128
EPS = {1e-6: 0, 1e-5: 1, 64e-5: 2, 1e-12: 3, 0.0: 4}

CONSTS = [
    ("ident", 128), ("ones", 128), ("blk", 128), ("rot", 64), ("rot2", 128), ("seg", 416),
    ("mf", 7 * C), ("mb", 7 * C), ("qf", 2 * C), ("qb", 2 * C), ("tri", C),
    ("eps", 5), ("freq", 1), ("rev4", 4), ("rev8", 8), ("m128", 9), ("blkid", NBLK), ("pid", 1),
    ("tok2", 2 * NT), ("negrow", 128), ("lastcol", 128), ("causal", 128), ("metapos", NMETA),
]
COFF = {}
_o = 0
for _n, _w in CONSTS:
    COFF[_n] = (_o, _w)
    _o += _w
CW = (_o + 7) // 8 * 8


def make_consts():
    a = np.zeros((128, CW), np.float32)

    def put(name, v, rows=128):
        o, w = COFF[name]
        a[:rows, o:o + w] = v

    p = np.arange(128)[:, None]
    f = np.arange(128)[None, :]
    put("ident", p == f)
    put("ones", 1.0)
    put("blk", p // 64 == f // 64)
    f64 = np.arange(64)[None, :]
    p64 = np.arange(64)[:, None]
    put("rot", np.where(p64 == f64 + 32, -1.0, 0.0) + np.where(p64 == f64 - 32, 1.0, 0.0), 64)
    same = p // 64 == f // 64
    put("rot2", np.where(same & (p == f + 32) & (f % 64 < 32), -1.0, 0.0)
        + np.where(same & (p == f - 32) & (f % 64 >= 32), 1.0, 0.0))
    seg = np.ones(416)
    seg[::C] = 0.0
    put("seg", seg[None, :])
    s = np.arange(C)[:, None]
    t = np.arange(C)[None, :]
    mf, mb = [], []
    for lv in range(7):
        h = 1 << lv
        same = (s // (2 * h)) == (t // (2 * h))
        mf.append(same & (t % (2 * h) >= h) & (s % (2 * h) < h))
        mb.append(same & (s % (2 * h) >= h) & (t % (2 * h) < h))
    put("mf", np.concatenate(mf, 1), C)
    put("mb", np.concatenate(mb, 1), C)
    put("qf", np.concatenate([s < t, s <= t], 1), C)
    put("qb", np.concatenate([s > t, s >= t], 1), C)
    put("tri", s < t, C)
    for k, i in EPS.items():
        a[:, COFF["eps"][0] + i] = k
    put("freq", (np.float32(10000.0) ** (-(np.arange(64) % 32 * 2).astype(np.float32) / np.float32(64)))[:, None], 64)
    put("rev4", (4 - np.arange(4))[None, :])
    put("rev8", (8 - np.arange(8))[None, :])
    put("m128", (128 * np.arange(9))[None, :])
    put("blkid", np.arange(NBLK)[None, :])
    put("pid", p)
    tk = (np.arange(NT)[None, :, None] * C + np.arange(C)[:, None, None]) * 2 + np.arange(2)[None, None, :]
    put("tok2", tk.reshape(C, 2 * NT), C)
    put("negrow", np.where(f < 64, -1e30, 0.0))
    put("lastcol", f >= 64)
    put("causal", p <= f)
    put("metapos", np.arange(NMETA)[None, :])
    return a


COLUMNS = ["rwkv_mu_prev", "rwkv_mu_next", "mla_q_norm", "mla_kv_norm", "rwkv_k_k", "rwkv_k_a", "rwkv_w0",
           "rwkv_a0", "rwkv_v0", "rwkv_r_k", "conv_w_2", "conv_b_2"]


def lay_out(inputs):
    out = {n: np.ascontiguousarray(a) for n, a in inputs.items()}
    for n in COLUMNS:
        a = out[n]
        if n == "rwkv_r_k":
            a = a.reshape(a.shape[0], -1)
        out[n + "_c"] = np.ascontiguousarray(np.swapaxes(a.reshape(a.shape[:-1] + (-1, 128)), -1, -2))
    out["b_spatial_2_c"] = np.ascontiguousarray(np.swapaxes(out["b_spatial_2"], -1, -2))
    out["consts"] = make_consts()
    out["tables"] = make_tables()
    return out


def make_tables():
    pos = np.arange(SEQ, dtype=np.float32)
    inv = (1.0 / (np.float32(10000.0) ** (np.arange(0, 64, 2, dtype=np.float32) / np.float32(64)))).astype(np.float32)
    ang = (pos[:, None] * inv[None, :]).astype(np.float32).astype(np.float64)
    row = np.arange(128) % 32
    return np.stack([np.cos(ang)[:, row].T, np.sin(ang)[:, row].T], 1).astype(np.float32)


class Sem:
    def __init__(self, handle):
        self.handle = handle
        self.count = 0


class Queue:

    def __init__(self, sem, serial):
        self.sem, self.serial = sem, serial
        self.items, self.seen, self.fence = [], {}, []

    def now(self):
        return (self.sem, self.sem.count)

    def push(self, issue, toks, sem, step):
        waits = []
        for s, v in list(toks) + self.fence:
            if v > self.seen.get(s, 0):
                self.seen[s] = v
                waits.append((s, v))
        self.fence = []
        sem.count += step
        self.items.append((waits, issue, sem, step))
        return (sem, sem.count)

    def emit(self, eng):
        for waits, issue, sem, step in self.items:
            for s, v in waits:
                eng.wait_ge(s.handle, v)
            last = issue(eng)
            if step:
                last.then_inc(sem.handle, step)


class Split:

    def __init__(self, hi, hf, lo, x):
        self.hi, self.hf, self.lo, self.x = hi, hf, lo, x

    def at(self, *ix):
        return Split(*(v[(slice(None),) + ix] for v in (self.hi, self.hf, self.lo, self.x)))


def three(out, a, b, first, last):
    return [(out, a.hi, b.hi, first, False), (out, a.hi, b.lo, False, False), (out, a.lo, b.hi, False, last)]


class Program:
    def __init__(self, nc, ctx, T, upto):
        self.nc, self.T, self.upto = nc, T, upto
        self.ctx = ctx
        self.nsem = 0

        def q(serial):
            return Queue(self.sem(), serial)

        self.pe, self.act, self.dve, self.pool, self.sp = q(False), q(True), q(True), q(True), q(False)
        self.engs = [self.pe, self.act, self.dve, self.pool, self.sp]
        self.base = (nc.sbuf_base + 31) // 32 * 32
        self.tensors = {}
        self.ps = [ctx.enter_context(nc.psum_tensor(f"ps{i}", [128, 512], F32)) for i in range(8)]
        self.psfree = [[] for _ in range(8)]
        self.top = 0
        self.streams = {}
        self.K = {}
        self.strand = {}

    def sem(self):
        self.nsem += 1
        return Sem(self.ctx.enter_context(self.nc.semaphore(f"s{self.nsem}")))

    def stream(self, name):
        if name not in self.streams:
            self.streams[name] = self.sem()
        return self.streams[name]

    def place(self, o, width, dt):
        if (o, width, dt) not in self.tensors:
            self.tensors[o, width, dt] = self.nc.alloc_sbuf_tensor_at(
                f"m{len(self.tensors)}", [128, width], dt, offset=self.base + 4 * o)
        return self.tensors[o, width, dt][:, :]

    def region(self, width):
        o = (self.top + 7) // 8 * 8
        self.top = o + width
        assert self.top <= SB, self.top
        return self.place(o, width, F32)

    def split(self, a, b):
        o = (self.top + 7) // 8 * 8
        self.top = o + 2 * a * b
        assert self.top <= SB, self.top

        def view(k, dt):
            return self.place(o + k * a * b, a * b, dt).rearrange("p (a b) -> p a b", b=b)

        return Split(view(1, F32R), view(1, F32R).bitcast(F32), view(0, F32R), view(0, F32))

    def region2(self, a, b):
        return self.region(a * b).rearrange("p (a b) -> p a b", b=b)

    def region3(self, a, b, c):
        return self.region(a * b * c).rearrange("p (a b c) -> p a b c", b=b, c=c)

    def barrier(self):
        toks = [e.now() for e in self.engs if e.sem.count] + [(s, s.count) for s in self.streams.values() if s.count]
        for e in self.engs:
            e.fence = list(toks)
        self.psfree = [[] for _ in range(8)]

    def mms(self, mats, *toks):
        def issue(eng):
            for out, a, b, st, sp in mats:
                last = eng.matmul(out, a, b, start=st, stop=sp)
            return last
        return self.pe.push(issue, toks, self.pe.sem, 1)

    def trs(self, pairs, *toks):
        def issue(eng):
            for out, a in pairs:
                n, p = a.shape[0], a.base_partition()
                last = eng.transpose(out, a, self.K["ident"][p:p + n, p:p + n])
            return last
        return self.pe.push(issue, toks, self.pe.sem, 1)

    def step(self, q, issue, toks, after=True):
        toks = list(toks)
        if after and q.serial and q in self.strand:
            toks.append(self.strand[q])
        t = q.push(issue, toks, q.sem, 1)
        self.strand[q] = t
        return t

    def weave(self, strands, width):
        strands = list(strands)
        live, nxt = {}, 0
        outer = self.strand
        while live or nxt < len(strands):
            for slot in range(width):
                if slot not in live and nxt < len(strands) and nxt % width == slot:
                    live[slot] = (strands[nxt], dict(outer))
                    nxt += 1
                if slot in live:
                    gen, self.strand = live[slot]
                    try:
                        next(gen)
                    except StopIteration:
                        outer.update(self.strand)
                        del live[slot]
        self.strand = outer

    def v(self, issue, *toks, after=True):
        return self.step(self.dve, issue, toks, after)

    def a(self, issue, *toks, after=True):
        return self.step(self.act, issue, toks, after)

    def g(self, issue, *toks, after=True):
        return self.step(self.pool, issue, toks, after)

    def tt(self, q, out, x, y, op, *toks):
        return self.step(q, lambda e: e.tensor_tensor(out, x, y, op), toks)

    def copy(self, q, out, x, *toks):
        if q is self.act:
            return self.step(q, lambda e: e.activation(out, x, ACT.Copy), toks)
        return self.step(q, lambda e: e.tensor_copy(out, x), toks)

    def part(self, qh, ql, s, x, *toks):
        t = self.copy(qh, s.hi, x, *toks)
        return self.tt(ql, s.lo, x, s.hf, ALU.subtract, t, *toks)

    def actf(self, out, x, f, *toks, bias=None, scale=1.0, accum=None):
        kw = {} if bias is None else {"bias": bias}
        return self.a(lambda e: e.activation(out, x, f, scale=scale, accum_out=accum, **kw), *toks)

    def dma(self, q, out, x, stream, *toks, **kw):
        s = self.stream(stream)
        return q.push(lambda e: e.dma_start(out, x, **kw), toks, s, 16)

    def gather(self, out, table, idx, bound, stream, *toks):
        s = self.stream(stream)
        return self.pool.push(lambda e: e.indirect_dma_start(
            out, None, table, bass.IndirectOffsetOnAxis(idx, 0), bounds_check=bound, oob_is_err=False), toks, s, 16)

    def scatter(self, table, idx, x, bound, stream, *toks):
        s = self.stream(stream)
        return self.pool.push(lambda e: e.indirect_dma_start(
            table, bass.IndirectOffsetOnAxis(idx, 0), x, None, bounds_check=bound, oob_is_err=False), toks, s, 16)


def rows(ap, n):
    return ap.unsqueeze(0).to_broadcast([n, ap.shape[0]])


def bc(ap, shape):
    return ap.to_broadcast(shape)


def layer_norm(P, x, n, gt, bt, tmp, st, eps, *toks):
    s12, mv, sd = tmp[0:n, 0:12], tmp[0:n, 12:14], tmp[0:n, 14:15]
    rs = tmp[0:n, 15:16]
    xx = x[0:n, :]
    P.v(lambda e: e.bn_stats(s12[:, 0:6], xx[:, 0:512]), *toks)
    P.v(lambda e: e.bn_stats(s12[:, 6:12], xx[:, 512:1024]))
    t = P.v(lambda e: e.bn_aggr(mv, s12))
    t = P.actf(sd, mv[:, 1:2], ACT.Sqrt, t, bias=P.K["eps"][0:n, EPS[eps]:EPS[eps] + 1])
    yield
    P.v(lambda e: e.reciprocal(rs, sd), t)
    t = P.v(lambda e: e.scalar_tensor_tensor(mv[:, 0:1], mv[:, 0:1], -1.0, rs, ALU.mult, ALU.mult))
    t = P.actf(xx, xx, ACT.Identity, t, bias=mv[:, 0:1], scale=rs)
    yield
    t = P.tt(P.dve, xx[:, 0:640], xx[:, 0:640], gt[0:n, 0:640], ALU.mult, t)
    t1 = P.tt(P.dve, xx[:, 0:640], xx[:, 0:640], bt[0:n, 0:640], ALU.add)
    P.tt(P.pool, xx[:, 640:1024], xx[:, 640:1024], gt[0:n, 640:1024], ALU.mult, t)
    t2 = P.tt(P.pool, xx[:, 640:1024], xx[:, 640:1024], bt[0:n, 640:1024], ALU.add)
    return [t1, t2]


def feature_major(P, x, n, hT, col, banks, tx):
    out = []
    for half in range(2):
        b = banks[half]
        psv = P.ps[b][:, 0:4 * n].rearrange("p (j t) -> p j t", t=n)
        t = P.trs([(psv[:, j, :], x[0:n, 128 * (4 * half + j):128 * (4 * half + j + 1)]) for j in range(4)],
                  *tx, *P.psfree[b])
        q = P.act if half else P.dve
        t = P.copy(q, hT[:, 4 * half:4 * half + 4, col:col + n], psv, t)
        P.psfree[b] = [t]
        out.append(t)
    return out


def feature_parts(P, x, n, s, col, banks, tx, skip=0):
    out = []
    for half in range(2):
        b = banks[half]
        psv = P.ps[b][:, 0:4 * n].rearrange("p (j t) -> p j t", t=n)
        t = P.trs([(psv[:, j, :], x[0:n, 128 * (4 * half + j):128 * (4 * half + j + 1)]) for j in range(4)],
                  *tx, *P.psfree[b])
        t = P.part(P.act, P.dve, s.at(slice(4 * half, 4 * half + 4), slice(col, col + n - skip)), psv[:, :, skip:n], t)
        P.psfree[b] = [t]
        out.append(t)
    return out


class Ring:

    def __init__(self, P, places, source, count, name, ql, *toks):
        self.P, self.places, self.source, self.count, self.name, self.ql = P, places, source, count, name, ql
        self.free = [list(toks) for _ in places]
        self.loaded, self.tok = {}, {}
        for n in range(len(places) - 1):
            self.load(n)
        self.halve(0)

    def at(self, n):
        return self.places[n % len(self.places)]

    def load(self, n):
        if n < self.count:
            s = n % len(self.places)
            self.loaded[n] = self.P.dma(self.P.sp, self.places[s].x, self.source(n), f"{self.name}{s}", *self.free[s])

    def ahead(self, n):
        self.load(n + len(self.places) - 1)

    def halve(self, n):
        if n < self.count:
            w = self.at(n)
            self.tok[n] = self.P.part(self.P.act, self.ql(n), w, w.x, self.loaded[n])

    def done(self, n, t):
        self.free[n % len(self.places)] = [t]


def load_consts(P):
    P.cr = P.region(CW)
    for n, (o, w) in COFF.items():
        P.K[n] = P.cr[:, o:o + w]
    t = P.dma(P.sp, P.cr, P.T["consts"], "k")
    P.kt = t
    P.barrier()


def positions(P):
    T = P.T
    mark = P.top
    P.cos, P.sin = P.region(L), P.region(L)
    pi = P.region(SEQ).bitcast(I32)
    six = P.region(SEQ).bitcast(I32)
    ang, k, r = P.region(L), P.region(L), P.region(L)
    n = 64
    t = P.dma(P.sp, pi[0:n, :], rows(T["positions"][0], n), "k")
    P.v(lambda e: e.memset(six[0:n, :], NMETA))
    P.tt(P.dve, pi[0:n, :], pi[0:n, :], six[0:n, :], ALU.add, t)
    P.copy(P.dve, ang[0:n, 0:NMETA], P.K["metapos"][0:n, :])
    P.copy(P.dve, ang[0:n, NMETA:L], pi[0:n, :])
    a, kk, rr = ang[0:n, :], k[0:n, :], r[0:n, :]
    P.v(lambda e: e.tensor_scalar(a, a, P.K["freq"][0:n, :], None, ALU.mult))
    magic = 1.5 * 2 ** 23
    P.v(lambda e: e.tensor_scalar(kk, a, float(np.float32(1 / (2 * math.pi))), magic, ALU.mult, ALU.add))
    P.v(lambda e: e.tensor_scalar(kk, kk, magic, None, ALU.subtract))
    two_pi = 2 * math.pi
    c1 = 6.28125
    c2 = float(np.float32(round((two_pi - c1) * 2 ** 19) / 2 ** 19))
    c3 = two_pi - c1 - c2
    P.v(lambda e: e.scalar_tensor_tensor(rr, kk, -c1, a, ALU.mult, ALU.add))
    P.v(lambda e: e.scalar_tensor_tensor(rr, kk, -c2, rr, ALU.mult, ALU.add))
    P.v(lambda e: e.scalar_tensor_tensor(rr, kk, -c3, rr, ALU.mult, ALU.add))
    t = P.v(lambda e: e.tensor_scalar(rr, rr, 3.1415925, -3.1415925, ALU.min, ALU.max))
    P.actf(P.sin[0:n, :], rr, ACT.Sin, t)
    t = P.actf(P.cos[0:n, :], rr, ACT.Sin, scale=0.5)
    co = P.cos[0:n, :]
    P.tt(P.dve, co, co, co, ALU.mult, t)
    t = P.v(lambda e: e.tensor_scalar(co, co, -2.0, 1.0, ALU.mult, ALU.add))
    P.dma(P.sp, T["cossin"][:, 0:L], co, "k", t)
    P.dma(P.sp, T["cossin"][:, L:2 * L], P.sin[0:n, :], "k", t)
    P.barrier()
    P.top = mark


def embed(P, hT):
    T = P.T
    base = P.top
    gt, bt = P.region(D), P.region(D)
    P.dma(P.sp, gt[0:C, :], rows(T["emb_ln_g"], C), "k")
    tg = P.dma(P.sp, bt[0:C, :], rows(T["emb_ln_b"], C), "k")
    xs = [P.region(D) for _ in range(3)]
    tmp = [P.region(16) for _ in range(3)]
    free = [[], [], []]

    def tile(i):
        s = i % 3
        x = xs[s]
        if i == 0:
            P.dma(P.sp, x[0:NMETA, :], T["meta_tokens"], f"x{s}", *free[s])
            t = P.dma(P.sp, x[NMETA:C, :], T["x"][0, 0:C - NMETA, :], f"x{s}", *free[s])
        else:
            t = P.dma(P.sp, x[0:C, :], T["x"][0, C * i - NMETA:C * (i + 1) - NMETA, :], f"x{s}", *free[s])
        yield
        ts = yield from layer_norm(P, x, C, gt, bt, tmp[s], None, 1e-5, t, tg)
        td = P.dma(P.sp, T["h"][C * i:C * (i + 1), :], x[0:C, :], f"ho{s}", *ts)
        yield
        free[s] = feature_parts(P, x, C, hT, C * i, (2 * s, 2 * s + 1), ts) + [td]
        yield

    P.weave([tile(i) for i in range(NT)], 3)
    P.barrier()
    P.top = base


def project(P, li, hT, cq, ckv, kpe, u):
    T = P.T
    base = P.top
    NW = 3
    ws = [P.split(8, 128) for _ in range(NW)]
    pt = [P.region(L + 2) for _ in range(2)]
    mu = P.region2(3, 15)
    tm = P.dma(P.sp, mu[:, 0, :], T["rwkv_mu_prev_c"][li], "k")
    tm = P.dma(P.sp, mu[:, 1, :], T["rwkv_mu_next_c"][li], "k")
    P.tt(P.dve, mu[:, 2, :], mu[:, 0, :], mu[:, 1, :], ALU.add, tm)
    tmu = P.v(lambda e: e.tensor_scalar(mu[:, 2, :], mu[:, 2, :], -1.0, 1.0, ALU.mult, ALU.add))
    for b in range(2):
        P.v(lambda e, b=b: e.memset(pt[b][:, 0:1], 0.0))
        tz = P.v(lambda e, b=b: e.memset(pt[b][:, L + 1:L + 2], 0.0))
    cols = [("q", 0, 0, 128), ("q", 1, 128, 128), ("kv", 0, 256, 128), ("pe", 0, 384, 64)]
    cols += [("u", j, 448 + 128 * j, 128) for j in range(15)]
    ring = Ring(P, ws, lambda n: T["w_in"][li, :, cols[n][2]:cols[n][2] + 128].rearrange("(t p) n -> p t n", p=128),
                len(cols), "w", lambda n: P.pool if n % 2 else P.dve)
    pfree = [[], []]
    bank = 0
    for n, (kind, j, c0, m) in enumerate(cols):
        w, tw = ring.at(n), ring.tok[n]
        ring.ahead(n)
        for gi, (t0, tn) in enumerate(GROUPS):
            b = bank % 6
            bank += 1
            out = P.ps[b][0:m, 0:tn]
            t = P.mms([x for k in range(8) for x in three(P.ps[b][:, 0:tn], w.at(k), hT.at(k, slice(t0, t0 + tn)),
                                                          k == 0, k == 7)], tw, *P.psfree[b])
            if gi == 0:
                ring.halve(n + 1)
            if kind == "u":
                dst = pt[j % 2][:, 1 + t0:1 + t0 + tn]
            else:
                dst = {"q": cq[:, j, :] if kind == "q" else None, "kv": ckv, "pe": kpe}[kind][0:m, t0:t0 + tn]
            te = P.copy(P.act, dst, out, t, *(pfree[j % 2] + [tz] if kind == "u" and gi == 0 else []))
            P.psfree[b] = [te]
            ring.done(n, t)
        if kind == "u":
            p = pt[j % 2]
            o = u[:, j, :]
            ta = P.a(lambda e, o=o, p=p, j=j: e.activation(o, p[:, 1:L + 1], ACT.Copy, scale=mu[:, 2, j:j + 1]), tmu)
            P.v(lambda e, o=o, p=p, j=j: e.scalar_tensor_tensor(
                o, p[:, 0:L], mu[:, 0, j:j + 1], o, ALU.mult, ALU.add), ta)
            tv = P.v(lambda e, o=o, p=p, j=j: e.scalar_tensor_tensor(
                o, p[:, 2:L + 2], mu[:, 1, j:j + 1], o, ALU.mult, ALU.add))
            pfree[j % 2] = [tv]
    P.barrier()
    P.top = base


def mla(P, li, cq, ckv, kpe):
    T = P.T
    base = P.top
    P.cos, P.sin = P.region(L), P.region(L)
    P.dma(P.sp, P.cos[0:64, :], T["cossin"][:, 0:L], "k")
    P.dma(P.sp, P.sin[0:64, :], T["cossin"][:, L:2 * L], "k")
    wuq = P.region2(2, 768)
    wkv = P.region(1024)
    gq, gkv = P.region(2), P.region(1)
    rk = P.region(L)
    raw = P.region(L)
    qn = P.region2(4, L)
    qp = P.region2(4, L)
    kn = P.region2(4, L)
    vt = P.region2(NT, 512)
    Pr = [P.region(L) for _ in range(2)]
    PT = [P.region2(NT, C) for _ in range(2)]
    st = [P.region(8) for _ in range(4)]
    ot = [rk[:, 0:512], rk[:, 512:1024]]
    sq = qn
    P.dma(P.sp, wuq, T["mla_w_uq"][li].rearrange("(t p) n -> p t n", p=128), "k")
    P.dma(P.sp, wkv, T["mla_w_ukv"][li], "k")
    P.dma(P.sp, gq, T["mla_q_norm_c"][li], "k")
    tk = P.dma(P.sp, gkv, T["mla_kv_norm_c"][li], "k")
    for j in range(2):
        t1 = P.actf(sq[:, j, :], cq[:, j, :], ACT.Square)
    t1 = P.actf(sq[:, 2, :], ckv, ACT.Square)
    for which in range(2):
        parts = [0, 1] if which == 0 else [2]
        tl = []
        for g, (t0, tn) in enumerate(GROUPS):
            out = P.ps[g][:, 0:tn]
            t = P.mms([(out, P.K["ones"], sq[:, j, t0:t0 + tn], j == parts[0], j == parts[-1]) for j in parts],
                      t1, *P.psfree[g])
            te = P.actf(rk[:, t0:t0 + tn], out, ACT.Sqrt, t, bias=P.K["eps"][:, 0:1],
                        scale=1.0 / (128 * len(parts)))
            P.psfree[g] = [te]
        P.v(lambda e: e.reciprocal(rk, rk), te)
        if which == 0:
            for j in range(2):
                tv = P.v(lambda e, j=j: e.scalar_tensor_tensor(cq[:, j, :], cq[:, j, :], gq[:, j:j + 1], rk,
                                                               ALU.mult, ALU.mult), tk)
            P.act.fence.append(tv)
        else:
            tn_ = P.v(lambda e: e.scalar_tensor_tensor(ckv, ckv, gkv[:, 0:1], rk, ALU.mult, ALU.mult), tk)
    bank = 0

    def fm(dst, m, terms, *toks):
        nonlocal bank
        for t0, tn in GROUPS:
            b = bank % 6
            bank += 1
            out = P.ps[b][0:m, 0:tn]
            t = P.mms([(out, w, x[:, t0:t0 + tn], i == 0, i == len(terms) - 1) for i, (w, x) in enumerate(terms)],
                      *toks, *P.psfree[b])
            te = P.copy(P.act, dst[0:m, t0:t0 + tn], out, t)
            P.psfree[b] = [te]
        return te

    def rope(dst, src, ts):
        nonlocal bank
        tm = None
        for t0, tn in GROUPS:
            b = bank % 6
            bank += 1
            out = P.ps[b][0:64, 0:tn]
            t = P.mms([(out, P.K["rot"][0:64, 0:64], src[0:64, t0:t0 + tn], True, True)], ts, *P.psfree[b])
            P.tt(P.dve, raw[0:64, t0:t0 + tn], out, P.sin[0:64, t0:t0 + tn], ALU.mult, t)
            P.tt(P.dve, dst[0:64, t0:t0 + tn], src[0:64, t0:t0 + tn], P.cos[0:64, t0:t0 + tn], ALU.mult)
            tm = P.tt(P.dve, dst[0:64, t0:t0 + tn], dst[0:64, t0:t0 + tn], raw[0:64, t0:t0 + tn], ALU.add)
            P.psfree[b] = [tm]
        return tm

    tr = rope(kpe, kpe, tn_)
    for h in range(4):
        tq = fm(qn[:, h, :], 128, [(wuq[:, j, 192 * h:192 * h + 128], cq[:, j, :]) for j in range(2)], tk, tn_)
        tp = fm(qp[:, h, :], 64, [(wuq[:, j, 192 * h + 128:192 * h + 192], cq[:, j, :]) for j in range(2)])
        tr = rope(qp[:, h, :], qp[:, h, :], tp)
        tq = fm(kn[:, h, :], 128, [(wkv[:, 256 * h:256 * h + 128], ckv)])
    for i in range(NT):
        b = bank % 6
        bank += 1
        wv = wkv.rearrange("p (h e) -> p h e", h=4)[:, :, 128:256]
        t = P.mms([(P.ps[b][0:C, 0:512].rearrange("p (h e) -> p h e", h=4), ckv[:, C * i:C * i + C], wv, True, True)],
                  *P.psfree[b])
        tv = P.copy(P.act, vt[0:C, i, :], P.ps[b][0:C, 0:512], t)
        P.psfree[b] = [tv]
    scale = 192.0 ** -0.5
    ofree, done = [[], []], {}
    toks = [tv, tr, tq]

    def item(n, i, h):
        s = n % 2
        bs = [4 * s + b for b in range(3)]
        ob = 4 * s + 3
        p, pt, z = Pr[s], PT[s], st[n % 4]
        mats = []
        for b, (t0, tn) in zip(bs, GROUPS):
            mats.append((P.ps[b][0:C, 0:tn], qn[:, h, C * i:C * i + C], kn[:, h, t0:t0 + tn], True, False))
            mats.append((P.ps[b][0:C, 0:tn], qp[0:64, h, C * i:C * i + C], kpe[0:64, t0:t0 + tn], False, True))
        t = P.mms(mats, *toks, *[x for b in bs for x in P.psfree[b]])
        yield
        for k, (b, (t0, tn)) in enumerate(zip(bs, GROUPS)):
            P.v(lambda e, b=b, k=k, tn=tn: e.tensor_reduce(z[0:C, k:k + 1], P.ps[b][0:C, 0:tn], AX.X, ALU.max), t)
        P.v(lambda e: e.tensor_reduce(z[0:C, 3:4], z[0:C, 0:3], AX.X, ALU.max))
        tm = P.v(lambda e: e.tensor_scalar(z[0:C, 3:4], z[0:C, 3:4], -scale, None, ALU.mult))
        yield
        te = []
        for k, (b, (t0, tn)) in enumerate(zip(bs, GROUPS)):
            te.append(P.actf(p[0:C, t0:t0 + tn], P.ps[b][0:C, 0:tn], ACT.Exp, tm,
                             bias=z[0:C, 3:4], scale=scale, accum=z[0:C, 4 + k:5 + k]))
            P.psfree[b] = [te[-1]]
        yield
        tcs = []
        for k, b in enumerate(bs):
            lo, hi = 4 * k, min(4 * k + 4, NT)
            pv = P.ps[b][0:C, 0:C * (hi - lo)].rearrange("p (j t) -> p j t", t=C)
            t = P.trs([(pv[:, j - lo, :], p[0:C, C * j:C * j + C]) for j in range(lo, hi)], te[k], *P.psfree[b])
            tcs.append(P.copy(P.dve if k < 2 else P.act, pt[0:C, lo:hi, :], pv, t))
            P.psfree[b] = [tcs[-1]]
        P.v(lambda e: e.tensor_reduce(z[0:C, 7:8], z[0:C, 4:7], AX.X, ALU.add), te[-1])
        P.v(lambda e: e.reciprocal(z[0:C, 7:8], z[0:C, 7:8]))
        yield
        out = P.ps[ob][0:C, 0:128]
        t = P.mms([(out, pt[0:C, j, :], vt[0:C, j, 128 * h:128 * h + 128], j == 0, j == NT - 1) for j in range(NT)],
                  *tcs, *P.psfree[ob])
        yield
        o = ot[i % 2][0:C, 128 * h:128 * h + 128]
        to = P.v(lambda e: e.tensor_scalar(o, out, z[0:C, 7:8], None, ALU.mult), t, *ofree[i % 2])
        P.psfree[ob] = [to]
        P.actf(raw[0:C, 128 * s:128 * s + 128], o, ACT.Square, to, accum=P.mss[0:C, i, h:h + 1])
        done.setdefault(i, []).append(to)
        if len(done[i]) == 4:
            ofree[i % 2] = [P.dma(P.sp, T["mix"][C * i:C * i + C, 0:512], ot[i % 2][0:C, :], f"ho{i % 2}", *done[i]),
                            P.act.now()]
        yield

    P.weave([item(4 * i + h, i, h) for i in range(NT) for h in range(4)], 2)
    P.barrier()
    P.top = base


def rwkv(P, li, u):
    T = P.T
    base = P.top
    r, k, v = u[:, 0:4, :], u[:, 4:8, :], u[:, 8:12, :]
    kk = P.region2(4, L)
    par = P.region2(9, 4)
    names = [("rwkv_k_k", None), ("rwkv_k_a", None), ("rwkv_w0", 0), ("rwkv_w0", 1), ("rwkv_a0", 0), ("rwkv_a0", 1)]
    for i, (n, d) in enumerate(names):
        src = T[n + "_c"][li] if d is None else T[n + "_c"][li, d]
        tp = P.dma(P.sp, par[:, i, :], src, "k")
    tp = P.dma(P.sp, par[:, 6, :], T["rwkv_r_k_c"][li], "k")
    w2, a2 = P.region(512), P.region(512)
    for d in range(2):
        P.dma(P.sp, w2[64 * d:64 * d + 64, :], T["rwkv_w2"][li, d], "k")
        tp = P.dma(P.sp, a2[64 * d:64 * d + 64, :], T["rwkv_a2"][li, d], "k")
    P.v(lambda e: e.tensor_scalar(par[:, 7, :], par[:, 1, :], -1.0, 1.0, ALU.mult, ALU.add), tp)
    rk8 = P.region2(4, 8)
    P.v(lambda e: e.memset(rk8, 0.0))
    for j in range(4):
        P.v(lambda e, j=j: e.tensor_scalar(rk8[:, j, 2 * j:2 * j + 2], P.K["blk"][:, 0:128:64], par[:, 6, j:j + 1],
                                           None, ALU.mult), tp)
    tmpb = P.top
    if li == 0:
        P.dma(P.sp, T["vfirst"].rearrange("p (j t) -> p j t", j=4), v, "vf")
    else:
        vf = P.region2(4, 416)
        v1, v2, v0, t32 = P.region2(4, 32), P.region(512), P.region(4), P.region(416)
        gate = P.region(416)
        P.dma(P.sp, v1, T["rwkv_v1"][li - 1].rearrange("(t p) n -> p t n", p=128), "k2")
        P.dma(P.sp, v2[0:32, :], T["rwkv_v2"][li - 1], "k2")
        tk = P.dma(P.sp, v0, T["rwkv_v0_c"][li - 1], "k2")
        vd = T["vfirst"].rearrange("p (j t) -> p j t", j=4)
        tv = None
        for t0, tn in GROUPS:
            tf = P.dma(P.sp, vf[:, :, 0:tn], vd[:, :, t0:t0 + tn], "vf", *([tv] if tv else []))
            t = P.mms([(P.ps[0][0:32, 0:tn], v1[:, j, :], v[:, j, t0:t0 + tn], j == 0, j == 3) for j in range(4)],
                      tk, *P.psfree[0])
            te = P.copy(P.act, t32[0:32, 0:tn], P.ps[0][0:32, 0:tn], t)
            P.psfree[0] = [te]
            for j in range(4):
                t = P.mms([(P.ps[1 + j][:, 0:tn], v2[0:32, 128 * j:128 * j + 128], t32[0:32, 0:tn], True, True)],
                          te, *P.psfree[1 + j])
                tg = P.actf(gate[:, 0:tn], P.ps[1 + j][:, 0:tn], ACT.Sigmoid, t, *([tv] if tv else []),
                            bias=v0[:, j:j + 1])
                P.psfree[1 + j] = [tg]
                P.tt(P.dve, vf[:, j, 0:tn], vf[:, j, 0:tn], v[:, j, t0:t0 + tn], ALU.subtract, tf, tg)
                P.tt(P.dve, vf[:, j, 0:tn], vf[:, j, 0:tn], gate[:, 0:tn], ALU.mult)
                tv = P.tt(P.dve, v[:, j, t0:t0 + tn], v[:, j, t0:t0 + tn], vf[:, j, 0:tn], ALU.add)
        P.barrier()
        P.top = tmpb
    sq = P.region(L)
    ls = None
    for j in range(4):
        tv = P.v(lambda e, j=j: e.tensor_scalar(kk[:, j, :], k[:, j, :], par[:, 0, j:j + 1], None, ALU.mult), tp)
        ts = P.actf(sq, kk[:, j, :], ACT.Square, tv, *([ls] if ls else []))
        for g, (t0, tn) in enumerate(GROUPS):
            out = P.ps[g][:, 0:tn]
            t = P.mms([(out, P.K["blk"], sq[:, t0:t0 + tn], True, True)], ts, *P.psfree[g])
            te = P.actf(sq[:, t0:t0 + tn], out, ACT.Sqrt, t, bias=P.K["eps"][:, 3:4])
            P.psfree[g] = [te]
        P.v(lambda e: e.reciprocal(sq, sq), te)
        ls = P.tt(P.dve, kk[:, j, :], kk[:, j, :], sq, ALU.mult)
    P.actf(u[:, 12, :], u[:, 12, :], ACT.Tanh)
    P.actf(u[:, 14, :], u[:, 14, :], ACT.Sigmoid)
    P.barrier()
    P.top = tmpb
    both = P.region(L)
    bon = [both[32 * d:32 * d + 8, :] for d in range(2)]
    saved = P.top
    ident = bc(P.K["ident"][0:C, 0:C].unsqueeze(1), [C, 4, C])
    heads = [(4 * o + j, slice(64 * o, 64 * o + 64), j, slice(128 * j + 64 * o, 128 * j + 64 * o + 64))
             for o in range(2) for j in range(4)]

    def direction(d):
        q_ = "qf" if d == 0 else "qb"
        qmask = bc(P.K[q_][0:C, :].unsqueeze(1), [C, 2, 2 * C])
        lmask = P.K["mf" if d == 0 else "mb"]
        lora = slice(64 * d, 64 * d + 64)
        S = P.region2(4, 128)
        blk4 = bc(P.K["blk"].unsqueeze(1), [128, 4, 128])
        tot, old, f = P.region(4), P.region(4), P.region(4)
        sig, cs, x1, aa = (P.region2(4, C) for _ in range(4))
        lm2 = P.region2(8, C)
        ea = lm2.rearrange("p h t -> p (h t)")[:, 0:4 * C].rearrange("p (j t) -> p j t", t=C)
        ei = lm2.rearrange("p h t -> p (h t)")[:, 4 * C:8 * C].rearrange("p (j t) -> p j t", t=C)
        kr, hb = P.region3(4, 2, C), P.region3(2, 4, C)
        tm, vt = P.region2(2, 512), P.region(512)
        ak, ab = P.region3(8, 2, C), P.region3(8, 2, C)
        T1, TT, XX = P.region2(8, C), P.region2(8, C), P.region2(8, C)
        LM = [P.region2(8, C), lm2]
        rh = P.region(512)
        uu = T1.rearrange("p h t -> p (h t)")[:, 0:512]
        ys = XX.rearrange("p h t -> p (h t)")[:, 0:512]
        dS = rh.rearrange("p (j c) -> p j c", c=128)
        used = [0]

        def bank():
            b = 4 * d + used[0] % 4
            used[0] += 1
            return b

        def squares(b):
            return P.ps[b][0:C, 0:416].rearrange("p (j t) -> p j t", t=C)

        P.v(lambda e: e.memset(S, 0.0))
        tdone, ty, tys = [], [], []
        for _ in range(STAGGER * d):
            yield
        for step in range(NT):
            i = step if d == 0 else NT - 1 - step
            sl = slice(C * i, C * i + C)
            b0, b1 = bank(), bank()
            psw = P.ps[b0][:, 0:416].rearrange("p (j t) -> p j t", t=C)
            psa = P.ps[b1][:, 0:416].rearrange("p (j t) -> p j t", t=C)
            t0 = P.mms([(psw[:, j, :], w2[lora, 128 * j:128 * j + 128], u[lora, 12, sl], True, True)
                        for j in range(4)], *P.psfree[b0])
            t1 = P.mms([(psa[:, j, :], a2[lora, 128 * j:128 * j + 128], u[lora, 13, sl], True, True)
                        for j in range(4)], *P.psfree[b1])
            bv = bank()
            t2 = P.trs([(P.ps[bv][0:C, 128 * j:128 * j + 128], v[:, j, sl]) for j in range(4)], *P.psfree[bv])
            yield
            t = P.tt(P.dve, sig, psw, bc(par[:, 2 + d, :].unsqueeze(2), [128, 4, C]), ALU.add, t0, *tdone)
            P.psfree[b0] = [t]
            t0 = P.actf(sig, sig, ACT.Tanh, t, scale=0.5)
            ta = P.tt(P.dve, aa, psa, bc(par[:, 4 + d, :].unsqueeze(2), [128, 4, C]), ALU.add, t1)
            P.psfree[b1] = [ta]
            ta = P.actf(aa, aa, ACT.Tanh, ta, scale=0.5)
            yield
            ts = P.v(lambda e: e.tensor_scalar(sig, sig, 0.5, 0.5, ALU.mult, ALU.add), t0)
            P.g(lambda e: e.tensor_scalar(aa, aa, 0.5, 0.5, ALU.mult, ALU.add), ta, *ty, *tdone)
            tvt = P.copy(P.act, vt[0:C, :], P.ps[bv][0:C, :], t2, *ty)
            P.psfree[bv] = [tvt]
            yield
            P.copy(P.dve, old, tot) if step else None
            P.v(lambda e: e.tensor_tensor_scan(cs.rearrange("p j t -> p (j t)"), P.K["seg"],
                                               sig.rearrange("p j t -> p (j t)"), 0.0, ALU.mult, ALU.add))
            yield
            P.copy(P.dve, tot, cs[:, :, C - 1])
            P.v(lambda e: e.scalar_tensor_tensor(cs, bc(tot.unsqueeze(2), [128, 4, C]), -0.5, cs, ALU.mult, ALU.add))
            P.tt(P.pool, hb[:, 1, :, :], aa, kk[:, :, sl], ALU.mult)
            yield
            tc = P.tt(P.dve, x1, *((cs, sig) if d == 0 else (sig, cs)), ALU.subtract)
            P.tt(P.pool, aa, aa, bc(par[:, 1, :].unsqueeze(2), [128, 4, C]), ALU.mult)
            yield
            te1 = P.actf(ei, cs if d == 0 else x1, ACT.Exp, tc, *tdone, scale=KAPPA)
            P.tt(P.pool, aa, aa, bc(par[:, 7, :].unsqueeze(2), [128, 4, C]), ALU.add)
            yield
            if d == 0:
                te2 = P.actf(x1, x1, ACT.Exp, scale=-KAPPA)
                eK = x1
            else:
                te2 = P.actf(sig, cs, ACT.Exp, scale=KAPPA)
                eK = sig
            tg = P.tt(P.pool, aa, aa, k[:, :, sl], ALU.mult)
            yield
            te3 = P.actf(ea, cs if d == 0 else x1, ACT.Exp, scale=-KAPPA)
            P.v(lambda e: e.scalar_tensor_tensor(hb[:, 1, :, :], hb[:, 1, :, :], -1.0, ei, ALU.mult, ALU.mult),
                te1, tg, *ty)
            yield
            P.tt(P.dve, kr[:, :, 0, :], kk[:, :, sl], eK, ALU.mult, te2)
            yield
            tk = P.tt(P.dve, kr[:, :, 1, :], r[:, :, sl], ea, ALU.mult, te3)
            yield
            th = P.tt(P.dve, hb[:, 0, :, :], aa, ei, ALU.mult)
            tz = P.tt(P.pool, aa, r[:, :, sl], aa, ALU.mult, th)
            yield
            tBs, tAs = [None] * 4, [None] * 4
            for m, dst in ((1, ab), (0, ak)):
                for part in range(4):
                    o, jj = part // 2, part % 2
                    pr = slice(64 * o, 64 * o + 64)
                    b = bank()
                    t = P.mms([(P.ps[b][0:C, 208 * x:208 * x + 208].rearrange("p (a t) -> p a t", a=2),
                                hb[pr, m, 2 * jj + x, :], kr[pr, 2 * jj + x, :, :], True, True) for x in range(2)],
                              th, tk, *P.psfree[b])
                    h0 = 4 * o + 2 * jj
                    t = P.tt(P.dve, dst[0:C, h0:h0 + 2, :, :].rearrange("p o a t -> p o (a t)"),
                             P.ps[b][0:C, 0:416].rearrange("p (o x) -> p o x", o=2), qmask, ALU.mult, t, *ty)
                    P.psfree[b] = [t]
                    (tBs if m else tAs)[part] = t
                    if part % 2:
                        yield
            for m in range(2):
                b = bank()
                t = P.trs([(P.ps[b][0:C, 128 * j:128 * j + 128], hb[:, m, j, :]) for j in range(4)], *P.psfree[b])
                ttm = P.copy(P.act, tm[0:C, m, :], P.ps[b][0:C, :], t, *ty)
                P.psfree[b] = [ttm]
            b = bank()
            pb = P.ps[b][32 * d:32 * d + 8, 0:C]
            t = P.mms([(pb, rk8[:, j, :], aa[:, j, :], j == 0, j == 3) for j in range(4)], tz, *P.psfree[b])
            P.psfree[b] = [P.copy(P.act, bon[d][:, sl], pb, t)]
            yield
            tT, xr = [[], []], [[[], []], [[], []]]
            for lv in range(7):
                lm = []
                L_ = LM[lv % 2]
                for g in range(2):
                    hs = slice(4 * g, 4 * g + 4)
                    lm.append(P.tt(P.pool, L_[0:C, hs, :], ab[0:C, hs, 0, :],
                                   bc(lmask[0:C, C * lv:C * lv + C].unsqueeze(1), [C, 4, C]), ALU.mult,
                                   tBs[2 * g], tBs[2 * g + 1], *xr[lv % 2][g], th, tk, tz))
                tx = []
                for g in range(2):
                    hs = slice(4 * g, 4 * g + 4)
                    b = bank()
                    if lv == 0:
                        t = P.trs([(squares(b)[:, j, :], L_[0:C, 4 * g + j, :]) for j in range(4)],
                                  lm[g], *P.psfree[b])
                        P.tt(P.dve, TT[0:C, hs, :], L_[0:C, hs, :], ident, ALU.add, lm[g], *tdone)
                        t = P.tt(P.dve, T1[0:C, hs, :], squares(b), ident, ALU.add, t)
                        tT[g] = [t]
                        P.psfree[b] = [t]
                        xr[0][g] = [t]
                    else:
                        t = P.mms([(squares(b)[:, j, :], L_[0:C, 4 * g + j, :], T1[0:C, 4 * g + j, :], True, True)
                                   for j in range(4)], lm[g], *tT[g], *P.psfree[b])
                        tx.append(P.copy(P.act, XX[0:C, hs, :], squares(b), t, *tys))
                        P.psfree[b] = [tx[g]]
                        xr[lv % 2][g] = [t]
                yield
                if lv == 0:
                    continue
                for g in range(2):
                    hs = slice(4 * g, 4 * g + 4)
                    if lv < 6:
                        b = bank()
                        t = P.mms([(squares(b)[:, j, :], TT[0:C, 4 * g + j, :], XX[0:C, 4 * g + j, :], True, True)
                                   for j in range(4)], tx[g], *tT[g], *P.psfree[b])
                        P.psfree[b] = [P.tt(P.dve, T1[0:C, hs, :], T1[0:C, hs, :], squares(b), ALU.add, t)]
                    b = bank()
                    t = P.mms([(squares(b)[:, j, :], XX[0:C, 4 * g + j, :], TT[0:C, 4 * g + j, :], True, True)
                               for j in range(4)], tx[g], *tT[g], *P.psfree[b])
                    t = P.tt(P.dve, TT[0:C, hs, :], TT[0:C, hs, :], squares(b), ALU.add, t)
                    tT[g] = [t]
                    P.psfree[b] = [t]
                yield
            if step:
                t = P.tt(P.dve, f, old, tot, ALU.add)
                tf = P.actf(f, f, ACT.Exp, t, scale=-0.5 * KAPPA)
                tS = P.tt(P.dve, S, S, bc(f.unsqueeze(2), [128, 4, 128]), ALU.mult, tf)
            else:
                tS = P.dve.now()

            def with_state(dst, row, terms):
                mats = []
                for j in range(4):
                    mats.append((dst[:, 128 * j:128 * j + 128], kr[:, j, row, :], S[:, j, :], True, False))
                    for o in range(2):
                        hc = slice(128 * j + 64 * o, 128 * j + 64 * o + 64)
                        for n, (x, y_) in enumerate(terms):
                            mats.append((dst[:, hc], x[0:C, 4 * o + j, row, :], y_[0:C, hc], False,
                                         o == 1 and n == len(terms) - 1))
                return mats

            b = bank()
            t = P.mms(with_state(P.ps[b][0:C, :], 0, [(ak, vt)]), tS, tvt, *tAs, *P.psfree[b])
            trh = P.copy(P.act, rh[0:C, :], P.ps[b][0:C, :], t)
            P.psfree[b] = [trh]
            yield
            b = bank()
            t = P.mms([(P.ps[b][0:C, hc], TT[0:C, g, :], rh[0:C, hc], True, True) for g, pr, j, hc in heads],
                      trh, *tT[0], *tT[1], *P.psfree[b])
            tu = P.copy(P.act, uu[0:C, :], P.ps[b][0:C, :], t)
            P.psfree[b] = [tu]
            yield
            b = bank()
            mats = []
            for j in range(4):
                jc = slice(128 * j, 128 * j + 128)
                mats.append((P.ps[b][:, jc], tm[0:C, 0, jc], vt[0:C, jc], True, False))
                mats.append((P.ps[b][:, jc], tm[0:C, 1, jc], uu[0:C, jc], False, True))
            t = P.mms(mats, ttm, tu, *P.psfree[b])
            ds = P.ps[b][:, :].rearrange("p (j c) -> p j c", c=128)
            b2 = bank()
            ty_ = P.mms(with_state(P.ps[b2][0:C, :], 1, [(ak, vt), (ab, uu)]), *P.psfree[b2])
            tdone = [ty_]
            ty = [ty_]
            td = P.tt(P.dve, dS, ds, blk4, ALU.mult, t)
            P.psfree[b] = [td]
            P.tt(P.dve, S, S, dS, ALU.add, ty_)
            t = P.copy(P.act, ys[0:C, :], P.ps[b2][0:C, :], ty_, *tys)
            P.psfree[b2] = [t]
            tys = [P.dma(P.sp, T[f"y{d}"][sl, :], ys[0:C, :], f"y{d}", t)]
            yield

    P.weave([direction(0), direction(1)], 2)
    P.barrier()
    P.top = saved
    g2, gng, gnb = P.region(512), P.region(512), P.region(512)
    P.dma(P.sp, g2, T["rwkv_g2"][li], "k")
    P.dma(P.sp, gng[0:C, :], rows(T["rwkv_gn_g"][li], C), "k")
    tk = P.dma(P.sp, gnb[0:C, :], rows(T["rwkv_gn_b"][li], C), "k")
    bt = P.region2(NT, 8)
    t = P.trs([(P.ps[6][0:C, 8 * i:8 * i + 8], bon[0][:, C * i:C * i + C]) for i in range(NT)])
    P.copy(P.dve, bt[0:C], P.ps[6][0:C, 0:8 * NT].rearrange("p (i h) -> p i h", h=8), t)
    t = P.trs([(P.ps[7][0:C, 8 * i:8 * i + 8], bon[1][:, C * i:C * i + C]) for i in range(NT)])
    tb = P.tt(P.dve, bt[0:C], bt[0:C], P.ps[7][0:C, 0:8 * NT].rearrange("p (i h) -> p i h", h=8), ALU.add, t)
    P.psfree[7] = P.psfree[6] = [tb]
    NS = 4
    yf = [P.region(512) for _ in range(NS)]
    yb_ = [P.region(512) for _ in range(NS)]
    sqs = [P.region(512) for _ in range(NS)]
    st = [P.region2(3, 8) for _ in range(NS)]
    yfree = [[] for _ in range(NS)]

    def tile(i):
        s = i % NS
        b = 2 * s
        yy, y2 = yf[s][0:C, :], yb_[s][0:C, :]
        P.dma(P.sp, yy, T["y0"][C * i:C * i + C, :], f"x{s}", *yfree[s])
        tl = P.dma(P.sp, y2, T["y1"][C * i:C * i + C, :], f"x{s}", *yfree[s])
        y3 = yy.rearrange("p (h n) -> p h n", h=8)
        q = sqs[s][0:C, :]
        q3 = q.rearrange("p (h n) -> p h n", h=8)
        m, vr = st[s][0:C, 0, :], st[s][0:C, 1, :]
        tvt = P.trs([(P.ps[b][0:C, 128 * j:128 * j + 128], v[:, j, C * i:C * i + C]) for j in range(4)], *P.psfree[b])
        tgt = P.mms([(P.ps[b + 1][0:C, :], u[:, 14, C * i:C * i + C], g2, True, True)], tk, *P.psfree[b + 1])
        yield
        P.tt(P.dve, yy, yy, y2, ALU.add, tl)
        P.v(lambda e: e.tensor_reduce(m, y3, AX.X, ALU.add))
        P.v(lambda e: e.tensor_scalar(m, m, 1.0 / 64, None, ALU.mult))
        t = P.tt(P.dve, y3, y3, bc(m.unsqueeze(2), [C, 8, 64]), ALU.subtract)
        t = P.actf(q, yy, ACT.Square, t)
        yield
        t = P.v(lambda e: e.tensor_reduce(vr, q3, AX.X, ALU.add), t)
        t = P.actf(vr, vr, ACT.Sqrt, t, bias=P.K["eps"][0:C, 2:3], scale=1.0 / 64)
        yield
        P.v(lambda e: e.reciprocal(vr, vr), t)
        t = P.tt(P.dve, y3, y3, bc(vr.unsqueeze(2), [C, 8, 64]), ALU.mult)
        t = P.tt(P.pool, yy, yy, gng[0:C, :], ALU.mult, tk, t)
        tp = P.tt(P.pool, yy, yy, gnb[0:C, :], ALU.add)
        t = P.tt(P.dve, q3, P.ps[b][0:C, :].rearrange("p (h n) -> p h n", h=8),
                 bc(bt[0:C, i, :].unsqueeze(2), [C, 8, 64]), ALU.mult, tvt, tb)
        P.psfree[b] = [t]
        yield
        P.tt(P.dve, yy, yy, q, ALU.add, tp)
        t = P.tt(P.dve, yy, yy, P.ps[b + 1][0:C, :], ALU.mult, tgt)
        P.psfree[b + 1] = [t]
        yfree[s] = [P.dma(P.sp, T["mix"][C * i:C * i + C, 512:1024], yy, f"ho{s}", t)]
        yield

    P.weave([tile(i) for i in range(NT)], NS)
    P.barrier()
    P.top = base


def mixer_out(P, li):
    T = P.T
    P.gates = P.region2(2, NT)
    P.slots = P.region(NBLK).bitcast(I32)
    P.toks = P.region(NBLK).bitcast(I32)
    P.widx = P.region(NBLK).bitcast(I32)
    base = P.top
    lg = P.region2(NT, 36)
    bias = P.region(36)
    wr = P.region2(8, 36)
    wo = P.split(8, D)
    gt, bt = P.region(D), P.region(D)
    on = P.region(512)
    NS = 4
    mx = [P.region(D) for _ in range(NS)]
    hx = [P.region(D) for _ in range(NS)]
    x1 = [P.region(D) for _ in range(NS)]
    mT = [P.split(8, C) for _ in range(NS)]
    hT = [P.region2(8, C) for _ in range(NS)]
    tmp = [P.region(16) for _ in range(NS)]
    mfree, hfree, xfree = ([[] for _ in range(NS)] for _ in range(3))
    tfree = [[] for _ in range(NS)]
    tw = []
    for k in range(8):
        t = P.dma(P.act, wo.x[:, k, :], T["w_out"][li, 128 * k:128 * k + 128, :], f"o{k}")
        tw.append(P.part(P.act, P.pool if k % 2 else P.dve, wo.at(k), wo.x[:, k, :], t))
    P.dma(P.sp, on[0:C, :], rows(T["mla_out_norm"][li], C), "k")
    P.dma(P.sp, gt[0:C, :], rows(T["ln1_g"][li], C), "k")
    P.dma(P.sp, bt[0:C, :], rows(T["ln1_b"][li], C), "k")
    P.dma(P.sp, wr[:, :, 0:4], T["moe_w_group"][li].rearrange("(t p) n -> p t n", p=128), "k")
    P.dma(P.sp, wr[:, :, 4:36], T["moe_w_expert"][li].rearrange("(t p) n -> p t n", p=128), "k")
    P.dma(P.sp, bias[0:C, 0:4], rows(T["moe_b_group"][li], C), "k")
    tk = P.dma(P.sp, bias[0:C, 4:36], rows(T["moe_b_expert"][li], C), "k")
    ms = P.mss[0:C]
    t = P.actf(ms, ms, ACT.Sqrt, bias=P.K["eps"][0:C, 0:1], scale=1.0 / 128)
    tms = P.v(lambda e: e.reciprocal(ms, ms), t)

    def tile(i):
        s = i % NS
        ta = P.dma(P.sp, mx[s][0:C, :], T["mix"][C * i:C * i + C, :], f"x{s}", *mfree[s])
        tb = P.dma(P.sp, hx[s][0:C, :], T["h"][C * i:C * i + C, :], f"x{3 + s}", *hfree[s])
        yield
        m3 = mx[s][0:C, 0:512].rearrange("p (h n) -> p h n", h=4)
        P.tt(P.dve, m3, m3, bc(ms[:, i, :].unsqueeze(2), [C, 4, 128]), ALU.mult, ta, tms, tk)
        tn = P.tt(P.dve, mx[s][0:C, 0:512], mx[s][0:C, 0:512], on[0:C, :], ALU.mult)
        yield
        tt = feature_parts(P, mx[s], C, mT[s], 0, (0, 1), [ta, tn] + tfree[s])
        mfree[s] = [P.pe.now()]
        yield
        x = x1[s]
        for c in range(2):
            b = 2 + c + 2 * (i % 2)
            t = P.mms([x_ for k in range(8) for x_ in three(P.ps[b][0:C, :], mT[s].at(k),
                                                            wo.at(k, slice(512 * c, 512 * c + 512)), k == 0, k == 7)],
                      *tw, *tt, *P.psfree[b])
            tfree[s] = [t]
            t = P.v(lambda e, c=c, b=b: e.scalar_tensor_tensor(
                x[0:C, 512 * c:512 * c + 512], hx[s][0:C, 512 * c:512 * c + 512], ALPHA1, P.ps[b][0:C, :],
                ALU.mult, ALU.add), t, tb, *xfree[s])
            P.psfree[b] = [t]
        hfree[s] = [t]
        yield
        ts = yield from layer_norm(P, x, C, gt, bt, tmp[s], None, 1e-5, tk, t)
        td = P.dma(P.pool, T["h"][C * i:C * i + C, :], x[0:C, :], f"hp{s}", *ts)
        yield
        tt = feature_major(P, x, C, hT[s], 0, (6, 7), ts)
        xfree[s] = tt + [td]
        yield
        t = P.mms([(P.ps[6][0:C, 0:36], hT[s][:, k, :], wr[:, k, :], k == 0, k == 7) for k in range(8)],
                  *tt, *P.psfree[6])
        t = P.copy(P.act, lg[0:C, i, :], P.ps[6][0:C, 0:36], t)
        P.psfree[6] = [t]
        yield

    P.weave([tile(i) for i in range(NT)], NS)
    P.barrier()
    P.top = base + NT * 36 + 36
    n = C

    def r3(w):
        return P.region2(NT, w)[0:n]

    lgc = lg[0:n]
    col = [P.region(NT)[0:n, :] for _ in range(8)]
    gm, gs, gp, em, es_, m2, p2, mx4 = col
    eg, og, sc = r3(4), r3(4), r3(4)
    es, ex, o1, o2, sc8 = r3(8), r3(8), r3(8), r3(8), r3(8)
    O1, O2, OO, run, rk = r3(32), r3(32), r3(32), r3(32), r3(32)
    tot, cnt, nb, cum, start = (P.region(32) for _ in range(5))
    cm9 = P.region2(32, 9)
    cmb = P.region2(NBLK, 32)
    eb = P.region(NBLK)
    dst = P.region2(2, NT)[0:n]
    di = P.region2(2, NT).bitcast(I32)[0:n]
    dq = P.region2(2, NT).bitcast(I32)[0:n]
    dr = P.region2(2, NT).bitcast(I32)[0:n]
    tv = P.region(2 * NT).bitcast(I32)
    full = P.region(NBLK).bitcast(I32)

    def b3(x, w):
        return bc(x.unsqueeze(2), [n, NT, w])

    def first_of(out, x, m, score, rev, w):
        P.tt(P.dve, score, x, b3(m, w), ALU.is_equal)
        P.tt(P.dve, score, score, bc(rev[0:n, :].unsqueeze(1), [n, NT, w]), ALU.mult)
        P.v(lambda e: e.tensor_reduce(mx4, score, AX.X, ALU.max))
        P.tt(P.dve, out, score, b3(mx4, w), ALU.is_equal)

    def top(x, m):
        P.v(lambda e: e.tensor_reduce(m, x, AX.X, ALU.max))

    P.v(lambda e: e.memset(full, SKIP))
    tf = P.dma(P.sp, T["rowtab"].rearrange("(p b) a -> p (b a)", p=128), full, "rt", P.dve.now())
    P.tt(P.dve, lgc, lgc, bc(bias[0:n, :].unsqueeze(1), [n, NT, 36]), ALU.add)
    G = lgc[:, :, 0:4]
    top(G, gm)
    t = P.tt(P.dve, eg, G, b3(gm, 4), ALU.subtract)
    t = P.actf(eg, eg, ACT.Exp, t)
    P.v(lambda e: e.tensor_reduce(gs, eg, AX.X, ALU.add), t)
    P.v(lambda e: e.reciprocal(gp, gs))
    first_of(og, G, gm, sc, P.K["rev4"], 4)
    for g in range(4):
        E = lgc[:, :, 4 + 8 * g:12 + 8 * g]
        dst8 = es if g == 0 else ex
        P.tt(P.dve, dst8, E, bc(og[:, :, g:g + 1], [n, NT, 8]), ALU.mult)
        if g:
            P.tt(P.dve, es, es, ex, ALU.add)
    top(es, em)
    t = P.tt(P.dve, ex, es, b3(em, 8), ALU.subtract)
    t = P.actf(ex, ex, ACT.Exp, t)
    P.v(lambda e: e.tensor_reduce(es_, ex, AX.X, ALU.add), t)
    P.v(lambda e: e.reciprocal(es_, es_))
    first_of(o1, es, em, sc8, P.K["rev8"], 8)
    P.v(lambda e: e.scalar_tensor_tensor(es, o1, -1e30, es, ALU.mult, ALU.add))
    top(es, m2)
    first_of(o2, es, m2, sc8, P.K["rev8"], 8)
    t = P.tt(P.dve, p2, m2, em, ALU.subtract)
    t = P.actf(p2, p2, ACT.Exp, t)
    g1, g2 = P.gates[0:n, 0, :], P.gates[0:n, 1, :]
    P.tt(P.dve, g1, gp, es_, ALU.mult, t)
    P.tt(P.dve, g2, g1, p2, ALU.mult)
    for g in range(4):
        for o, O in ((o1, O1), (o2, O2)):
            P.tt(P.dve, O[:, :, 8 * g:8 * g + 8], o, bc(og[:, :, g:g + 1], [n, NT, 8]), ALU.mult)
    P.tt(P.dve, OO, O1, O2, ALU.add)
    P.v(lambda e: e.memset(run[:, 0, :], 0.0))
    for i in range(1, NT):
        P.tt(P.dve, run[:, i, :], run[:, i - 1, :], OO[:, i - 1, :], ALU.add)
    t = P.tt(P.dve, tot[0:n, :], run[:, NT - 1, :], OO[:, NT - 1, :], ALU.add)
    pr = P.ps[0][0:n, 0:320]
    t1 = P.mms([(pr, P.K["tri"][0:n, :], OO.rearrange("p i e -> p (i e)"), True, False),
                (pr, P.K["ones"][0:n, 0:n], run.rearrange("p i e -> p (i e)"), False, True)], t)
    t2 = P.mms([(P.ps[1][:, 0:32], P.K["ones"][0:n, :], tot[0:n, :], True, True)])
    P.copy(P.dve, cnt, P.ps[1][:, 0:32], t2)
    P.tt(P.dve, cm9, bc(cnt.unsqueeze(2), [128, 32, 9]), bc(P.K["m128"].unsqueeze(1), [128, 32, 9]), ALU.is_gt)
    P.v(lambda e: e.tensor_reduce(nb, cm9, AX.X, ALU.add))
    P.v(lambda e: e.tensor_tensor_scan(cum, P.K["ones"][:, 0:32], nb, 0.0, ALU.mult, ALU.add))
    P.tt(P.dve, start, cum, nb, ALU.subtract)
    P.v(lambda e: e.tensor_scalar(start, start, 128.0, None, ALU.mult))
    P.tt(P.dve, rk, pr.rearrange("p (i e) -> p i e", e=32), bc(start[0:n, :].unsqueeze(1), [n, NT, 32]), ALU.add, t1)
    for kx, O in enumerate((O1, O2)):
        P.tt(P.dve, O, O, rk, ALU.mult)
        P.v(lambda e, kx=kx, O=O: e.tensor_reduce(dst[:, kx, :], O, AX.X, ALU.add))
    P.copy(P.dve, di, dst)
    P.v(lambda e: e.tensor_scalar(dq, di, 7, None, ALU.arith_shift_right))
    P.v(lambda e: e.tensor_scalar(dr, di, 127, None, ALU.bitwise_and))
    P.v(lambda e: e.scalar_tensor_tensor(di, dr, float(NBLK), dq, ALU.mult, ALU.add))
    P.copy(P.dve, tv[0:n, :], P.K["tok2"][0:n, :])
    P.tt(P.dve, cmb, bc(cum.unsqueeze(1), [128, NBLK, 32]), bc(P.K["blkid"].unsqueeze(2), [128, NBLK, 32]), ALU.is_le)
    P.v(lambda e: e.tensor_reduce(eb, cmb, AX.X, ALU.add))
    P.v(lambda e: e.tensor_scalar(eb, eb, 128.0, P.K["pid"], ALU.mult, ALU.add))
    t = P.v(lambda e: e.tensor_scalar(P.widx, eb, float(4096 * li), None, ALU.add))
    for i in range(NT):
        for kx in range(2):
            ts = P.scatter(T["rowtab"], di[:, kx, i:i + 1], tv[0:n, 2 * i + kx:2 * i + kx + 1], NROWS - 1, "rs", t, tf)
    t = P.dma(P.sp, P.slots, T["rowtab"].rearrange("(p b) a -> p (b a)", p=128), "rt", ts)
    P.v(lambda e: e.tensor_scalar(P.toks, P.slots, 1, None, ALU.arith_shift_right), t)
    P.barrier()
    P.top = base


def moe(P, li, dst, off):
    T = P.T
    base = P.top
    NB = 3
    w13 = [P.split(2, 2048) for _ in range(NB)]
    w2 = [P.split(1, 2048) for _ in range(NB)]
    xb = [P.region(D) for _ in range(NB)]
    xT = [P.split(8, 128) for _ in range(2)]
    sg = [P.region(256) for _ in range(2)]
    aT = [P.split(2, 128) for _ in range(2)]
    yo = [P.region(D) for _ in range(2)]
    for s in range(NB):
        for q, x in ((P.pool, w13[s].x), (P.dve, w2[s].x), (P.dve, xb[s])):
            P.step(q, lambda e, x=x: e.memset(x, 0.0), [])
    P.barrier()
    v1 = T["moe_w1"].rearrange("l e (p t) n -> (l e p) (t n)", p=128)
    v3 = T["moe_w3"].rearrange("l e (p t) n -> (l e p) (t n)", p=128)
    v2 = T["moe_w2"].rearrange("l e (p t) n -> (l e p) (t n)", p=128)
    wb = 4096 * (li + 1) - 1
    wfree, w2free, xfree = [[] for _ in range(NB)], [[] for _ in range(NB)], [[] for _ in range(NB)]
    got = {}

    def load(b):
        s = b % NB
        tx = P.gather(xb[s], T["h"], P.toks[:, b:b + 1], L - 1, f"gx{s}", *xfree[s])
        ix = P.widx[:, b:b + 1]
        t1 = P.gather(w13[s].x[:, 0, :], v1, ix, wb, f"gw{s}", *wfree[s])
        t3 = P.gather(w13[s].x[:, 1, :], v3, ix, wb, f"gu{s}", *wfree[s])
        got[b] = [tx, t1, t3]

    def load2(b):
        s = b % NB
        got[b].append(P.gather(w2[s].x[:, 0, :], v2, P.widx[:, b:b + 1], wb, f"gv{s}", *w2free[s]))

    acts = {}
    xTfree, sgfree, aTfree, yofree = [[], []], [[], []], [[], []], [[], []]

    def halves(b):
        s = b % NB
        _, t1, t3 = got[b][0:3]
        a1 = P.part(P.act, P.dve, w13[s].at(0), w13[s].x[:, 0, :], t1)
        a3 = P.part(P.act, P.dve, w13[s].at(1), w13[s].x[:, 1, :], t3)
        ready[b] = [a1, a3]

    def halves2(b):
        s = b % NB
        t2 = got[b][3]
        t = P.copy(P.act, w2[s].hi, w2[s].x, t2)
        w = w2[s]
        a2 = [P.tt(q, w.lo[:, 0, c], w.x[:, 0, c], w.hf[:, 0, c], ALU.subtract, t, t2)
              for q, c in ((P.pool, slice(0, 1024)), (P.dve, slice(1024, 2048)))]
        ready[b].append(a2)

    ready = {}

    def up(b):
        s, o = b % NB, b % 2
        tx = got[b][0]
        xv = xb[s].rearrange("p (f t) -> p t f", t=8)
        te = []
        for half in range(2):
            pv = P.ps[half][:, 0:512].rearrange("p (j t) -> p j t", t=128)
            t = P.trs([(pv[:, j, :], xv[:, 4 * half + j, :]) for j in range(4)], tx, *P.psfree[half])
            te.append(P.part(P.act, P.dve, xT[o].at(slice(4 * half, 4 * half + 4)), pv, t, *xTfree[o]))
            P.psfree[half] = [te[-1]]
        xfree[s] = [t]

    def up2(b, te=None):
        s, o = b % NB, b % 2
        bk = 2 + o
        out = P.ps[bk][:, :].rearrange("p (m n) -> p m n", m=2)
        t = P.mms([x for k in range(8) for x in three(out, xT[o].at(k), w13[s].at(slice(0, 2), slice(256 * k, 256 * k + 256)),
                                                      k == 0, k == 7)],
                  ready[b][0], ready[b][1], xparts[b], *P.psfree[bk])
        xTfree[o] = [t]
        wfree[s] = [t]
        t = P.actf(sg[o], P.ps[bk][:, 0:256], ACT.Silu, t, *sgfree[o])
        t = P.tt(P.dve, sg[o], sg[o], P.ps[bk][:, 256:512], ALU.mult, t)
        P.psfree[bk] = [t]
        acts[b] = t

    xparts = {}

    def down(b):
        s, o = b % NB, b % 2
        av = sg[o].rearrange("p (f t) -> p t f", t=2)
        pv = P.ps[4][:, 0:256].rearrange("p (j t) -> p j t", t=128)
        t = P.trs([(pv[:, j, :], av[:, j, :]) for j in range(2)], acts[b], *P.psfree[4])
        sgfree[o] = [t]
        ta = P.part(P.act, P.dve, aT[o], pv, t, *aTfree[o])
        P.psfree[4] = [ta]
        return ta

    def down2(b, ta):
        s, o = b % NB, b % 2
        te = []
        for c in range(2):
            bk = 5 + c
            t = P.mms([x for k in range(2) for x in three(P.ps[bk][:, :], aT[o].at(k),
                                                          w2[s].at(0, slice(1024 * k + 512 * c, 1024 * k + 512 * c + 512)),
                                                          k == 0, k == 1)], ta, *ready[b][2], *P.psfree[bk])
            te.append(P.copy(P.act, yo[o][:, 512 * c:512 * c + 512], P.ps[bk][:, :], t, *yofree[o]))
            P.psfree[bk] = [te[-1]]
        w2free[s] = [t]
        aTfree[o] = [t]
        yofree[o] = [P.scatter(T["ys"], P.slots[:, b:b + 1], yo[o], 2 * L - 1, f"so{o}", *te)]

    for b in range(NB - 1):
        load(b)
        load2(b)
    up(0)
    xparts[0] = P.dve.now()
    halves(0)
    parts = {}
    for b in range(NBLK + 2):
        if b + NB - 1 < NBLK:
            load(b + NB - 1)
        if b + 1 < NBLK:
            up(b + 1)
            xparts[b + 1] = P.dve.now()
            halves(b + 1)
        if b < NBLK:
            up2(b)
        if b >= 2:
            down2(b - 2, parts[b - 2])
        if 1 <= b <= NBLK:
            parts[b - 1] = down(b - 1)
        if b and b + 1 < NBLK:
            load2(b + 1)
        if b < NBLK:
            halves2(b)
    P.barrier()
    P.top = base
    gt, bt = P.region(D), P.region(D)
    NC = 4
    yv = [P.region2(2, D) for _ in range(NC)]
    hx = [P.region(D) for _ in range(NC)]
    tmp = [P.region(16) for _ in range(NC)]
    P.dma(P.sp, gt[0:C, :], rows(T["ln2_g"][li], C), "k")
    tk = P.dma(P.sp, bt[0:C, :], rows(T["ln2_b"][li], C), "k")
    free = [[] for _ in range(NC)]

    def tile(i):
        s = i % NC
        P.dma(P.sp, yv[s][0:C], T["ys"][2 * C * i:2 * C * (i + 1), :].rearrange("(t k) n -> t k n", k=2),
              f"x{s}", *free[s])
        t = P.dma(P.sp, hx[s][0:C, :], T["h"][C * i:C * i + C, :], f"x{s}", *free[s])
        x = hx[s][0:C, :]
        yield
        t = P.actf(x, x, ACT.Copy, t, scale=ALPHA1)
        for kx in range(2):
            t = P.v(lambda e, kx=kx: e.scalar_tensor_tensor(
                x, yv[s][0:C, kx, :], P.gates[0:C, kx, i:i + 1], x, ALU.mult, ALU.add), t)
        yield
        ts = yield from layer_norm(P, hx[s], C, gt, bt, tmp[s], None, 1e-5, tk)
        td = P.dma(P.pool, T["h"][C * i:C * i + C, :], x, f"hp{s}", *ts)
        skip = off if i == 0 else 0
        free[s] = [td] + feature_parts(P, hx[s], C, dst, C * i - off + skip, (2 * (i % 4), 2 * (i % 4) + 1), ts, skip)
        yield

    P.weave([tile(i) for i in range(NT)], NC)
    P.barrier()
    P.top = base


def b2_projections(P, x0, qk, vt, cat):
    T = P.T
    base = P.top
    xT = P.split(8, SEQ)
    low = P.top
    P.top = P.qk_at
    wv = [P.split(8, 512)]
    assert P.top <= base
    P.top = low
    wv.append(P.split(8, 512))
    wsp = P.region2(4, 128)
    wT = P.region2(4, 128)
    bs, lg, lb = P.region(4), P.region(512), P.region(512)
    z = [P.region(512) for _ in range(2)]
    sq = P.region(512)
    st = [P.region2(2, 4) for _ in range(2)]
    tw = []
    order = [0, 2, 1]

    def weights(n):
        w = wv[n % 2]
        c0 = 1024 + 512 * order[n]
        ts = []
        for k in range(8):
            t = P.dma(P.sp, w.x[:, k, :], T["w_in_2"][0, 128 * k:128 * k + 128, c0:c0 + 512], f"o{8 * (n % 2) + k}",
                      *(tw[n - 2][1] if n >= 2 else []))
            ts.append(P.part(P.act, P.pool if k % 2 else P.dve, w.at(k), w.x[:, k, :], t))
        tw.append((ts, []))

    weights(0)
    weights(1)
    P.dma(P.sp, wsp, T["w_spatial_2"][0].rearrange("g t s -> t g s"), "k")
    P.dma(P.sp, bs, T["b_spatial_2_c"][0], "k")
    P.dma(P.sp, lg, rows(T["gmlp_ln_g_2"][0], 128), "k")
    tk = P.dma(P.sp, lb, rows(T["gmlp_ln_b_2"][0], 128), "k")
    pv = P.ps[7][:, :].rearrange("p (g s) -> p g s", g=4)
    t = P.trs([(pv[:, g, :], wsp[:, g, :]) for g in range(4)], tk)
    twT = P.tt(P.dve, wT, pv, bc(P.K["causal"].unsqueeze(1), [128, 4, 128]), ALU.mult, t)
    P.psfree[7] = [twT]
    zfree = [[], []]

    def product(n, i):
        b = 3 * (i % 2) + n
        t = P.mms([x for k in range(8) for x in three(P.ps[b][:, :], xT.at(k, slice(128 * i, 128 * i + 128)),
                                                      wv[n % 2].at(k), k == 0, k == 7)], *tw[n][0], *P.psfree[b])
        if i == 7:
            tw[n][1].append(t)
        return b, t

    for i in range(8):
        b, t = product(0, i)
        P.psfree[b] = [P.copy(P.act, vt[:, i, :], P.ps[b][:, :], t)]
    weights(2)

    def gate(i):
        o = i % 2
        vg = z[o]
        b, t = product(1, i)
        te = P.actf(vg, P.ps[b][:, :], ACT.Gelu, t, *zfree[o])
        P.psfree[b] = [te]
        yield
        v3 = vg.rearrange("p (g n) -> p g n", g=4)
        m, vr = st[o][:, 0, :], st[o][:, 1, :]
        P.v(lambda e: e.tensor_reduce(m, v3, AX.X, ALU.add), te)
        P.v(lambda e: e.tensor_scalar(m, m, 1.0 / 128, None, ALU.mult))
        t = P.tt(P.dve, v3, v3, bc(m.unsqueeze(2), [128, 4, 128]), ALU.subtract)
        t = P.actf(sq, vg, ACT.Square, t, *sqfree)
        t = P.v(lambda e: e.tensor_reduce(vr, sq.rearrange("p (g n) -> p g n", g=4), AX.X, ALU.add), t)
        sqfree[:] = [t]
        t = P.actf(vr, vr, ACT.Sqrt, t, bias=P.K["eps"][:, 1:2], scale=1.0 / 128)
        yield
        P.v(lambda e: e.reciprocal(vr, vr), t)
        P.tt(P.dve, v3, v3, bc(vr.unsqueeze(2), [128, 4, 128]), ALU.mult)
        P.tt(P.dve, vg, vg, lg, ALU.mult, tk)
        t = P.tt(P.dve, vg, vg, lb, ALU.add)
        b = 6 + o
        pg = P.ps[b][:, :].rearrange("p (g s) -> p g s", g=4)
        t = P.mms([(pg[:, g, :], wT[:, g, :], v3[:, g, :], True, True) for g in range(4)], t, twT, *P.psfree[b])
        zfree[o] = [t]
        t = P.tt(P.dve, cat[:, i, 512:1024].rearrange("p (g n) -> p g n", g=4), pg,
                 bc(bs.unsqueeze(2), [128, 4, 128]), ALU.add, t)
        P.psfree[b] = [t]
        yield

    sqfree = []
    P.weave([gate(i) for i in range(8)], 2)
    for i in range(8):
        b, t = product(2, i)
        o = i % 2
        te = P.actf(z[o], P.ps[b][:, :], ACT.Gelu, t, *zfree[o])
        P.psfree[b] = [te]
        zfree[o] = [P.tt(P.dve, cat[:, i, 512:1024], cat[:, i, 512:1024], z[o], ALU.mult, te)]
    P.barrier()
    P.top = low
    tab = P.region2(2, SEQ)
    tt_ = P.dma(P.sp, tab, T["tables"], "k")
    ws = [P.split(8, 128) for _ in range(3)]
    rot = [P.region(512) for _ in range(2)]
    ring = Ring(P, ws, lambda n: T["w_in_2"][0, :, 128 * n:128 * n + 128].rearrange("(t p) n -> p t n", p=128),
                8, "w", lambda n: P.pool)
    bank = 0
    for n in range(8):
        w, tw = ring.at(n), ring.tok[n]
        ring.ahead(n)
        for c in range(2):
            cs = slice(512 * c, 512 * c + 512)
            b = bank % 3
            br = 3 + bank % 3
            bank += 1
            t = P.mms([x for k in range(8) for x in three(P.ps[b][:, :], w.at(k), xT.at(k, cs), k == 0, k == 7)],
                      tw, *P.psfree[b])
            ring.done(n, t)
            if c == 0:
                ring.halve(n + 1)
            dst = qk[:, n, cs]
            te = P.copy(P.act, dst, P.ps[b][:, :], t)
            P.psfree[b] = [te]
            t = P.mms([(P.ps[br][:, :], P.K["rot2"], dst, True, True)], te, *P.psfree[br])
            r = rot[c]
            tr = P.tt(P.dve, r, P.ps[br][:, :], tab[:, 1, cs], ALU.mult, t, tt_)
            P.psfree[br] = [tr]
            P.tt(P.dve, dst, dst, tab[:, 0, cs], ALU.mult)
            P.tt(P.dve, dst, dst, r, ALU.add)
    P.barrier()
    P.top = base


def b2_attention(P, qk, vt, cat):
    T = P.T
    base = P.top
    lq = P.region2(4, 64)
    lam = P.region(4)
    sub = P.region(128)
    pr = [[P.region(SEQ) for _ in range(2)] for _ in range(2)]
    pT = [P.region2(8, 128) for _ in range(2)]
    st = [P.region(16) for _ in range(4)]
    jk = [P.region(128) for _ in range(2)]
    ss = P.region2(8, 4)
    for j, n in enumerate(["lambda_q1_2", "lambda_k1_2", "lambda_q2_2", "lambda_k2_2"]):
        P.dma(P.sp, lq[:, j, :], rows(T[n][0], 128), "k")
    tk = P.dma(P.sp, sub, rows(T["subln_g_2"][0], 128), "k")
    for j in range(2):
        P.tt(P.dve, lq[:, 2 * j, :], lq[:, 2 * j, :], lq[:, 2 * j + 1, :], ALU.mult, tk)
        t = P.v(lambda e, j=j: e.tensor_reduce(lam[:, j:j + 1], lq[:, 2 * j, :], AX.X, ALU.add))
    t = P.actf(lam[:, 0:2], lam[:, 0:2], ACT.Exp, t)
    P.tt(P.dve, lam[:, 2:3], lam[:, 1:2], lam[:, 0:1], ALU.subtract, t)
    init = 0.8 - 0.6 * math.exp(-0.3 * 0)
    P.v(lambda e: e.tensor_scalar(lam[:, 2:3], lam[:, 2:3], -init, None, ALU.add))
    P.v(lambda e: e.tensor_scalar(sub, sub, 1.0 - init, None, ALU.mult))
    scale = 64.0 ** -0.5
    items = [(i, h) for i in range(8) for h in range(4)]

    def item(n, i, h):
        s = n % 2
        z, p, pt = st[n % 4], pr[s], pT[s]
        nk = 128 * (i + 1)
        chunks = [(c, min(512, nk - c)) for c in range(0, nk, 512)]
        ts = []
        for o in range(2):
            prt, one = slice(64 * o, 64 * o + 64), slice(64 * o, 64 * o + 1)
            mats, free = [], []
            for c, w in chunks:
                b = 4 * s + 2 * o + c // 512
                last = c + w == nk
                free += P.psfree[b]
                mats.append((P.ps[b][:, 0:w], qk[prt, h, 128 * i:128 * i + 128], qk[prt, 4 + h, c:c + w], True, not last))
                if last:
                    mats.append((P.ps[b][:, w - 128:w], P.K["negrow"][one, :], P.K["lastcol"][one, :], False, True))
            ts.append(P.mms(mats, *free))
        yield
        for o in range(2):
            for c, w in chunks:
                b, k = 4 * s + 2 * o + c // 512, o + 2 * (c // 512)
                P.v(lambda e, k=k, b=b, w=w: e.tensor_reduce(z[:, k:k + 1], P.ps[b][:, 0:w], AX.X, ALU.max), ts[o])
        if nk > 512:
            P.tt(P.dve, z[:, 0:2], z[:, 0:2], z[:, 2:4], ALU.max)
        t = P.v(lambda e: e.tensor_scalar(z[:, 0:2], z[:, 0:2], -scale, None, ALU.mult))
        yield
        for c, w in chunks:
            for o in range(2):
                b, k = 4 * s + 2 * o + c // 512, 4 + o + 2 * (c // 512)
                te = P.actf(p[o][:, c:c + w], P.ps[b][:, 0:w], ACT.Exp, t, bias=z[:, o:o + 1],
                            scale=scale, accum=z[:, k:k + 1])
                P.psfree[b] = [te]
        yield
        if nk > 512:
            P.tt(P.dve, z[:, 4:6], z[:, 4:6], z[:, 6:8], ALU.add, te)
        P.v(lambda e: e.reciprocal(z[:, 4:6], z[:, 4:6]), te)
        P.tt(P.dve, z[:, 5:6], z[:, 5:6], lam[:, 2:3], ALU.mult)
        P.v(lambda e: e.tensor_scalar(p[1][:, 0:nk], p[1][:, 0:nk], z[:, 5:6], None, ALU.mult))
        ta = P.v(lambda e: e.scalar_tensor_tensor(p[0][:, 0:nk], p[0][:, 0:nk], z[:, 4:5],
                                                  p[1][:, 0:nk], ALU.mult, ALU.add))
        yield
        tcs = []
        for half in range(0, i + 1, 4):
            hi = min(half + 4, i + 1)
            b = 4 * s + half // 4
            pv = P.ps[b][:, 0:128 * (hi - half)].rearrange("p (j t) -> p j t", t=128)
            t = P.trs([(pv[:, j - half, :], p[0][:, 128 * j:128 * j + 128]) for j in range(half, hi)], ta,
                      *P.psfree[b])
            tcs.append(P.copy(P.act if half else P.dve, pt[:, half:hi, :], pv, t))
            P.psfree[b] = [tcs[-1]]
        yield
        b = 4 * s + 2
        out = P.ps[b][:, 0:128]
        t = P.mms([(out, pt[:, j, :], vt[:, j, 128 * h:128 * h + 128], j == 0, j == i) for j in range(i + 1)],
                  *tcs, *P.psfree[b])
        yield
        o = cat[:, i, 128 * h:128 * h + 128]
        t = P.copy(P.dve, o, out, t)
        P.psfree[b] = [t]
        P.actf(jk[s], o, ACT.Square, t, accum=ss[:, i, h:h + 1])
        yield

    P.weave([item(n, i, h) for n, (i, h) in enumerate(items)], 2)
    P.barrier()
    t = P.actf(ss, ss, ACT.Sqrt, bias=P.K["eps"][:, 1:2], scale=1.0 / 128)
    P.v(lambda e: e.reciprocal(ss, ss), t)
    for i in range(8):
        o3 = cat[:, i, 0:512].rearrange("p (h n) -> p h n", h=4)
        P.tt(P.dve, o3, o3, bc(ss[:, i, :].unsqueeze(2), [128, 4, 128]), ALU.mult)
        P.tt(P.dve, o3, o3, bc(sub.unsqueeze(1), [128, 4, 128]), ALU.mult)
    P.barrier()
    P.top = base


def b2_out(P, cat, x1T):
    T = P.T
    base = P.top
    wo = [P.split(1, D)]
    gt, bt = P.region(D), P.region(D)
    hx = [P.region(D) for _ in range(2)]
    cT = [P.split(8, 128) for _ in range(2)]
    tmp = [P.region(16) for _ in range(2)]
    P.top = CW + 8 * D
    wo += [P.split(1, D) for _ in range(7)]
    assert P.top <= CW + NF * SEQ
    tw = []
    for k in range(8):
        t = P.dma(P.act, wo[k].x[:, 0, :], T["w_out_2"][0, 128 * k:128 * k + 128, :], f"o{k}")
        tw.append(P.part(P.act, P.pool if k % 2 else P.dve, wo[k].at(0), wo[k].x[:, 0, :], t))
    P.dma(P.sp, gt, rows(T["ln1_g_2"][0], 128), "k")
    tk = P.dma(P.sp, bt, rows(T["ln1_b_2"][0], 128), "k")
    cfree, xfree = [[], []], [[], []]

    def tile(i):
        s = i % 2
        tb = P.dma(P.sp, hx[s], T["h"][NMETA + 128 * i:NMETA + 128 * (i + 1), :], f"x{s}", *xfree[s])
        tt = feature_parts(P, cat[:, i, :], 128, cT[s], 0, (0, 1), cfree[s])
        x = hx[s]
        yield
        for c in range(2):
            b = 2 + c + 2 * s
            t = P.mms([x_ for k in range(8) for x_ in three(P.ps[b][:, :], cT[s].at(k),
                                                            wo[k].at(0, slice(512 * c, 512 * c + 512)), k == 0, k == 7)],
                      *tw, *tt, *P.psfree[b])
            t = P.v(lambda e, c=c, b=b: e.scalar_tensor_tensor(
                x[:, 512 * c:512 * c + 512], x[:, 512 * c:512 * c + 512], ALPHA2, P.ps[b][:, :],
                ALU.mult, ALU.add), t, tb)
            P.psfree[b] = [t]
        cfree[s] = [t]
        yield
        ts = yield from layer_norm(P, x, 128, gt, bt, tmp[s], None, 1e-5, tk, t)
        td = P.dma(P.sp, T["mix"][128 * i:128 * i + 128, :], x, f"ho{s}", *ts)
        yield
        xfree[s] = feature_parts(P, x, 128, x1T[i // 4], 128 * (i % 4), (6, 7), ts) + [td]
        yield

    P.weave([tile(i) for i in range(8)], 2)
    P.barrier()
    P.top = base


def b2_ffn(P, act, x1T):
    T = P.T
    base = P.top
    wg = [P.split(8, 128) for _ in range(2)]
    wu = [P.split(8, 128) for _ in range(2)]
    P.top = base
    wd = [P.split(1, D) for _ in range(4)]
    gp = [P.region(514) for _ in range(2)]
    carry = P.region2(NF, 2)
    cw, cb = P.region2(3, NF), P.region(NF)
    tmp = [P.region(16) for _ in range(4)]
    end = P.top
    place = CW + 2 * NF * 512
    P.top = place
    res = [P.region2(4, D)]
    gt, bt = P.region(D), P.region(D)
    P.top = place + 2 * 8 * 512
    res.append(P.region2(4, D))
    P.top = end
    P.dma(P.sp, cw, T["conv_w_2_c"][0].rearrange("j p f -> p j f"), "k")
    tk = P.dma(P.sp, cb, T["conv_b_2_c"][0], "k")
    for o in range(2):
        tz = P.v(lambda e, o=o: e.memset(gp[o][:, 0:2], 0.0))

    def rings(*toks):
        return [Ring(P, w, lambda f, name=name: T[name][0, :, 128 * f:128 * f + 128].rearrange("(t p) n -> p t n", p=128),
                     NF, st, lambda f, q=q: q, *toks)
                for w, name, st, q in ((wg, "w_gate_2", "w", P.dve), (wu, "w_up_2", "v", P.pool))]

    def finish(c, i, te):
        x = res[c][:, i, :]
        ts = yield from layer_norm(P, x, 128, gt, bt, tmp[i], None, 1e-5, tg, *te)
        P.dma(P.sp, T["out"][0, 512 * c + 128 * i:512 * c + 128 * i + 128, :], x, f"ho{i % 2}", *ts)
        yield

    rg, ru = rings()
    gfree = [[], []]
    tdown = []
    for c in range(2):
        parts = {}
        for f in range(NF):
            o = f % 2
            wgf, wuf = rg.at(f), ru.at(f)
            rg.ahead(f)
            ru.ahead(f)
            t = P.mms([x for k in range(8) for x in three(P.ps[o][:, :], wgf.at(k), x1T[c].at(k), k == 0, k == 7)],
                      rg.tok[f], *P.psfree[o])
            rg.done(f, t)
            rg.halve(f + 1)
            te = P.copy(P.act, gp[o][:, 2:514], P.ps[o][:, :], t, tz, *gfree[o])
            P.psfree[o] = [te]
            b = 2 + o
            tu = P.mms([x for k in range(8) for x in three(P.ps[b][:, :], wuf.at(k), x1T[c].at(k), k == 0, k == 7)],
                       ru.tok[f], *P.psfree[b])
            ru.done(f, tu)
            ru.halve(f + 1)
            y, g = act.x[:, f, :], gp[o]
            if c:
                P.copy(P.dve, g[:, 0:2], carry[:, f, :])
            P.v(lambda e, y=y, g=g, f=f: e.tensor_scalar(y, g[:, 2:514], cw[:, 2, f:f + 1], cb[:, f:f + 1],
                                                         ALU.mult, ALU.add), te, tk, *tdown)
            P.v(lambda e, y=y, g=g, f=f: e.scalar_tensor_tensor(y, g[:, 1:513], cw[:, 1, f:f + 1], y,
                                                                ALU.mult, ALU.add))
            t = P.v(lambda e, y=y, g=g, f=f: e.scalar_tensor_tensor(y, g[:, 0:512], cw[:, 0, f:f + 1], y,
                                                                    ALU.mult, ALU.add))
            gfree[o] = [t if c else P.copy(P.dve, carry[:, f, :], g[:, 512:514])]
            t = P.actf(y, y, ACT.Silu, t)
            tm = P.tt(P.dve, y, y, P.ps[b][:, :], ALU.mult, t, tu)
            P.psfree[b] = [tm]
            parts[f] = tm
            if f:
                parts[f - 1] = P.part(P.act, P.dve, act.at(f - 1), act.x[:, f - 1, :], parts[f - 1])
        parts[NF - 1] = P.part(P.act, P.dve, act.at(NF - 1), act.x[:, NF - 1, :], parts[NF - 1])
        tx = P.dma(P.act, res[c], T["mix"][512 * c:512 * c + 512, :].rearrange("(i p) n -> p i n", p=128), f"x{c}", tu)
        if c == 0:
            P.dma(P.act, gt, rows(T["ln2_g_2"][0], 128), "k", tu)
            tg = P.dma(P.act, bt, rows(T["ln2_b_2"][0], 128), "k", tu)
        rd = Ring(P, wd, lambda f: T["w_down_2"][0, 128 * f:128 * f + 128, :].unsqueeze(1), NF, "d",
                  lambda f: P.pool if f % 2 else P.dve, tu)
        for f in range(NF):
            w = rd.at(f)
            rd.ahead(f)
            t = P.mms([x for i in range(4) for h in range(2)
                       for x in three(P.ps[2 * i + h][:, :], act.at(f, slice(128 * i, 128 * i + 128)),
                                      w.at(0, slice(512 * h, 512 * h + 512)), f == 0, f == NF - 1)],
                      rd.tok[f], parts[f], *([x for p in P.psfree for x in p] if f == 0 else []))
            rd.done(f, t)
            rd.halve(f + 1)
        tdown = [t]
        last = []
        for i in range(4):
            te = []
            for h in range(2):
                r, b = res[c][:, i, 512 * h:512 * h + 512], 2 * i + h
                te.append(P.v(lambda e, r=r, b=b: e.scalar_tensor_tensor(r, r, ALPHA2, P.ps[b][:, :], ALU.mult, ALU.add),
                              t, tx))
                P.psfree[b] = [te[-1]]
            last.append(finish(c, i, te))
        if c == 0:
            rg, ru = rings(t)
        P.weave(last, 4)
    P.barrier()


def second_block(P):
    base = P.top = CW
    cat = P.region2(8, D)
    P.qk_at = P.top
    qk = P.region2(8, SEQ)
    vt = P.region2(8, 512)
    b2_projections(P, None, qk, vt, cat)
    b2_attention(P, qk, vt, cat)
    P.top = base
    act = P.split(NF, 512)
    x1T = [P.split(8, 512) for _ in range(2)]
    b2_out(P, cat, x1T)
    b2_ffn(P, act, x1T)


def build(nc, T, upto="all"):
    with ExitStack() as ctx:
        P = Program(nc, ctx, T, upto)
        block = ctx.enter_context(nc.Block())
        load_consts(P)
        first_block(P)
        if upto == "all":
            second_block(P)
        P.barrier()
        P.sp.push(lambda e: e.nop(), [], P.sp.sem, 1)

        @block.sync
        def _(eng):
            P.sp.emit(eng)

        @block.scalar
        def _(eng):
            P.act.emit(eng)

        @block.vector
        def _(eng):
            P.dve.emit(eng)

        @block.gpsimd
        def _(eng):
            P.pool.emit(eng)

        @block.tensor
        def _(eng):
            P.pe.emit(eng)


def first_block(P):
    upto = P.upto
    positions(P)
    if upto == "pos":
        return
    P.mss = P.region2(NT, 4)
    mark = P.top
    for li in range(DEPTH):
        P.top = mark
        u = P.region2(15, L)
        cq, ckv, kpe = P.region2(2, L), P.region(L), P.region(L)
        m2 = P.top
        hT = P.split(8, L)
        if li == 0:
            embed(P, hT)
        if upto == f"embed{li}":
            return
        project(P, li, hT, cq, ckv, kpe, u)
        P.top = m2
        if upto == f"proj{li}":
            return
        mla(P, li, cq, ckv, kpe)
        if upto == f"mla{li}":
            return
        P.top = mark + 15 * L
        rwkv(P, li, u)
        if upto == f"rwkv{li}":
            return
        P.top = mark
        mixer_out(P, li)
        if upto == f"out{li}":
            return
        top = P.top
        P.top = m2 if li == 0 else CW + 8 * D + 8 * SEQ + 8 * 512
        dst = P.split(8, L) if li == 0 else P.split(8, SEQ)
        P.top = top
        moe(P, li, dst, 0 if li == 0 else NMETA)
        if upto == f"moe{li}":
            return


SCRATCH = [("h", (L, D)), ("mix", (L, D)), ("vfirst", (128, 4 * L)), ("ys", (2 * L, D)), ("cossin", (64, 2 * L)), ("y0", (L, 512)), ("y1", (L, 512)),
           ("rowtab", (NROWS, 1))]


def kernel(**inputs):
    import concourse.bacc as _bacc
    from concourse.bass_utils import run_bass_kernel_spmd as _run

    nc = _bacc.Bacc("TRN2", target_bir_lowering=False, num_devices=1)
    arrays, T = {}, {}
    for name, a in lay_out(inputs).items():
        arrays[f"in_{name}_dram"] = a
        T[name] = nc.dram_tensor(f"in_{name}_dram", a.shape, mybir.dt.from_np(a.dtype), kind="ExternalInput").ap()
    for name, shape in SCRATCH:
        T[name] = nc.dram_tensor(f"t_{name}", shape, I32 if name == "rowtab" else F32, kind="Internal").ap()
    T["out"] = nc.dram_tensor("out_0_dram", (1, SEQ, D), F32, kind="ExternalOutput").ap()
    build(nc, T)
    r = _run(nc, [arrays], core_ids=[0])
    return r.results[0]["out_0_dram"]
```
